# Optimizing a Trainium2 kernel written in Bass

```python
import jax, jax.numpy as jnp
from jax import lax
import numpy as np

D_MODEL = 2048
BATCH = 1
SEQ = 512
DEPTH = 1

CHUNK = 64
HEAD_DIM = 64
SWA_Q_HEADS = D_MODEL // 128
SWA_KV_HEADS = SWA_Q_HEADS // 4
SWA_WINDOW = 128
SWA_WINDOW_CHUNKS = SWA_WINDOW // CHUNK
SB_HEADS = D_MODEL // 128
SB_BLOCK = 128
N_MEM = 256
X_HEADS = 4
X_HEAD_DIM = 128
FFN_HIDDEN = -(-8 * D_MODEL // 768) * 256
ROPE_THETA = 10000.0
NORM_EPS = 1e-6
NEG_INF = -1e30

SWA_Q_W = SWA_Q_HEADS * HEAD_DIM
SWA_KV_W = SWA_KV_HEADS * HEAD_DIM
SB_W = SB_HEADS * HEAD_DIM
IN_SPLITS = (SWA_Q_W, SWA_Q_W + SWA_KV_W, SWA_Q_W + 2 * SWA_KV_W,
             SWA_Q_W + 2 * SWA_KV_W + SB_W, SWA_Q_W + 2 * SWA_KV_W + 2 * SB_W)
IN_WIDTH = SWA_Q_W + 2 * SWA_KV_W + 3 * SB_W

kernel_name = "hybrid_swa_sink_stickbreaking_gated_block"

def rmsnorm(x, g):
    xf = x.astype(jnp.float32)
    y = xf * lax.rsqrt(jnp.mean(xf * xf, axis=-1, keepdims=True) + NORM_EPS)
    return (y * g.astype(jnp.float32)).astype(x.dtype)

def rope(x, pos):
    half = x.shape[-1] // 2
    inv = ROPE_THETA ** (-jnp.arange(half, dtype=jnp.float32) / half)
    ang = pos.astype(jnp.float32)[..., None] * inv
    cos = jnp.cos(ang)[:, :, None, :]
    sin = jnp.sin(ang)[:, :, None, :]
    x1 = x[..., :half].astype(jnp.float32)
    x2 = x[..., half:].astype(jnp.float32)
    out = jnp.concatenate([x1 * cos - x2 * sin, x2 * cos + x1 * sin], axis=-1)
    return out.astype(x.dtype)

def swa_sink_attention(q, k, v, sinks):
    B, S, HQ, d = q.shape
    HKV = k.shape[2]
    G = HQ // HKV
    NC = S // CHUNK
    qc = q.reshape(B, NC, CHUNK, HKV, G, d)
    kc = k.reshape(B, NC, CHUNK, HKV, d)
    vc = v.reshape(B, NC, CHUNK, HKV, d)

    def band(t):
        parts = [jnp.pad(t, ((0, 0), (w, 0), (0, 0), (0, 0), (0, 0)))[:, :NC]
                 for w in range(SWA_WINDOW_CHUNKS - 1, -1, -1)]
        return jnp.concatenate(parts, axis=2)

    kb, vb = band(kc), band(vc)
    key_chunk = (jnp.arange(NC)[:, None] - (SWA_WINDOW_CHUNKS - 1)
                 + jnp.arange(SWA_WINDOW_CHUNKS * CHUNK)[None, :] // CHUNK)
    valid = key_chunk >= 0
    s = jnp.einsum('bnqkgd,bnskd->bnkgqs', qc, kb).astype(jnp.float32) * (d ** -0.5)
    s = jnp.where(valid[None, :, None, None, None, :], s, NEG_INF)
    sink = sinks.astype(jnp.float32).reshape(HKV, G)[None, None, :, :, None, None]
    m = jnp.maximum(jnp.max(s, axis=-1, keepdims=True), sink)
    p = jnp.exp(s - m)
    p = p / (jnp.sum(p, axis=-1, keepdims=True) + jnp.exp(sink - m))
    o = jnp.einsum('bnkgqs,bnskd->bnqkgd', p.astype(v.dtype), vb)
    return o.reshape(B, S, HQ * d)

def stick_breaking_attention(q, k, v):
    B, S, H, d = q.shape
    NB = S // SB_BLOCK
    qb = q.reshape(B, NB, SB_BLOCK, H, d).transpose(1, 0, 2, 3, 4)
    key_pos = jnp.arange(S)

    def block(args):
        qi, i = args
        q_pos = i * SB_BLOCK + jnp.arange(SB_BLOCK)
        z = jnp.einsum('bthd,bshd->bhts', qi, k).astype(jnp.float32) * (d ** -0.5)
        causal = key_pos[None, :] < q_pos[:, None]
        log_beta = jax.nn.log_sigmoid(z)
        log_1mb = jnp.where(causal, jax.nn.log_sigmoid(-z), 0.0)
        tail = lax.cumsum(log_1mb, axis=3, reverse=True) - log_1mb
        a = jnp.where(causal, jnp.exp(log_beta + tail), 0.0)
        return jnp.einsum('bhts,bshd->bthd', a.astype(v.dtype), v)

    o = lax.map(block, (qb, jnp.arange(NB)))
    return o.transpose(1, 0, 2, 3, 4).reshape(B, S, H * d)

def memory_cross_attention(h, mem_n, w_xq, w_xkv, w_xo):
    B, S, _ = h.shape
    M = mem_n.shape[1]
    q = (h @ w_xq).reshape(B, S, X_HEADS, X_HEAD_DIM)
    kv = (mem_n @ w_xkv).reshape(B, M, 2, X_HEADS, X_HEAD_DIM)
    k, v = kv[:, :, 0], kv[:, :, 1]
    s = jnp.einsum('bqhd,bmhd->bhqm', q, k).astype(jnp.float32) * (X_HEAD_DIM ** -0.5)
    p = jax.nn.softmax(s, axis=-1).astype(v.dtype)
    o = jnp.einsum('bhqm,bmhd->bqhd', p, v).reshape(B, S, X_HEADS * X_HEAD_DIM)
    return o @ w_xo

def swiglu(h, w_gu, w_down):
    g, u = jnp.split(h @ w_gu, 2, axis=-1)
    return (jax.nn.silu(g) * u) @ w_down

def setup_inputs(seed: int = 0) -> dict:
    key = jax.random.key(seed)
    ks = jax.random.split(key, 24)
    f32 = jnp.float32

    def w(k, shape, fan_in):
        return jax.random.normal(k, shape, f32) * (fan_in ** -0.5)

    def gain(k, shape):
        return 1.0 + 0.02 * jax.random.normal(k, shape, f32)

    x = jax.random.normal(ks[0], (BATCH, SEQ, D_MODEL), f32)
    mem = jax.random.normal(ks[1], (BATCH, N_MEM, D_MODEL), f32)
    offset = jax.random.randint(ks[2], (BATCH, 1), 0, 4096, dtype=jnp.int32)
    positions = (jnp.arange(SEQ, dtype=jnp.int32)[None, :] + offset).astype(jnp.int32)
    return {
        "x": x,
        "mem": mem,
        "positions": positions,
        "norm_mix_g": gain(ks[3], (DEPTH, D_MODEL)),
        "w_in": w(ks[4], (DEPTH, D_MODEL, IN_WIDTH), D_MODEL),
        "sinks": 0.5 * jax.random.normal(ks[5], (DEPTH, SWA_Q_HEADS), f32),
        "w_branch_a": w(ks[6], (DEPTH, SWA_Q_W, D_MODEL), SWA_Q_W),
        "w_branch_b": w(ks[7], (DEPTH, SB_W, D_MODEL), SB_W),
        "w_gate": w(ks[8], (DEPTH, D_MODEL, 2 * D_MODEL), D_MODEL),
        "b_gate": 0.02 * jax.random.normal(ks[9], (DEPTH, 2 * D_MODEL), f32),
        "w_out": w(ks[10], (DEPTH, D_MODEL, D_MODEL), D_MODEL),
        "norm_cross_g": gain(ks[11], (DEPTH, D_MODEL)),
        "norm_mem_g": gain(ks[12], (DEPTH, D_MODEL)),
        "w_xq": w(ks[13], (DEPTH, D_MODEL, X_HEADS * X_HEAD_DIM), D_MODEL),
        "w_xkv": w(ks[14], (DEPTH, D_MODEL, 2 * X_HEADS * X_HEAD_DIM), D_MODEL),
        "w_xo": w(ks[15], (DEPTH, X_HEADS * X_HEAD_DIM, D_MODEL), X_HEADS * X_HEAD_DIM),
        "norm_ffn_g": gain(ks[16], (DEPTH, D_MODEL)),
        "w_gu": w(ks[17], (DEPTH, D_MODEL, 2 * FFN_HIDDEN), D_MODEL),
        "w_down": w(ks[18], (DEPTH, FFN_HIDDEN, D_MODEL), FFN_HIDDEN),
        "final_norm_g": gain(ks[19], (D_MODEL,)),
    }

def reference(x, mem, positions, norm_mix_g, w_in, sinks, w_branch_a, w_branch_b,
              w_gate, b_gate, w_out, norm_cross_g, norm_mem_g, w_xq, w_xkv, w_xo,
              norm_ffn_g, w_gu, w_down, final_norm_g):
    B, S, D = x.shape
    for l in range(DEPTH):
        h = rmsnorm(x, norm_mix_g[l])
        proj = h @ w_in[l]
        q_a, k_a, v_a, q_b, k_b, v_b = jnp.split(proj, IN_SPLITS, axis=-1)
        q_a = rope(q_a.reshape(B, S, SWA_Q_HEADS, HEAD_DIM), positions)
        k_a = rope(k_a.reshape(B, S, SWA_KV_HEADS, HEAD_DIM), positions)
        v_a = v_a.reshape(B, S, SWA_KV_HEADS, HEAD_DIM)
        o_a = swa_sink_attention(q_a, k_a, v_a, sinks[l])
        o_b = stick_breaking_attention(q_b.reshape(B, S, SB_HEADS, HEAD_DIM),
                                       k_b.reshape(B, S, SB_HEADS, HEAD_DIM),
                                       v_b.reshape(B, S, SB_HEADS, HEAD_DIM))
        y_a = o_a @ w_branch_a[l]
        y_b = o_b @ w_branch_b[l]
        gates = jax.nn.sigmoid(h @ w_gate[l] + b_gate[l]).reshape(B, S, 2, D)
        x = x + (gates[:, :, 0] * y_a + gates[:, :, 1] * y_b) @ w_out[l]
        hc = rmsnorm(x, norm_cross_g[l])
        mem_n = rmsnorm(mem, norm_mem_g[l])
        x = x + memory_cross_attention(hc, mem_n, w_xq[l], w_xkv[l], w_xo[l])
        hf = rmsnorm(x, norm_ffn_g[l])
        x = x + swiglu(hf, w_gu[l], w_down[l])
    return rmsnorm(x, final_norm_g)


_drawn_inputs = setup_inputs


def setup_inputs(seed=0):
    import zlib

    import numpy as np

    out = dict(_drawn_inputs(seed))
    spreads = {}
    factors = {'norm_mix_g': 6.066,
     'sinks': 8.0,
     'b_gate': 8.0,
     'norm_cross_g': 8.0,
     'norm_mem_g': 8.0,
     'norm_ffn_g': 4.146,
     'final_norm_g': 2.915}
    for name, (base, spread) in spreads.items():
        noise = np.random.default_rng([zlib.crc32(name.encode()), seed]).standard_normal(out[name].shape)
        drawn = base * np.exp(spread * noise) if base else spread * noise
        out[name] = __import__('jax').numpy.asarray(drawn.astype(out[name].dtype))
    for name, factor in factors.items():
        out[name] = (out[name] * factor).astype(out[name].dtype)
    return out
```

```python
import numpy as np
from contextlib import ExitStack, contextmanager

import concourse.bass as bass
from concourse import mybir

P = 128
D = 2048
S = 512
KT = D // P
HD = 64
HALF = HD // 2
SWA_HEADS, SWA_KV = D // 128, D // 128 // 4
SWA_W, KV_W = SWA_HEADS * HD, SWA_KV * HD
SB_W = (D // 128) * HD
PAIRS = SB_W // P
MIX_KT = SB_W // P
NM = 256
XH, XD = 4, 128
FFN = -(-8 * D // 768) * 256
UK = 8
RING = 4
AHEAD = RING - 1
GROUP = 4
GROUPS = FFN // P // GROUP
CHUNK = 64
EPS = 1e-6
NEG = -1e30
ROPE_THETA = 10000.0
QT = S // P

U_SB = 0
U_DB = U_SB + PAIRS * 6
U_SWA = U_DB + KT * 3
U_DA = U_SWA + 4 * 2 + PAIRS * 2
U_OUT = U_DA + KT * 3
U_XQ = U_OUT + KT * 2
U_XKV = U_XQ + XH * 2
U_XO = U_XKV + 2 * XH * 2
U_FFN = U_XO + KT // 2
FFN_UNITS = GROUP * 4 + KT // 2
UNITS = U_FFN + GROUPS * FFN_UNITS

A_DB = PAIRS * 4
A_SWA = A_DB + KT * 2
A_DA = A_SWA + 6 + PAIRS
A_OUT = A_DA + KT * 2
A_XQ = A_OUT + KT * 2
A_XKV = A_XQ + XH
A_XO = A_XKV + 2 * XH + 2
A_FFN = A_XO + KT
A_END = A_FFN + GROUPS * (GROUP * 2 + KT)

G_MIX, G_CROSS, G_MEM, G_FFN, G_FINAL = (KT * n for n in range(5))
B_GATE = 5 * KT
SINK = B_GATE + 2 * KT
PARAMS = SINK + SWA_HEADS

SB_OFF = (0, 512, 1024, 896)
SB_LEN = tuple(S - P * j for j in range(QT))
SB_COLS = sum(SB_LEN)


ROUND = float(3 << 22)
TWO_PI = (6.28125, 0.0019350051879882812, float(2 * np.pi - 6.28125 - 0.0019350051879882812))
PI_DOWN = 3.1415925
SWA_STEPS = 2 * 14


class Tally:

    def __init__(self, n=0):
        self.n, self.loops = n, []

    def at(self, k=0):
        v = self.n + k
        for i, stride in self.loops:
            v = i * stride + v
        return v

    def add(self, k=1):
        self.n += k


@contextmanager
def repeat(eng, times, strides):
    with eng.Fori(0, times) as i:
        began = [(t, t.n, s) for t, s in strides]
        for t, s in strides:
            t.loops.append((i, s))
        yield i
        for t, n, s in began:
            assert t.n - n == s, (t.n - n, s)
            t.n = n + s * times
            t.loops.pop()


def block_kernel(nc, w, xT, memT, params, rope_const, pos, out):
    F32, F32R, BF16, I32 = mybir.dt.float32, mybir.dt.float32r, mybir.dt.bfloat16, mybir.dt.int32
    ALU, ACT, AX = mybir.AluOpType, mybir.ActivationFunctionType, mybir.AxisListType
    ctx = ExitStack()
    with ctx:
        def sb(name, shape, dt, stack=ctx):
            return stack.enter_context(nc.sbuf_tensor(name, shape, dt))

        def sem(name):
            return ctx.enter_context(nc.semaphore(name))

        stat_x = sb("stat_x", [P, 3, 4], F32)
        par = sb("par", [P, PARAMS], F32)
        rc = sb("rc", [P, 2], F32)
        ident = sb("ident", [P, P], F32)
        ones = sb("ones", [P, P], F32)
        ones_r = sb("ones_r", [P, P], F32R)
        tri_r = sb("tri_r", [P, P], F32R)
        eps_t = sb("eps_t", [P, 1], F32)
        rstd = sb("rstd", [P, S], F32)
        sq_sum = sb("sq_sum", [P, S], F32)
        act_hi = sb("act_hi", [P, KT, S], F32R)
        act_lo = sb("act_lo", [P, KT, S], F32R)
        raw = sb("raw", [P, RING, UK * P], F32)
        w_hi = sb("w_hi", [P, RING, UK * P], F32R)
        w_lo = sb("w_lo", [P, RING, UK * P], F32R)

        with ExitStack() as a:
            x = sb("x", [P, KT, S], F32, a)
        o_hi = sb("o_hi", [P, MIX_KT, S], F32R)
        o_lo = sb("o_lo", [P, MIX_KT, S], F32R)

        with ExitStack() as a:
            sb_mask = sb("sb_mask", [P, SB_COLS], BF16, a)
            zb = [sb(f"zb{n}", [P, SB_COLS], F32, a) for n in range(2)]
            pf = [sb(f"pf{n}", [P, SB_COLS], F32, a) for n in range(2)]
            pa_hi = [sb(f"pa_hi{n}", [P, SB_COLS], F32R, a) for n in range(2)]
            pa_lo = [sb(f"pa_lo{n}", [P, SB_COLS], F32R, a) for n in range(2)]
            q_hi, k_hi, v_hi = (sb(f"{n}_hi", [P, S], F32R, a) for n in "qkv")
            q_lo, k_lo, v_lo = (sb(f"{n}_lo", [P, S], F32R, a) for n in "qkv")
            scaled = sb("scaled", [P, S], F32, a)
        vt = rb = sq_sum

        with ExitStack() as a:
            merged = sb("merged", [P, KT, S], F32, a)
        act2_hi = sb("act2_hi", [P, UK, S], F32R)
        act2_lo = sb("act2_lo", [P, UK, S], F32R)

        with ExitStack() as a:
            cos_t = sb("cos_t", [P, S], F32, a)
            sin_t = sb("sin_t", [P, S], F32, a)
            ka = sb("ka", [P, 2, S], F32, a)
            va = sb("va", [P, QT, KV_W], F32, a)
            qa = sb("qa", [P, S], F32, a)
            ra = sb("ra", [P, S], F32, a)
            s_a = sb("s_a", [P, 4, 2 * P], F32, a)
            pt_a = sb("pt_a", [P, 8 * P], F32, a)
            band = sb("band", [P, 2, 2 * P], BF16, a)
            stat_a = sb("stat_a", [P, 6, 4], F32, a)
        with ExitStack() as a:
            gate = sb("gate", [P, 2, S], F32, a)
        mem_stat = sb("mem_stat", [P, NM], F32)
        qx = sb("qx", [P, XH, S], F32)
        with ExitStack() as a:
            mem = sb("mem", [P, KT, NM], F32, a)
        with ExitStack() as a:
            kx = sb("kx", [P, XH, NM], F32, a)
            vx = sb("vx", [P, 2, XH * XD], F32, a)
            s_x = sb("s_x", [P, 4, NM], F32, a)
            pt_x = sb("pt_x", [P, 2, S], F32, a)
        with ExitStack() as a:
            gt = sb("gt", [P, S], F32, a)
            sg = sb("sg", [P, S], F32, a)

        acc = [ctx.enter_context(nc.psum_tensor(f"acc{n}", [P, S], F32)) for n in range(2)]
        ps = [ctx.enter_context(nc.psum_tensor(f"ps{n}", [P, 3 * S], F32)) for n in range(2)]

        raw_in = [sem(f"raw_in{n}") for n in range(RING)]
        hi_done, lo_done = sem("hi_done"), sem("lo_done")
        unit_done = sem("unit_done")
        half_done = sem("half_done")
        acc_free = sem("acc_free")
        par_in, pos_in, mem_in = sem("par_in"), sem("pos_in"), sem("mem_in")
        x_in = [sem(f"x_in{n}") for n in range(4)]
        const_ready, const_r_ready = sem("const_ready"), sem("const_r_ready")
        h_hi, h_lo = sem("h_hi"), sem("h_lo")
        mg_hi, mg_lo = sem("mg_hi"), sem("mg_lo")
        mem_hi, mem_lo = sem("mem_hi"), sem("mem_lo")
        sq_ready, sq_done = sem("sq_ready"), sem("sq_done")
        stat_done, std_ready, rstd_ready = sem("stat_done"), sem("std_ready"), sem("rstd_ready")
        z_done, t_done, pv_done = sem("z_done"), sem("t_done"), sem("pv_done")
        zb_ready, lb_ready, p_ready = sem("zb_ready"), sem("lb_ready"), sem("p_ready")
        soft_ready = sem("soft_ready")
        p_hi_done, p_lo_done = sem("p_hi_done"), sem("p_lo_done")
        u_ready, a_ready, a_hi_done, a_lo_done = (sem(n) for n in ("u_ready", "a_ready", "a_hi_done", "a_lo_done"))
        o_hi_done = sem("o_hi_done")
        ps_free = sem("ps_free")
        qk_hi_done, qk_lo_done = sem("qk_hi_done"), sem("qk_lo_done")
        vt_ready, tr_done, v_hi_done, v_lo_done = (sem(n) for n in ("vt_ready", "tr_done", "v_hi_done", "v_lo_done"))
        sig_ready, mix_ready = sem("sig_ready"), sem("mix_ready")
        ang_ready, trig_ready = sem("ang_ready"), sem("trig_ready")
        rot_ready, qa_ready = sem("rot_ready"), sem("qa_ready")
        s_done, max_ready, exp_ready, prob_ready = (sem(n) for n in ("s_done", "max_ready", "exp_ready", "prob_ready"))
        ptr_done, pt_ready = sem("ptr_done"), sem("pt_ready")
        hid_hi = sem("hid_hi")
        hid_lo = sem("hid_lo")
        gain_ready, out_ready, stored = sem("gain_ready"), sem("out_ready"), sem("stored")
        act_step, dve_step = sem("act_step"), sem("dve_step")

        def act_tile(k):
            return act_hi[:, k, :], act_lo[:, k, :]

        def hc_tile(k):
            return act_tile(k) if k < UK else (act2_hi[:, k - UK, :], act2_lo[:, k - UK, :])

        def o_tile(k):
            return o_hi[:, k, :], o_lo[:, k, :]

        def act2_tile(k):
            return act2_hi[:, k, :], act2_lo[:, k, :]

        mem_hi_v = act_hi[:, UK:KT, :].rearrange("p a (b n) -> p (a b) n", n=NM)
        mem_lo_v = act_lo[:, UK:KT, :].rearrange("p a (b n) -> p (a b) n", n=NM)

        def mem_tile(k):
            return mem_hi_v[:, k, :], mem_lo_v[:, k, :]

        def f(ap):
            return ap.bitcast(F32)

        block = ctx.enter_context(nc.Block())

        @block.sync
        def _(sp):
            for s in range(RING):
                sp.dma_start(raw[:, s, :], w[s, :, :]).then_inc(raw_in[s], 16)
            with sp.Fori(1, UNITS // RING) as i:
                for s in range(RING):
                    sp.wait_ge(lo_done, i * RING + (s - RING + 1))
                    sp.dma_start(raw[:, s, :], w[i * RING + s, :, :]).then_inc(raw_in[s], 16)
            with sp.Fori(0, KT) as m:
                sp.wait_ge(out_ready, m + 1)
                sp.dma_start(out[m, :, :], x[:, m, :]).then_inc(stored, 16)
            sp.wait_ge(stored, 16 * KT)

        @block.gpsimd
        def _(pool):
            step = Tally()

            def link(ins):
                ins.then_inc(sq_ready, 1)
                step.add()
                pool.wait_ge(sq_ready, step.at())

            link(nc.gpsimd.memset(ident[:], 0.0))
            link(nc.gpsimd.affine_select(out=ident[:], in_=ident[:], compare_op=ALU.not_equal, fill=1.0,
                                         base=0, pattern=[[-1, P]], channel_multiplier=1))
            nc.gpsimd.memset(ones[:], 1.0).then_inc(const_ready, 1)
            nc.gpsimd.memset(eps_t[:], EPS).then_inc(const_ready, 1)
            link(nc.gpsimd.memset(scaled[:, 0:P], 1.0))
            nc.gpsimd.affine_select(out=scaled[:, 0:P], in_=scaled[:, 0:P], compare_op=ALU.is_gt, fill=0.0,
                                    base=0, pattern=[[-1, P]], channel_multiplier=1).then_inc(const_ready, 1)
            link(nc.gpsimd.memset(sb_mask[:], 0.0))
            for j in range(QT):
                d = sb_mask[:, SB_OFF[j]:SB_OFF[j] + P]
                last = nc.gpsimd.affine_select(out=d, in_=d, compare_op=ALU.is_gt, fill=NEG, base=0,
                                               pattern=[[1, P]], channel_multiplier=-1)
            last.then_inc(const_ready, 1)

            def squares(tile, tmp, total):
                link(nc.gpsimd.tensor_tensor(tmp, tile, tile, ALU.mult))
                link(nc.gpsimd.tensor_tensor(total, total, tmp, ALU.add))

            link(nc.gpsimd.memset(sq_sum[:], 0.0))
            for c in range(4):
                pool.wait_ge(x_in[c], 16)
                with repeat(pool, 4, [(step, 2)]) as i:
                    squares(x[:, 4 * c + i, :], rstd[:], sq_sum[:])
            nc.gpsimd.tensor_copy(sq_sum[:, 0:1], sq_sum[:, 0:1]).then_inc(sq_done, 1)

            pool.wait_ge(acc_free, A_DB + 1)
            link(nc.gpsimd.memset(band[:], 0.0))
            link(nc.gpsimd.memset(band[:, :, 0:CHUNK], NEG))
            link(nc.gpsimd.memset(band[CHUNK:P, :, CHUNK:P], NEG))
            link(nc.gpsimd.memset(band[0:CHUNK, :, P + CHUNK:2 * P], NEG))
            nc.gpsimd.memset(band[:, 0, 0:P], NEG).then_inc(const_ready, 1)

            pool.wait_ge(mem_in, 16)
            link(nc.gpsimd.memset(mem_stat[:], 0.0))
            with repeat(pool, KT, [(step, 2)]) as m:
                squares(mem[:, m, :], rstd[:, 0:NM], mem_stat[:])
            nc.gpsimd.tensor_copy(mem_stat[:, 0:1], mem_stat[:, 0:1]).then_inc(sq_done, 1)

            def x_squares(first_out):
                pool.wait_ge(acc_free, first_out + 1)
                link(nc.gpsimd.memset(sq_sum[:], 0.0))
                with repeat(pool, KT, [(step, 2)]) as m:
                    pool.wait_ge(acc_free, m + (first_out + 1))
                    squares(x[:, m, :], rstd[:], sq_sum[:])
                nc.gpsimd.tensor_copy(sq_sum[:, 0:1], sq_sum[:, 0:1]).then_inc(sq_done, 1)

            x_squares(A_OUT + KT)
            x_squares(A_XO)
            x_squares(A_END - KT)

        @block.scalar
        def _(act):
            act.dma_start(par[:], params).then_inc(par_in, 16)
            for c in range(4):
                act.dma_start(x[:, 4 * c:4 * c + 4, :], xT[:, 4 * c:4 * c + 4, :]).then_inc(x_in[c], 16)
            hd, step, pair, out_no, tr = Tally(), Tally(), Tally(), Tally(), Tally()

            def link(ins):
                ins.then_inc(act_step, 1)
                step.add()
                act.wait_ge(act_step, step.at())

            converted = Tally()

            def convert():
                s = converted.n % RING
                loop = [(i, st // RING) for i, st in converted.loops]
                turn = converted.n // RING + 1
                for i, st in loop:
                    turn = i * st + turn
                act.wait_ge(raw_in[s], turn * 16)
                if converted.loops or converted.n >= RING:
                    act.wait_ge(unit_done, converted.at(1 - RING))
                nc.scalar.activation(w_hi[:, s, :], raw[:, s, :], ACT.Copy).then_inc(hi_done, 1)
                converted.add()

            def units(n=1):
                for _ in range(n):
                    convert()

            convert()
            act.wait_ge(par_in, 16)
            for c in range(4):
                act.wait_ge(x_in[c], 16)
                with act.Fori(0, 4) as i:
                    nc.scalar.activation(act_hi[:, 4 * c + i, :], x[:, 4 * c + i, :], ACT.Copy,
                                         scale=par[:, bass.ds(i + (G_MIX + 4 * c), 1)]).then_inc(h_hi, 1)
                if c < 2:
                    convert()
            assert converted.n == AHEAD

            def std(n, bank, dst, width):
                act.wait_ge(stat_done, n)
                if n == 1:
                    act.wait_ge(const_ready, 4)
                nc.scalar.activation(dst[:, 0:width], bank[:, 0:width], ACT.Sqrt, bias=eps_t[:, 0:1],
                                     scale=1.0 / D).then_inc(std_ready, 1)

            def soft(par_):
                act.wait_ge(zb_ready, hd.at(1 + par_))
                link(nc.scalar.activation(pf[par_][:], zb[par_][:], ACT.Abs))
                link(nc.scalar.activation(pf[par_][:], pf[par_][:], ACT.Exp, scale=-1.0))
                nc.scalar.activation(pf[par_][:], pf[par_][:], ACT.Ln, bias=1.0).then_inc(soft_ready, 1)

            def p_high(par_):
                act.wait_ge(p_ready, hd.at(1 + par_))
                nc.scalar.activation(pa_hi[par_][:], pf[par_][:], ACT.Copy).then_inc(p_hi_done, 1)

            def a_high(par_):
                act.wait_ge(u_ready, hd.at(1 + par_))
                nc.scalar.activation(pf[par_][:], zb[par_][:], ACT.Exp).then_inc(a_ready, 1)
                act.wait_ge(a_ready, hd.at(1 + par_))
                nc.scalar.activation(pa_hi[par_][:], pf[par_][:], ACT.Copy).then_inc(a_hi_done, 1)

            def o_high(par_):
                act.wait_ge(pv_done, hd.at(1 + par_))
                rows = slice(HD * par_, HD * par_ + HD)
                nc.scalar.activation(o_hi[rows, pair.at(), :], ps[par_][rows, 0:S], ACT.Copy)\
                    .then_inc(o_hi_done, 1)

            def read_out():
                act.wait_ge(acc_free, out_no.at(1))
                out_no.add()

            def qk_high(dst):
                read_out()
                nc.scalar.activation(dst[:], scaled[:], ACT.Copy).then_inc(qk_hi_done, 1)

            def sb_body(attend, project):
                if attend:
                    soft(0)
                if project:
                    units()
                if attend:
                    act.wait_ge(tr_done, tr.at(1))
                    nc.scalar.activation(v_hi[:], acc[1][:], ACT.Copy).then_inc(v_hi_done, 1)
                    tr.add()
                    out_no.add()
                    p_high(0)
                    soft(1)
                if project:
                    units()
                if attend:
                    p_high(1)
                if project:
                    qk_high(q_hi)
                    units()
                if attend:
                    a_high(0)
                if project:
                    units()
                if attend:
                    a_high(1)
                if project:
                    qk_high(k_hi)
                    units()
                if attend:
                    o_high(0)
                if project:
                    units()
                    out_no.add()
                if attend:
                    o_high(1)
                    hd.add(2)
                    pair.add()

            units(3)
            std(1, ps[0], rstd, S)
            qk_high(q_hi)
            units()
            qk_high(k_hi)
            units(2)
            out_no.add()
            with repeat(act, (PAIRS - 2) // 2, [(converted, 12), (hd, 4), (step, 8), (pair, 2), (out_no, 8), (tr, 2)]):
                sb_body(True, True)
                sb_body(True, True)
            sb_body(True, True)
            sb_body(True, False)

            def gates(first):
                with repeat(act, KT // 4, [(converted, 12), (out_no, 8)]) as i:
                    for b in range(4):
                        units(2)
                        read_out()
                        nc.scalar.activation(gate[:, b % 2, :], gate[:, b % 2, :], ACT.Sigmoid,
                                             bias=par[:, bass.ds(i * 4 + (b + B_GATE + first), 1)])\
                            .then_inc(sig_ready, 1)
                        units()
                        out_no.add()

            gates(KT)

            act.dma_start(rc[:], rope_const).then_inc(pos_in, 16)
            act.wait_ge(acc_free, A_SWA)
            act.dma_start(ra[:].bitcast(I32), pos).then_inc(pos_in, 16)
            act.wait_ge(ang_ready, 1)
            nc.scalar.activation(sin_t[:], sin_t[:], ACT.Sin)
            nc.scalar.activation(cos_t[:], cos_t[:], ACT.Sin).then_inc(trig_ready, 1)
            swa = Tally()

            def rotate():
                read_out()
                for h in range(2):
                    for a, b in ((0, HALF), (HALF, 0)):
                        last = nc.scalar.activation(rb[HD * h + a:HD * h + a + HALF, :],
                                                    ra[HD * h + b:HD * h + b + HALF, :], ACT.Copy)
                last.then_inc(rot_ready, 1)

            def swa_exp(hf):
                act.wait_ge(max_ready, swa.at(1 + hf))
                for n in range(4):
                    nc.scalar.activation(s_a[:, n, :], s_a[:, n, :], ACT.Exp, bias=stat_a[:, 1, n:n + 1],
                                         accum_out=stat_a[:, 3, n:n + 1])
                nc.scalar.activation(stat_a[:, 4, :], stat_a[:, 2, :], ACT.Exp).then_inc(exp_ready, 1)

            def swa_pt(hf):
                act.wait_ge(ptr_done, swa.at(1 + hf))
                nc.scalar.activation(pt_a[:], ps[hf][:, 0:2 * S], ACT.Copy).then_inc(pt_ready, 1)

            def swa_o(hf):
                act.wait_ge(pv_done, hd.at(1 + hf))
                for h in range(2):
                    rows = slice(HD * h, HD * h + HD)
                    last = nc.scalar.activation(o_hi[rows, pair.at(), 2 * P * hf:2 * P * (hf + 1)],
                                                ps[hf][rows, 2 * S + 2 * P * h:2 * S + 2 * P * (h + 1)], ACT.Copy)
                last.then_inc(o_hi_done, 1)

            def swa_body(attend, project):
                if attend:
                    swa_exp(0)
                if project:
                    units()
                if attend:
                    swa_pt(0)
                    swa_exp(1)
                if project:
                    units()
                if attend:
                    swa_o(0)
                    swa_pt(1)
                    swa_o(1)
                if project:
                    rotate()
                if attend:
                    swa.add(2)
                    hd.add(2)
                    pair.add()

            units(4)
            out_no.add(2)
            units(2)
            act.wait_ge(tr_done, PAIRS + 2)
            rotate()
            out_no.add(2)
            units(2)
            rotate()
            pair.n = 0
            swa_body(False, True)
            moves = [(converted, 4), (swa, 4), (hd, 4), (pair, 2), (out_no, 2)]
            for turns in (2, 1):
                with repeat(act, turns, moves):
                    swa_body(True, True)
                    swa_body(True, True)
            swa_body(True, True)
            swa_body(True, False)

            gates(0)

            act.wait_ge(unit_done, U_OUT)
            for c in range(4):
                act.dma_start(x[:, 4 * c:4 * c + 4, :], xT[:, 4 * c:4 * c + 4, :]).then_inc(x_in[c], 16)
            act.wait_ge(mix_ready, KT)
            act.dma_start(mem[:], memT).then_inc(mem_in, 16)
            with act.Fori(0, KT) as m:
                nc.scalar.activation(act_hi[:, m, :], merged[:, m, :], ACT.Copy).then_inc(mg_hi, 1)
            with repeat(act, KT // 4, [(converted, 4)]):
                units(4)
            out_no.add(KT)

            def x_high(dst, m, gain):
                read_out()
                nc.scalar.activation(dst, x[:, m, :], ACT.Copy, scale=par[:, bass.ds(m + gain, 1)])\
                    .then_inc(h_hi, 1)

            for half, dst in ((0, act_hi), (1, act2_hi)):
                with repeat(act, 2, [(converted, 4), (out_no, 4)]) as i:
                    for b in range(4):
                        units()
                        x_high(dst[:, i * 4 + b, :], i * 4 + (b + UK * half), G_CROSS)

            act.wait_ge(unit_done, U_XQ)
            act.wait_ge(mem_in, 16)
            for p in range(XH):
                units(2)
                with act.Fori(4 * p, 4 * p + 4) as m:
                    nc.scalar.activation(mem_hi_v[:, m, :], mem[:, m, :], ACT.Copy,
                                         scale=par[:, bass.ds(m + G_MEM, 1)]).then_inc(mem_hi, 1)
                if p == 0:
                    std(2, ps[0], rstd, S)
            units(3)
            std(3, ps[1], mem_stat, NM)
            units(5)
            def x_exp(h):
                act.wait_ge(max_ready, swa.at(1 + h))
                for n in range(4):
                    last = nc.scalar.activation(s_x[:, n, :], ps[h % 2][:, n * NM:(n + 1) * NM], ACT.Exp,
                                                bias=stat_x[:, 1, n:n + 1], scale=XD ** -0.5,
                                                accum_out=stat_x[:, 2, n:n + 1])
                last.then_inc(exp_ready, 1)

            def x_pt(h):
                act.wait_ge(ptr_done, swa.at(1 + h))
                nc.scalar.activation(pt_x[:], ps[h % 2][:, 0:2 * S].rearrange("p (a b) -> p a b", a=2), ACT.Copy)\
                    .then_inc(pt_ready, 1)

            def x_o(h):
                act.wait_ge(pv_done, hd.at(1))
                nc.scalar.activation(act2_hi[:, h, :], ps[h % 2][:, 2 * S:3 * S], ACT.Copy).then_inc(o_hi_done, 1)
                hd.add()

            x_exp(0)
            units(8)
            out_no.add(2 * XH + 2)
            for h in range(XH):
                x_pt(h)
                if h + 1 < XH:
                    x_exp(h + 1)
                x_o(h)
            out_no.add(XH)

            with repeat(act, KT // 8, [(converted, 4), (out_no, 8)]) as i:
                for b in range(4):
                    units()
                    for n in range(2):
                        x_high(act_hi[:, i * 8 + (2 * b + n), :], i * 8 + (2 * b + n), G_FFN)

            std(4, ps[0], rstd, S)

            def ffn(last):
                with repeat(act, GROUP, [(converted, 4), (out_no, 2)]) as t:
                    units(2)
                    read_out()
                    nc.scalar.activation(sg[:], gt[:], ACT.Sigmoid).then_inc(sig_ready, 1)
                    units(2)
                    read_out()
                    nc.scalar.activation(act2_hi[:, t, :], gt[:], ACT.Copy).then_inc(hid_hi, 1)
                if last:
                    units(KT // 2 - AHEAD)
                else:
                    with repeat(act, 2, [(converted, 4)]):
                        units(4)
                    out_no.add(KT)

            with repeat(act, GROUPS - 1, [(converted, FFN_UNITS), (out_no, GROUP * 2 + KT)]):
                ffn(False)
            ffn(True)
            assert converted.n == UNITS
            std(5, ps[1], rstd, S)

        @block.vector
        def _(dve):
            hd, step, pair, out_no, tr, sig = Tally(), Tally(), Tally(), Tally(), Tally(), Tally()
            converted, swa, hid = Tally(), Tally(), Tally()

            def link(ins):
                ins.then_inc(dve_step, 1)
                step.add()
                dve.wait_ge(dve_step, step.at())

            def units(n=1):
                for _ in range(n):
                    s = converted.n % RING
                    dve.wait_ge(hi_done, converted.at(1))
                    nc.vector.tensor_tensor(w_lo[:, s, :], raw[:, s, :], f(w_hi[:, s, :]), ALU.subtract)\
                        .then_inc(lo_done, 1)
                    converted.add()

            def output():
                a = acc[out_no.n % 2]
                out_no.add()
                return a

            unit = Tally()

            def rstd_of(n, dst, width):
                dve.wait_ge(std_ready, n)
                nc.vector.reciprocal(dst[:, 0:width], dst[:, 0:width]).then_inc(rstd_ready, 1)
                dve.wait_ge(rstd_ready, n)

            def scale_out(dst, k=2):
                unit.add(k)
                dve.wait_ge(unit_done, unit.at())
                nc.vector.tensor_tensor(dst, output()[:], rstd[:], ALU.mult).then_inc(acc_free, 1)

            nc.vector.memset(stat_x[:, 2, :], 0.0).then_inc(hid_lo, 1)
            for n in range(2):
                nc.vector.memset(stat_x[:, n, :], 0.0).then_inc(ps_free, 1)
            dve.wait_ge(const_ready, 4)
            nc.vector.tensor_copy(ones_r[:], ones[:]).then_inc(const_r_ready, 1)
            nc.vector.tensor_copy(tri_r[:], scaled[:, 0:P]).then_inc(const_r_ready, 1)
            units(1)
            h = Tally()

            def x_low(dst, hi, m, gain):
                dve.wait_ge(h_hi, h.at(1))
                nc.vector.scalar_tensor_tensor(dst, x[:, m, :], par[:, bass.ds(m + gain, 1)], f(hi),
                                               ALU.mult, ALU.subtract).then_inc(h_lo, 1)
                h.add()

            for c in range(4):
                with repeat(dve, 4, [(h, 1)]) as i:
                    x_low(act_lo[:, 4 * c + i, :], act_hi[:, 4 * c + i, :], 4 * c + i, G_MIX)
                if c < 2:
                    units()

            def z_out(n):
                dve.wait_ge(z_done, hd.at(1 + n))
                nc.vector.scalar_tensor_tensor(zb[n][:], ps[n][:, 0:SB_COLS], HD ** -0.5, sb_mask[:],
                                               ALU.mult, ALU.add).then_inc(zb_ready, 1)

            def softplus(n):
                dve.wait_ge(soft_ready, hd.at(1 + n))
                nc.vector.scalar_tensor_tensor(pf[n][:], zb[n][:], 0.0, pf[n][:], ALU.max, ALU.add)\
                    .then_inc(p_ready, 1)
                dve.wait_ge(p_ready, hd.at(1 + n))
                nc.vector.tensor_tensor(zb[n][:], zb[n][:], pf[n][:], ALU.subtract).then_inc(lb_ready, 1)
                dve.wait_ge(p_hi_done, hd.at(1 + n))
                nc.vector.tensor_tensor(pa_lo[n][:], pf[n][:], f(pa_hi[n][:]), ALU.subtract)\
                    .then_inc(p_lo_done, 1)

            def tail(n):
                dve.wait_ge(t_done, hd.at(1 + n))
                nc.vector.tensor_tensor(zb[n][:], zb[n][:], ps[n][:, 0:SB_COLS], ALU.subtract)\
                    .then_inc(u_ready, 1)

            def a_low(n):
                dve.wait_ge(a_hi_done, hd.at(1 + n))
                nc.vector.tensor_tensor(pa_lo[n][:], pf[n][:], f(pa_hi[n][:]), ALU.subtract)\
                    .then_inc(a_lo_done, 1)

            def o_low(n):
                dve.wait_ge(o_hi_done, hd.at(1 + n))
                rows = slice(HD * n, HD * n + HD)
                nc.vector.tensor_tensor(o_lo[rows, pair.at(), :], ps[n][rows, 0:S], f(o_hi[rows, pair.at(), :]),
                                        ALU.subtract).then_inc(ps_free, 1)

            qk = Tally()

            def qk_out(hi, lo):
                if qk.loops or qk.n:
                    dve.wait_ge(qk_lo_done, qk.at())
                scale_out(scaled[:])
                dve.wait_ge(qk_hi_done, qk.at(1))
                nc.vector.tensor_tensor(lo[:], scaled[:], f(hi[:]), ALU.subtract).then_inc(qk_lo_done, 1)
                qk.add()

            def sb_body(attend, project):
                if attend:
                    z_out(0)
                    z_out(1)
                if project:
                    units()
                if attend:
                    dve.wait_ge(v_hi_done, tr.at(1))
                    nc.vector.tensor_tensor(v_lo[:], output()[:], f(v_hi[:]), ALU.subtract).then_inc(acc_free, 1)
                    tr.add()
                    softplus(0)
                if project:
                    units()
                if attend:
                    softplus(1)
                if project:
                    qk_out(q_hi, q_lo)
                    units()
                if attend:
                    tail(0)
                    a_low(0)
                if project:
                    units()
                if attend:
                    tail(1)
                    a_low(1)
                if project:
                    qk_out(k_hi, k_lo)
                    units()
                if attend:
                    o_low(0)
                if project:
                    units()
                    scale_out(vt[:])
                if attend:
                    o_low(1)
                    hd.add(2)
                    pair.add()

            units(3)
            rstd_of(1, rstd, S)
            qk_out(q_hi, q_lo)
            units()
            qk_out(k_hi, k_lo)
            units(2)
            scale_out(vt[:])
            with repeat(dve, (PAIRS - 2) // 2, [(converted, 12), (unit, 12), (hd, 4), (pair, 2), (out_no, 8),
                                                (tr, 2), (qk, 4)]):
                sb_body(True, True)
                sb_body(True, True)
            sb_body(True, True)
            sb_body(True, False)

            def gates(first_pass):
                with repeat(dve, KT // 4, [(converted, 12), (unit, 12), (out_no, 8), (sig, 4)]) as i:
                    for b in range(4):
                        m = i * 4 + b
                        g = gate[:, b % 2, :]
                        units(2)
                        scale_out(g)
                        units()
                        unit.add()
                        dve.wait_ge(unit_done, unit.at())
                        dve.wait_ge(sig_ready, sig.at(1))
                        dst = merged[:, m, :] if first_pass else g
                        nc.vector.tensor_tensor(dst, output()[:], g, ALU.mult).then_inc(acc_free, 1)
                        if not first_pass:
                            dve.wait_ge(acc_free, out_no.at())
                            nc.vector.tensor_tensor(merged[:, m, :], merged[:, m, :], g, ALU.add)\
                                .then_inc(mix_ready, 1)
                        sig.add()

            gates(True)

            dve.wait_ge(pos_in, 32)
            dve.wait_ge(const_ready, 5)
            link(nc.vector.tensor_copy(sin_t[:], ra[:].bitcast(I32)))
            link(nc.vector.tensor_scalar(sin_t[:], sin_t[:], rc[:, 0:1], None, ALU.mult))
            link(nc.vector.tensor_scalar(ra[:], sin_t[:], 1 / (2 * np.pi), None, ALU.mult))
            link(nc.vector.tensor_scalar(ra[:], ra[:], ROUND, None, ALU.add))
            link(nc.vector.tensor_scalar(ra[:], ra[:], -ROUND, None, ALU.add))
            for c in TWO_PI:
                link(nc.vector.scalar_tensor_tensor(sin_t[:], ra[:], -c, sin_t[:], ALU.mult, ALU.add))
            link(nc.vector.tensor_scalar(cos_t[:], sin_t[:], np.pi / 2, None, ALU.add))
            link(nc.vector.tensor_scalar(ra[:], cos_t[:], np.pi, -2 * np.pi, ALU.is_gt, ALU.mult))
            link(nc.vector.tensor_tensor(cos_t[:], cos_t[:], ra[:], ALU.add))
            link(nc.vector.tensor_scalar(cos_t[:], cos_t[:], PI_DOWN, -PI_DOWN, ALU.min, ALU.max))
            nc.vector.tensor_scalar(sin_t[:], sin_t[:], PI_DOWN, -PI_DOWN, ALU.min, ALU.max).then_inc(ang_ready, 1)

            rot = Tally()

            def rope(dst, k=2):
                dve.wait_ge(qa_ready, rot.at())
                scale_out(ra[:], k)
                dve.wait_ge(rot_ready, rot.at(1))
                link(nc.vector.tensor_tensor(ra[:], ra[:], cos_t[:], ALU.mult))
                link(nc.vector.tensor_tensor(rb[:], rb[:], sin_t[:], ALU.mult))
                nc.vector.tensor_tensor(dst, ra[:], rb[:], ALU.add).then_inc(qa_ready, 1)
                rot.add()

            def v_out(n, width, dst):
                dve.wait_ge(tr_done, tr.at(1))
                nc.vector.tensor_copy(dst, output()[:].rearrange("p (a b) -> p a b", b=width)).then_inc(acc_free, 1)
                tr.add()

            def swa_max(hf):
                dve.wait_ge(s_done, swa.at(1 + hf))
                mask = band[:] if hf == 0 else band[:, 1:2, :].broadcast_to([P, 2, 2 * P])
                for n in range(2):
                    last = nc.vector.scalar_tensor_tensor(
                        s_a[:, 2 * n:2 * n + 2, :], ps[hf][:, S * n:S * (n + 1)].rearrange("p (a b) -> p a b", a=2),
                        HD ** -0.5, mask, ALU.mult, ALU.add)
                link(last)
                link(nc.vector.reduce_max(stat_a[:, 0, :], s_a[:], AX.X))
                for n in range(2):
                    last = nc.vector.tensor_scalar(stat_a[:, 0, 2 * n:2 * n + 2], stat_a[:, 0, 2 * n:2 * n + 2],
                                                   par[:, bass.ds(pair.at() * 2 + (SINK + n), 1)], None, ALU.max)
                link(last)
                link(nc.vector.tensor_scalar(stat_a[:, 1, :], stat_a[:, 0, :], -1.0, None, ALU.mult))
                for n in range(2):
                    last = nc.vector.tensor_scalar(stat_a[:, 2, 2 * n:2 * n + 2], stat_a[:, 1, 2 * n:2 * n + 2],
                                                   par[:, bass.ds(pair.at() * 2 + (SINK + n), 1)], None, ALU.add)
                last.then_inc(max_ready, 1)

            def swa_prob(hf):
                dve.wait_ge(exp_ready, swa.at(1 + hf))
                link(nc.vector.tensor_tensor(stat_a[:, 5, :], stat_a[:, 3, :], stat_a[:, 4, :], ALU.add))
                link(nc.vector.reciprocal(stat_a[:, 5, :], stat_a[:, 5, :]))
                nc.vector.tensor_tensor(s_a[:], s_a[:], stat_a[:, 5, :].unsqueeze(2).broadcast_to([P, 4, 2 * P]),
                                        ALU.mult).then_inc(prob_ready, 1)

            def swa_o(hf):
                dve.wait_ge(o_hi_done, hd.at(1 + hf))
                for n in range(2):
                    rows = slice(HD * n, HD * n + HD)
                    cols = slice(2 * P * hf, 2 * P * (hf + 1))
                    last = nc.vector.tensor_tensor(o_lo[rows, pair.at(), cols],
                                                   ps[hf][rows, 2 * S + 2 * P * n:2 * S + 2 * P * (n + 1)],
                                                   f(o_hi[rows, pair.at(), cols]), ALU.subtract)
                last.then_inc(ps_free, 1)

            def swa_body(attend, project):
                if attend:
                    swa_max(0)
                    swa_prob(0)
                if project:
                    units()
                if attend:
                    dve.wait_ge(ptr_done, swa.at(1))
                    swa_max(1)
                    swa_prob(1)
                if project:
                    units()
                if attend:
                    swa_o(0)
                    swa_o(1)
                if project:
                    rope(qa[:])
                if attend:
                    swa.add(2)
                    hd.add(2)
                    pair.add()

            units(4)
            scale_out(ra[:])
            scale_out(rb[:])
            dve.wait_ge(trig_ready, 1)
            link(nc.vector.tensor_scalar(sin_t[:], sin_t[:], rc[:, 1:2], None, ALU.mult))
            units(2)
            dve.wait_ge(tr_done, PAIRS + 1)
            scale_out(ra[:])
            v_out(0, P, va[:, :, 0:P])
            v_out(1, P, va[:, :, P:2 * P])
            dve.wait_ge(rot_ready, 1)
            link(nc.vector.tensor_tensor(ra[:], ra[:], cos_t[:], ALU.mult))
            link(nc.vector.tensor_tensor(rb[:], rb[:], sin_t[:], ALU.mult))
            nc.vector.tensor_tensor(ka[:, 0, :], ra[:], rb[:], ALU.add).then_inc(qa_ready, 1)
            rot.add()
            units(2)
            rope(ka[:, 1, :])
            pair.n = 0
            swa_body(False, True)
            for turns in (2, 1):
                with repeat(dve, turns, [(converted, 4), (unit, 4), (swa, 4), (hd, 4), (pair, 2), (out_no, 2),
                                         (rot, 2), (step, SWA_STEPS)]):
                    swa_body(True, True)
                    swa_body(True, True)
            swa_body(True, True)
            swa_body(True, False)

            gates(False)

            with dve.Fori(0, KT) as m:
                dve.wait_ge(mg_hi, m + 1)
                nc.vector.tensor_tensor(act_lo[:, m, :], merged[:, m, :], f(act_hi[:, m, :]), ALU.subtract)\
                    .then_inc(mg_lo, 1)

            def add_out(m):
                nc.vector.tensor_tensor(x[:, m, :], x[:, m, :], output()[:], ALU.add).then_inc(acc_free, 1)

            for c in range(4):
                dve.wait_ge(x_in[c], 32)
                for b in range(4):
                    units()
                    unit.add()
                    dve.wait_ge(unit_done, unit.at())
                    add_out(4 * c + b)

            for half, hi, lo in ((0, act_hi, act_lo), (1, act2_hi, act2_lo)):
                with repeat(dve, 2, [(converted, 4), (unit, 4), (out_no, 4), (h, 4)]) as i:
                    for b in range(4):
                        units()
                        unit.add()
                        dve.wait_ge(unit_done, unit.at())
                        add_out(i * 4 + (b + UK * half))
                        x_low(lo[:, i * 4 + b, :], hi[:, i * 4 + b, :], i * 4 + (b + UK * half), G_CROSS)

            mems = Tally()
            for p in range(XH):
                units(2)
                with repeat(dve, 4, [(mems, 1)]) as i:
                    dve.wait_ge(mem_hi, mems.at(1))
                    nc.vector.scalar_tensor_tensor(mem_lo_v[:, i + 4 * p, :], mem[:, i + 4 * p, :],
                                                   par[:, bass.ds(i + (4 * p + G_MEM), 1)],
                                                   f(mem_hi_v[:, i + 4 * p, :]), ALU.mult, ALU.subtract)\
                        .then_inc(mem_lo, 1)
                    mems.add()
                if p == 0:
                    rstd_of(2, rstd, S)
                scale_out(qx[:, p, :])

            def kv_out(dst):
                unit.add(2)
                dve.wait_ge(unit_done, unit.at())
                nc.vector.tensor_tensor(dst, output()[:, 0:NM], mem_stat[:], ALU.mult).then_inc(acc_free, 1)

            units(3)
            rstd_of(3, mem_stat, NM)
            kv_out(kx[:, 0, :])
            units(1)
            kv_out(kx[:, 1, :])
            units(2)
            kv_out(kx[:, 2, :])
            units(2)
            kv_out(kx[:, 3, :])

            def x_max(n):
                dve.wait_ge(s_done, swa.at(1))
                link(nc.vector.reduce_max(stat_x[:, 0, :], ps[n % 2][:, 0:4 * NM].rearrange("p (a b) -> p a b", a=4),
                                          AX.X))
                nc.vector.tensor_scalar(stat_x[:, 1, :], stat_x[:, 0, :], -XD ** -0.5, None, ALU.mult)\
                    .then_inc(max_ready, 1)

            def x_prob(n):
                dve.wait_ge(exp_ready, swa.at(1))
                link(nc.vector.reciprocal(stat_x[:, 0, :], stat_x[:, 2, :]))
                nc.vector.tensor_tensor(s_x[:], s_x[:], stat_x[:, 0, :].unsqueeze(2).broadcast_to([P, 4, NM]),
                                        ALU.mult).then_inc(prob_ready, 1)
                swa.add()

            def x_o(n):
                dve.wait_ge(o_hi_done, hd.at(1))
                nc.vector.tensor_tensor(act2_lo[:, n, :], ps[n % 2][:, 2 * S:3 * S], f(act2_hi[:, n, :]),
                                        ALU.subtract).then_inc(ps_free, 1)
                hd.add()

            x_max(0)
            units(2)
            kv_out(vt[:, 0:NM])
            x_prob(0)
            units(2)
            kv_out(vt[:, NM:2 * NM])
            units(2)
            dve.wait_ge(tr_done, PAIRS + 3)
            kv_out(vt[:, 0:NM])
            v_out(0, XD, vx[:, :, 0:2 * XD].rearrange("p a (h b) -> p h a b", h=2))
            units(2)
            kv_out(vt[:, NM:2 * NM])
            v_out(1, XD, vx[:, :, 2 * XD:4 * XD].rearrange("p a (h b) -> p h a b", h=2))
            for n in range(XH):
                if n + 1 < XH:
                    x_max(n + 1)
                    x_prob(n + 1)
                x_o(n)

            with repeat(dve, KT // 8, [(converted, 4), (unit, 4), (out_no, 8), (h, 8)]) as i:
                for b in range(4):
                    units()
                    for n in range(2):
                        m = i * 8 + (2 * b + n)
                        dve.wait_ge(half_done if n == 0 else unit_done, unit.at(1 - (0 if n else U_XO)))
                        add_out(m)
                        x_low(act_lo[:, m, :], act_hi[:, m, :], m, G_FFN)
                    unit.add()

            rstd_of(4, rstd, S)
            half = Tally(KT // 2)

            def ffn(last):
                with repeat(dve, GROUP, [(converted, 4), (unit, 4), (out_no, 2), (sig, 1), (step, 2), (hid, 1)]) as t:
                    units(2)
                    dve.wait_ge(hid_lo, hid.at(1))
                    scale_out(gt[:])
                    dve.wait_ge(sig_ready, sig.at(1))
                    link(nc.vector.tensor_tensor(gt[:], gt[:], sg[:], ALU.mult))
                    link(nc.vector.tensor_tensor(gt[:], gt[:], rstd[:], ALU.mult))
                    sig.add()
                    units(2)
                    unit.add(2)
                    dve.wait_ge(unit_done, unit.at())
                    nc.vector.tensor_tensor(gt[:], gt[:], output()[:], ALU.mult).then_inc(acc_free, 1)
                    dve.wait_ge(hid_hi, hid.at(1))
                    nc.vector.tensor_tensor(act2_lo[:, t, :], gt[:], f(act2_hi[:, t, :]), ALU.subtract)\
                        .then_inc(hid_lo, 1)
                    hid.add()

                def down(m, split):
                    if split:
                        units()
                    dve.wait_ge(half_done, half.at(1))
                    add_out(m)
                    dve.wait_ge(unit_done, unit.at(1))
                    add_out(m + 1)
                    unit.add()
                    half.add()

                if last:
                    for n in range(KT // 2):
                        down(2 * n, n < KT // 2 - AHEAD)
                else:
                    with repeat(dve, 2, [(converted, 4), (unit, 4), (out_no, 8), (half, 4)]) as i:
                        for b in range(4):
                            down(i * 8 + 2 * b, True)

            with repeat(dve, GROUPS - 1, [(converted, FFN_UNITS), (unit, FFN_UNITS), (out_no, GROUP * 2 + KT),
                                          (sig, GROUP), (step, 2 * GROUP), (hid, GROUP), (half, KT // 2)]):
                ffn(False)
            ffn(True)
            assert out_no.n == A_END and unit.n == UNITS and converted.n == UNITS

            rstd_of(5, rstd, S)
            with dve.Fori(0, KT) as m:
                nc.vector.scalar_tensor_tensor(x[:, m, :], x[:, m, :], par[:, bass.ds(m + G_FINAL, 1)], rstd[:],
                                               ALU.mult, ALU.mult).then_inc(out_ready, 1)

        @block.tensor
        def _(pe):
            u, out_no, hd, tr, swa = Tally(), Tally(), Tally(), Tally(), Tally()
            half, hid = Tally(), Tally()

            def output():
                a = acc[out_no.n % 2]
                if out_no.loops or out_no.n >= 2:
                    pe.wait_ge(acc_free, out_no.at(-1))
                out_no.add()
                return a

            def split_products(dst, pairs):
                for n, (wh, wl, ah, al) in enumerate(pairs):
                    nc.tensor.matmul(dst, wh, ah, start=n == 0, stop=False)
                    nc.tensor.matmul(dst, wh, al, start=False, stop=False)
                    last = nc.tensor.matmul(dst, wl, ah, start=False, stop=n == len(pairs) - 1)
                return last

            def unit(dst, tiles, start, stop, arrive=None):
                s = u.n % RING
                pe.wait_ge(lo_done, u.at(1))
                for k, (ah, al) in enumerate(tiles):
                    if arrive:
                        pe.wait_ge(*arrive(k))
                    wh, wl = (t[:, s, P * k:P * (k + 1)] for t in (w_hi, w_lo))
                    nc.tensor.matmul(dst, wh, ah, start=start and k == 0, stop=False)
                    nc.tensor.matmul(dst, wh, al, start=False, stop=False)
                    last = nc.tensor.matmul(dst, wl, ah, start=False, stop=stop and k == UK - 1)
                last.then_inc(unit_done, 1)
                u.add()

            def two_outputs(hidden=None):
                s = u.n % RING
                pe.wait_ge(lo_done, u.at(1))
                for n in range(2):
                    dst = output()[:]
                    for k in range(GROUP):
                        if hidden is not None and n == 0 and k % (GROUP - 1) == 0:
                            pe.wait_ge(hid_lo, hidden + (1 if k else 0))
                        ah, al = act2_tile(k)
                        wh, wl = (t[:, s, P * (GROUP * n + k):P * (GROUP * n + k + 1)] for t in (w_hi, w_lo))
                        nc.tensor.matmul(dst, wh, ah, start=k == 0, stop=False)
                        nc.tensor.matmul(dst, wh, al, start=False, stop=False)
                        last = nc.tensor.matmul(dst, wl, ah, start=False, stop=k == GROUP - 1)
                    last.then_inc(unit_done if n else half_done, 1)
                u.add()

            def panel(tile, width=S, arrive=None):
                dst = output()[:, 0:width]
                for n in range(2):
                    unit(dst, [tile(UK * n + k) for k in range(UK)], n == 0, n == 1,
                         arrive and (lambda k, n=n: arrive(UK * n + k)))

            def stat(n, squares, bank, src, width):
                pe.wait_ge(sq_done, squares)
                nc.tensor.matmul(bank[:, 0:width], ones[:], src[:, 0:width], start=True, stop=True)\
                    .then_inc(stat_done, 1)

            def scores(n):
                if n == 0:
                    pe.wait_ge(qk_lo_done, hd.at(2))
                pe.wait_ge(ps_free, hd.at(n + 1))
                rows = slice(HD * n, HD * n + HD)
                for j in range(QT):
                    keys, cols = slice(P * j, P * (j + 1)), slice(P * j, S)
                    last = split_products(ps[n][:, SB_OFF[j]:SB_OFF[j] + SB_LEN[j]],
                                          [(k_hi[rows, keys], k_lo[rows, keys], q_hi[rows, cols], q_lo[rows, cols])])
                last.then_inc(z_done, 1)

            def tails(n):
                pe.wait_ge(p_lo_done, hd.at(1 + n))
                for j in range(QT):
                    terms = [(tri_r, j)] + [(ones_r, i) for i in range(j + 1, QT)]
                    for m, (mat, i) in enumerate(terms):
                        dst = ps[n][:, SB_OFF[j] + P * (i - j):SB_OFF[j] + SB_LEN[j]]
                        cols = slice(SB_OFF[i], SB_OFF[i] + SB_LEN[i])
                        nc.tensor.matmul(dst, mat[:], pa_hi[n][:, cols], start=m == 0, stop=False)
                        last = nc.tensor.matmul(dst, mat[:], pa_lo[n][:, cols], start=False, stop=m == len(terms) - 1)
                last.then_inc(t_done, 1)

            def values(n):
                if n == 0:
                    pe.wait_ge(acc_free, v_out_no.at())
                pe.wait_ge(a_lo_done, hd.at(1 + n))
                for j in range(QT):
                    toks, cols = slice(P * j, P * (j + 1)), slice(SB_OFF[j], SB_OFF[j] + SB_LEN[j])
                    dst = ps[n][:, P * j:S]
                    nc.tensor.matmul(dst, v_hi[:, toks], pa_hi[n][:, cols], start=j == 0, stop=False)
                    nc.tensor.matmul(dst, v_hi[:, toks], pa_lo[n][:, cols], start=False, stop=False)
                    last = nc.tensor.matmul(dst, v_lo[:, toks], pa_hi[n][:, cols], start=False, stop=j == QT - 1)
                last.then_inc(pv_done, 1)

            v_out_no = Tally(4)

            def turn(src, blocks):
                dst = output()
                for b in range(blocks):
                    last = nc.tensor.transpose(dst[:, P * b:P * (b + 1)], src[:, P * b:P * (b + 1)], ident[:])
                last.then_inc(tr_done, 1)
                tr.add()

            def sb_body(attend, project):
                if attend:
                    scores(0)
                    scores(1)
                    pe.wait_ge(acc_free, out_no.at())
                    turn(vt, QT)
                if project:
                    panel(act_tile)
                if attend:
                    tails(0)
                if project:
                    dst = output()[:]
                    unit(dst, [act_tile(k) for k in range(UK)], True, False)
                if attend:
                    tails(1)
                if project:
                    unit(dst, [act_tile(UK + k) for k in range(UK)], False, True)
                if attend:
                    values(0)
                if project:
                    panel(act_tile)
                if attend:
                    values(1)
                    hd.add(2)
                    v_out_no.add(4)

            pe.wait_ge(const_r_ready, 2)
            panel(act_tile, arrive=lambda k: (h_lo, k + 1))
            panel(act_tile)
            stat(1, 1, ps[0], sq_sum, S)
            panel(act_tile)
            with repeat(pe, (PAIRS - 2) // 2, [(u, 12), (out_no, 8), (hd, 4), (tr, 2), (v_out_no, 8)]):
                sb_body(True, True)
                sb_body(True, True)
            sb_body(True, True)
            sb_body(True, False)
            assert out_no.n == A_DB and u.n == U_DB

            def gates(o_written):
                with repeat(pe, KT // 4, [(u, 12), (out_no, 8)]):
                    for b in range(4):
                        panel(act_tile)
                        if b == 0:
                            pe.wait_ge(ps_free, 2 + o_written)
                        unit(output()[:], [o_tile(k) for k in range(UK)], True, True)

            gates(2 * PAIRS)
            assert out_no.n == A_SWA and u.n == U_SWA

            def swa_scores(hf, kt):
                if hf == 0:
                    pe.wait_ge(qa_ready, roped.at(1))
                pe.wait_ge(ps_free, hd.at(hf + 1))
                for i in range(2):
                    t = 2 * hf + i
                    for n in range(2):
                        rows = slice(HD * n, HD * n + HD)
                        for side, kb in ((0, max(t - 1, 0)), (1, t)):
                            at = S * n + 2 * P * i + P * side
                            last = nc.tensor.matmul(ps[hf][:, at:at + P], qa[rows, P * t:P * (t + 1)],
                                                    ka[rows, kt, P * kb:P * (kb + 1)], start=True, stop=True)
                last.then_inc(s_done, 1)

            def swa_turn(hf):
                pe.wait_ge(prob_ready, swa.at(1 + hf))
                for b in range(8):
                    last = nc.tensor.transpose(ps[hf][:, P * b:P * (b + 1)],
                                               s_a[:, b // 2, P * (b % 2):P * (b % 2 + 1)], ident[:])
                last.then_inc(ptr_done, 1)

            def swa_values(hf, kt):
                pe.wait_ge(pt_ready, swa.at(1 + hf))
                for n in range(2):
                    for i in range(2):
                        t = 2 * hf + i
                        dst = ps[hf][:, 2 * S + P * (2 * n + i):2 * S + P * (2 * n + i + 1)]
                        sides = [(1, t)] + ([(0, t - 1)] if t else [])
                        for m, (side, kb) in enumerate(sides):
                            b = 2 * (2 * n + i) + side
                            last = nc.tensor.matmul(dst, va[:, kb, P * kt:P * (kt + 1)], pt_a[:, P * b:P * (b + 1)],
                                                    start=m == 0, stop=m == len(sides) - 1)
                last.then_inc(pv_done, 1)

            roped = Tally(2)

            def swa_body(kt, attend, project):
                if attend:
                    swa_scores(0, kt)
                    swa_scores(1, kt)
                if project:
                    dst = output()[:]
                    unit(dst, [act_tile(k) for k in range(UK)], True, False)
                if attend:
                    swa_turn(0)
                if project:
                    unit(dst, [act_tile(UK + k) for k in range(UK)], False, True)
                if attend:
                    swa_values(0, kt)
                    swa_turn(1)
                    swa_values(1, kt)
                    swa.add(2)
                    hd.add(2)
                    roped.add()

            panel(act_tile)
            panel(act_tile)
            panel(act_tile)
            turn(ra, QT)
            turn(rb, QT)
            panel(act_tile)
            swa_body(0, False, True)
            for kt, turns in ((0, 2), (1, 1)):
                with repeat(pe, turns, [(u, 4), (out_no, 2), (swa, 4), (hd, 4), (roped, 2)]):
                    swa_body(kt, True, True)
                    swa_body(kt, True, True)
            swa_body(1, True, True)
            swa_body(1, True, False)
            assert out_no.n == A_DA and u.n == U_DA

            gates(4 * PAIRS)
            assert out_no.n == A_OUT and u.n == U_OUT

            pe.wait_ge(mg_lo, UK)
            for n in range(2):
                if n:
                    pe.wait_ge(mg_lo, KT)
                with repeat(pe, KT // 4, [(u, 4), (out_no, 4)]):
                    for b in range(4):
                        unit(output()[:], [act_tile(UK * n + k) for k in range(UK)], True, True)

            panel(hc_tile, arrive=lambda k: (h_lo, KT + k + 1))
            stat(2, 3, ps[0], sq_sum, S)
            for _ in range(XH - 1):
                panel(hc_tile)
            panel(mem_tile, NM, arrive=lambda k: (mem_lo, k + 1))
            stat(3, 2, ps[1], mem_stat, NM)
            for _ in range(XH - 1):
                panel(mem_tile, NM)

            def x_scores(n):
                for t in range(QT):
                    last = nc.tensor.matmul(ps[n % 2][:, NM * t:NM * (t + 1)], qx[:, n, P * t:P * (t + 1)],
                                            kx[:, n, :], start=True, stop=True)
                last.then_inc(s_done, 1)

            def x_turn(n):
                pe.wait_ge(prob_ready, swa.at(1))
                for b in range(2):
                    for t in range(QT):
                        last = nc.tensor.transpose(ps[n % 2][:, S * b + P * t:S * b + P * (t + 1)],
                                                   s_x[:, t, P * b:P * (b + 1)], ident[:])
                last.then_inc(ptr_done, 1)

            def x_values(n):
                pe.wait_ge(pt_ready, swa.at(1))
                for b in range(2):
                    last = nc.tensor.matmul(ps[n % 2][:, 2 * S:3 * S], vx[:, b, XD * n:XD * (n + 1)], pt_x[:, b, :],
                                            start=b == 0, stop=b == 1)
                last.then_inc(pv_done, 1)
                swa.add()

            pe.wait_ge(acc_free, A_XKV + XH)
            x_scores(0)
            panel(mem_tile, NM)
            panel(mem_tile, NM)
            pe.wait_ge(acc_free, out_no.at())
            panel(mem_tile, NM)

            def v_turn():
                dst = output()
                for b in range(4):
                    last = nc.tensor.transpose(dst[:, P * b:P * (b + 1)], vt[:, P * b:P * (b + 1)], ident[:])
                last.then_inc(tr_done, 1)

            v_turn()
            panel(mem_tile, NM)
            pe.wait_ge(acc_free, out_no.at())
            v_turn()
            x_scores(1)
            for n in range(XH):
                x_turn(n)
                if n == 0:
                    pe.wait_ge(acc_free, out_no.at())
                x_values(n)
                if n + 2 < XH:
                    pe.wait_ge(ps_free, 4 * PAIRS + n + 3)
                    x_scores(n + 2)

            pe.wait_ge(ps_free, 4 * PAIRS + XH + 2)
            with repeat(pe, KT // 8, [(u, 4), (out_no, 8)]):
                for b in range(4):
                    two_outputs()

            stat(4, 4, ps[0], sq_sum, S)
            pe.wait_ge(h_lo, 3 * KT)

            def ffn():
                with repeat(pe, GROUP, [(u, 4), (out_no, 2)]):
                    panel(act_tile)
                    panel(act_tile)
                hid.add(GROUP)
                with repeat(pe, 2, [(u, 4), (out_no, 8)]):
                    for b in range(4):
                        two_outputs(hid.at() if b == 0 else None)

            with repeat(pe, GROUPS - 1, [(u, FFN_UNITS), (out_no, GROUP * 2 + KT), (hid, GROUP)]):
                ffn()
            ffn()
            assert out_no.n == A_END and u.n == UNITS
            stat(5, 5, ps[1], sq_sum, S)


def stream(m, halves_outside=False):
    k, n = m.shape
    b = m.reshape(k // P, P, n // P, P)
    if halves_outside:
        b = b.reshape(k // P // UK, UK, P, n // P, P).transpose(0, 3, 2, 1, 4)
    else:
        b = b.transpose(2, 0, 1, 3).reshape(-1, UK, P, P).transpose(0, 2, 1, 3)
    return b.reshape(-1, P, UK * P)


def columns(m, n):
    return m[:, P * n:P * (n + 1)]


GQ = SWA_HEADS // SWA_KV
LOWER = [g * GQ + i for g in range(0, SWA_KV, 2) for i in range(GQ)]
HEADS = [h + o * GQ for h in LOWER for o in (0, 1)]


def weight_stream(w_in, w_gate, w_a, w_b, w_out, w_xq, w_xkv, w_xo, w_gu, w_down):
    qa, ka, va, qb, kb, vb = np.split(w_in, np.cumsum([SWA_W, KV_W, KV_W, SB_W, SB_W]), axis=1)
    qa = qa.reshape(D, SWA_HEADS, HD)[:, HEADS].reshape(D, SWA_W)
    w_a = w_a.reshape(SWA_HEADS, HD, D)[HEADS].reshape(SWA_W, D)
    parts = [stream(columns(m, p)) for p in range(PAIRS) for m in (qb, kb, vb)]
    parts += [stream(x) for m in range(KT) for x in (columns(w_gate, KT + m), columns(w_b, m))]
    parts += [stream(columns(va, 0)), stream(columns(va, 1)), stream(ka), stream(qa)]
    parts += [stream(x) for m in range(KT) for x in (columns(w_gate, m), columns(w_a, m))]
    parts += [stream(w_out, True), stream(w_xq), stream(w_xkv), stream(w_xo)]
    width = GROUP * P
    for g in range(GROUPS):
        for t in range(GROUP):
            parts += [stream(columns(w_gu, g * GROUP + t)), stream(columns(w_gu, FFN // P + g * GROUP + t))]
        parts += [stream(w_down[width * g:width * (g + 1)])]
    return np.concatenate(parts)


def tiles(v):
    return v.reshape(-1, P).T


def kernel(x, mem, positions, norm_mix_g, w_in, sinks, w_branch_a, w_branch_b, w_gate, b_gate, w_out,
           norm_cross_g, norm_mem_g, w_xq, w_xkv, w_xo, norm_ffn_g, w_gu, w_down, final_norm_g):
    import concourse.bacc as bacc
    from concourse.bass_utils import run_bass_kernel_spmd

    a = {k: np.asarray(v) for k, v in locals().items() if k not in ("bacc", "run_bass_kernel_spmd")}
    w = weight_stream(*(a[k][0] for k in ("w_in", "w_gate", "w_branch_a", "w_branch_b", "w_out", "w_xq", "w_xkv",
                                          "w_xo", "w_gu", "w_down")))
    params = np.concatenate(
        [tiles(a[k].reshape(-1)) for k in ("norm_mix_g", "norm_cross_g", "norm_mem_g", "norm_ffn_g", "final_norm_g",
                                           "b_gate")]
        + [np.broadcast_to(a["sinks"][0][HEADS], (P, SWA_HEADS))], axis=1)
    inv = (ROPE_THETA ** (-np.arange(HALF, dtype=np.float64) / HALF)).astype(np.float32)
    sign = np.repeat(np.array([-1, 1], np.float32), HALF)
    arrays = {
        "w_stream": w,
        "x_t": a["x"][0].T.reshape(KT, P, S).transpose(1, 0, 2),
        "mem_t": a["mem"][0].T.reshape(KT, P, NM).transpose(1, 0, 2),
        "params": params,
        "rope_const": np.stack([np.tile(inv, P // HALF), np.tile(sign, P // HD)], axis=1),
        "pos": np.broadcast_to(a["positions"].astype(np.int32), (P, S)),
    }
    arrays = {k: np.ascontiguousarray(v) for k, v in arrays.items()}
    nc = bacc.Bacc("TRN2", target_bir_lowering=False, num_devices=1)
    args = [nc.dram_tensor(k, v.shape, mybir.dt.from_np(v.dtype), kind="ExternalInput").ap() for k, v in arrays.items()]
    out = nc.dram_tensor("out_t", (KT, P, S), mybir.dt.float32, kind="ExternalOutput").ap()
    block_kernel(nc, *args, out)
    r = run_bass_kernel_spmd(nc, [arrays], core_ids=[0])
    return r.results[0]["out_t"].reshape(D, S).T[None]
```

```python
import numpy as np
from contextlib import ExitStack, contextmanager

import concourse.bass as bass
from concourse import mybir

P = 128
D = 2048
S = 512
KT = D // P
HD = 64
HALF = HD // 2
SWA_HEADS, SWA_KV = D // 128, D // 128 // 4
SWA_W, KV_W = SWA_HEADS * HD, SWA_KV * HD
SB_W = (D // 128) * HD
PAIRS = SB_W // P
MIX_KT = SB_W // P
NM = 256
XH, XD = 4, 128
FFN = -(-8 * D // 768) * 256
UK = 8
RING = 4
AHEAD = RING - 1
GROUP = 4
GROUPS = FFN // P // GROUP
CHUNK = 64
EPS = 1e-6
NEG = -1e30
ROPE_THETA = 10000.0
QT = S // P

U_SB = 0
U_DB = U_SB + PAIRS * 6
U_SWA = U_DB + KT * 3
U_DA = U_SWA + 4 * 2 + PAIRS * 2
U_OUT = U_DA + KT * 3
U_XQ = U_OUT + KT * 2
U_XKV = U_XQ + XH * 2
U_XO = U_XKV + 2 * XH * 2
U_FFN = U_XO + KT // 2
FFN_UNITS = GROUP * 4 + KT // 2
UNITS = U_FFN + GROUPS * FFN_UNITS

A_DB = PAIRS * 4
A_SWA = A_DB + KT * 2
A_DA = A_SWA + 6 + PAIRS
A_OUT = A_DA + KT * 2
A_XQ = A_OUT + KT * 2
A_XKV = A_XQ + XH
A_XO = A_XKV + 2 * XH + 2
A_FFN = A_XO + KT
A_END = A_FFN + GROUPS * (GROUP * 2 + KT)

G_MIX, G_CROSS, G_MEM, G_FFN, G_FINAL = (KT * n for n in range(5))
B_GATE = 5 * KT
SINK = B_GATE + 2 * KT
PARAMS = SINK + SWA_HEADS

SB_OFF = (0, 512, 1024, 896)
SB_LEN = tuple(S - P * j for j in range(QT))
SB_COLS = sum(SB_LEN)


ROUND = float(3 << 22)
TWO_PI = (6.28125, 0.0019350051879882812, float(2 * np.pi - 6.28125 - 0.0019350051879882812))
PI_DOWN = 3.1415925


POOL_TILES = (1, 3, 5, 7, 9, 11)
OTHER_TILES = tuple(m for m in range(KT) if m not in POOL_TILES)


class Tally:

    def __init__(self, n=0):
        self.n, self.loops = n, []

    def at(self, k=0):
        v = self.n + k
        for i, stride in self.loops:
            v = i * stride + v
        return v

    def add(self, k=1):
        self.n += k


@contextmanager
def repeat(eng, times, strides):
    with eng.Fori(0, times) as i:
        began = [(t, t.n, s) for t, s in strides]
        for t, s in strides:
            t.loops.append((i, s))
        yield i
        for t, n, s in began:
            assert t.n - n == s, (t.n - n, s)
            t.n = n + s * times
            t.loops.pop()


def block_kernel(nc, w, xT, memT, params, rope_const, pos, out):
    F32, F32R, BF16, I32 = mybir.dt.float32, mybir.dt.float32r, mybir.dt.bfloat16, mybir.dt.int32
    ALU, ACT, AX = mybir.AluOpType, mybir.ActivationFunctionType, mybir.AxisListType
    ctx = ExitStack()
    with ctx:
        def sb(name, shape, dt, stack=ctx):
            return stack.enter_context(nc.sbuf_tensor(name, shape, dt))

        def sem(name):
            return ctx.enter_context(nc.semaphore(name))

        stat_x = sb("stat_x", [P, 3, 4], F32)
        par = sb("par", [P, PARAMS], F32)
        rc = sb("rc", [P, 2], F32)
        ident = sb("ident", [P, P], F32)
        ones = sb("ones", [P, P], F32)
        ones_r = sb("ones_r", [P, P], F32R)
        tri_r = sb("tri_r", [P, P], F32R)
        eps_t = sb("eps_t", [P, 1], F32)
        rstd = sb("rstd", [P, S], F32)
        sq_sum = sb("sq_sum", [P, S], F32)
        act_hi = sb("act_hi", [P, KT, S], F32R)
        act_lo = sb("act_lo", [P, KT, S], F32R)
        raw = sb("raw", [P, RING, UK * P], F32)
        w_hi = sb("w_hi", [P, RING, UK * P], F32R)
        w_lo = sb("w_lo", [P, RING, UK * P], F32R)

        with ExitStack() as a:
            x = sb("x", [P, KT, S], F32, a)
        o_hi = sb("o_hi", [P, MIX_KT, S], F32R)
        o_lo = sb("o_lo", [P, MIX_KT, S], F32R)

        with ExitStack() as a:
            sb_mask = sb("sb_mask", [P, SB_COLS], BF16, a)
            zb = [sb(f"zb{n}", [P, SB_COLS], F32, a) for n in range(2)]
            pf = [sb(f"pf{n}", [P, SB_COLS], F32, a) for n in range(2)]
            pa_hi = [sb(f"pa_hi{n}", [P, SB_COLS], F32R, a) for n in range(2)]
            pa_lo = [sb(f"pa_lo{n}", [P, SB_COLS], F32R, a) for n in range(2)]
            q_hi, k_hi, v_hi = (sb(f"{n}_hi", [P, S], F32R, a) for n in "qkv")
            q_lo, k_lo, v_lo = (sb(f"{n}_lo", [P, S], F32R, a) for n in "qkv")
            scaled = sb("scaled", [P, S], F32, a)
        vt = rb = sq_sum

        with ExitStack() as a:
            merged = sb("merged", [P, KT, S], F32, a)
        act2_hi = sb("act2_hi", [P, UK, S], F32R)
        act2_lo = sb("act2_lo", [P, UK, S], F32R)

        with ExitStack() as a:
            cos_t = sb("cos_t", [P, S], F32, a)
            sin_t = sb("sin_t", [P, S], F32, a)
            ka = sb("ka", [P, 2, S], F32, a)
            va = sb("va", [P, QT, KV_W], F32, a)
            qa = sb("qa", [P, S], F32, a)
            ra = sb("ra", [P, S], F32, a)
            s_a = sb("s_a", [P, 4, 2 * P], F32, a)
            pt_a = sb("pt_a", [P, 8 * P], F32, a)
            band = sb("band", [P, 2, 2 * P], BF16, a)
            stat_a = sb("stat_a", [P, 2, 6, 4], F32, a)
        mem_stat = sb("mem_stat", [P, NM], F32)
        qx = sb("qx", [P, XH, S], F32)
        with ExitStack() as a:
            mem = sb("mem", [P, KT, NM], F32, a)
        with ExitStack() as a:
            kx = sb("kx", [P, XH, NM], F32, a)
            vx = sb("vx", [P, 2, XH * XD], F32, a)
            s_x = sb("s_x", [P, 4, NM], F32, a)
            pt_x = sb("pt_x", [P, 2, S], F32, a)
        with ExitStack() as a:
            gt = sb("gt", [P, S], F32, a)
            sg = sb("sg", [P, S], F32, a)

        va_t = tuple(s_a[:, 2 * n:2 * n + 2, :].rearrange("p a b -> p (a b)") for n in range(2))
        gate_b, gate_a = (scaled, vt), (ra, rb)
        sq_half = scaled

        acc = [ctx.enter_context(nc.psum_tensor(f"acc{n}", [P, S], F32)) for n in range(2)]
        ps = [ctx.enter_context(nc.psum_tensor(f"ps{n}", [P, 3 * S], F32)) for n in range(2)]

        raw_in = [sem(f"raw_in{n}") for n in range(RING)]
        hi_done, lo_done = sem("hi_done"), sem("lo_done")
        unit_done = sem("unit_done")
        half_done = sem("half_done")
        acc_free = sem("acc_free")
        par_in, pos_in, mem_in = sem("par_in"), sem("pos_in"), sem("mem_in")
        x_in = [sem(f"x_in{n}") for n in range(4)]
        const_ready, const_r_ready = sem("const_ready"), sem("const_r_ready")
        half_squared, half_summed = sem("half_squared"), sem("half_summed")
        h_hi, h_lo = sem("h_hi"), sem("h_lo")
        mg_hi, mg_lo = sem("mg_hi"), sem("mg_lo")
        mem_hi, mem_lo = sem("mem_hi"), sem("mem_lo")
        sq_ready, sq_done = sem("sq_ready"), sem("sq_done")
        stat_done, std_ready, rstd_ready = sem("stat_done"), sem("std_ready"), sem("rstd_ready")
        z_done, t_done, pv_done = sem("z_done"), sem("t_done"), sem("pv_done")
        zb_ready, lb_ready, p_ready = sem("zb_ready"), sem("lb_ready"), sem("p_ready")
        soft_ready = sem("soft_ready")
        p_hi_done, p_lo_done = sem("p_hi_done"), sem("p_lo_done")
        u_ready, a_ready, a_hi_done, a_lo_done = (sem(n) for n in ("u_ready", "a_ready", "a_hi_done", "a_lo_done"))
        o_hi_done = sem("o_hi_done")
        ps_free = sem("ps_free")
        qk_hi_done, qk_lo_done = sem("qk_hi_done"), sem("qk_lo_done")
        vt_ready, tr_done, v_hi_done, v_lo_done = (sem(n) for n in ("vt_ready", "tr_done", "v_hi_done", "v_lo_done"))
        sig_ready, mix_ready = sem("sig_ready"), sem("mix_ready")
        ang_ready, trig_ready = sem("ang_ready"), sem("trig_ready")
        rot_ready, qa_ready = sem("rot_ready"), sem("qa_ready")
        s_done, max_ready, exp_ready, prob_ready = (sem(n) for n in ("s_done", "max_ready", "exp_ready", "prob_ready"))
        ptr_done, pt_ready = sem("ptr_done"), sem("pt_ready")
        hid_hi = sem("hid_hi")
        hid_lo = sem("hid_lo")
        gain_ready, out_ready, stored = sem("gain_ready"), sem("out_ready"), sem("stored")
        act_step, dve_step = sem("act_step"), sem("dve_step")

        def act_tile(k):
            return act_hi[:, k, :], act_lo[:, k, :]

        def hc_tile(k):
            return act_tile(k) if k < UK else (act2_hi[:, k - UK, :], act2_lo[:, k - UK, :])

        def o_tile(k):
            return o_hi[:, k, :], o_lo[:, k, :]

        def act2_tile(k):
            return act2_hi[:, k, :], act2_lo[:, k, :]

        mem_hi_v = act_hi[:, UK:KT, :].rearrange("p a (b n) -> p (a b) n", n=NM)
        mem_lo_v = act_lo[:, UK:KT, :].rearrange("p a (b n) -> p (a b) n", n=NM)

        def mem_tile(k):
            return mem_hi_v[:, k, :], mem_lo_v[:, k, :]

        def f(ap):
            return ap.bitcast(F32)

        block = ctx.enter_context(nc.Block())

        @block.sync
        def _(sp):
            for s in range(RING):
                sp.dma_start(raw[:, s, :], w[s, :, :]).then_inc(raw_in[s], 16)
            with sp.Fori(1, UNITS // RING) as i:
                for s in range(RING):
                    sp.wait_ge(lo_done, i * RING + (s - RING + 1))
                    sp.dma_start(raw[:, s, :], w[i * RING + s, :, :]).then_inc(raw_in[s], 16)
            with sp.Fori(0, KT) as m:
                sp.wait_ge(out_ready, m + 1)
                sp.dma_start(out[m, :, :], x[:, m, :]).then_inc(stored, 16)
            sp.wait_ge(stored, 16 * KT)

        @block.gpsimd
        def _(pool):
            step = Tally()

            def link(ins):
                ins.then_inc(sq_ready, 1)
                step.add()
                pool.wait_ge(sq_ready, step.at())

            link(nc.gpsimd.memset(ident[:], 0.0))
            link(nc.gpsimd.affine_select(out=ident[:], in_=ident[:], compare_op=ALU.not_equal, fill=1.0,
                                         base=0, pattern=[[-1, P]], channel_multiplier=1))
            nc.gpsimd.memset(ones[:], 1.0).then_inc(const_ready, 1)
            nc.gpsimd.memset(eps_t[:], EPS).then_inc(const_ready, 1)
            link(nc.gpsimd.memset(zb[0][:, 0:P], 1.0))
            nc.gpsimd.affine_select(out=zb[0][:, 0:P], in_=zb[0][:, 0:P], compare_op=ALU.is_gt, fill=0.0,
                                    base=0, pattern=[[-1, P]], channel_multiplier=1).then_inc(const_ready, 1)
            link(nc.gpsimd.memset(sb_mask[:], 0.0))
            for j in range(QT):
                d = sb_mask[:, SB_OFF[j]:SB_OFF[j] + P]
                last = nc.gpsimd.affine_select(out=d, in_=d, compare_op=ALU.is_gt, fill=NEG, base=0,
                                               pattern=[[1, P]], channel_multiplier=-1)
            last.then_inc(const_ready, 1)

            def squares(tile, tmp, total):
                link(nc.gpsimd.tensor_tensor(tmp, tile, tile, ALU.mult))
                link(nc.gpsimd.tensor_tensor(total, total, tmp, ALU.add))

            link(nc.gpsimd.memset(sq_sum[:], 0.0))
            for m in POOL_TILES:
                pool.wait_ge(x_in[m // 4], 16)
                squares(x[:, m, :], rstd[:], sq_sum[:])
            nc.gpsimd.tensor_copy(sq_sum[:, 0:1], sq_sum[:, 0:1]).then_inc(sq_done, 1)

            pool.wait_ge(acc_free, A_SWA)
            link(nc.gpsimd.memset(band[:], 0.0))
            link(nc.gpsimd.memset(band[:, :, 0:CHUNK], NEG))
            link(nc.gpsimd.memset(band[CHUNK:P, :, CHUNK:P], NEG))
            link(nc.gpsimd.memset(band[0:CHUNK, :, P + CHUNK:2 * P], NEG))
            nc.gpsimd.memset(band[:, 0, 0:P], NEG).then_inc(const_ready, 1)

            pool.wait_ge(mem_in, 16)
            link(nc.gpsimd.memset(mem_stat[:], 0.0))
            with repeat(pool, KT, [(step, 2)]) as m:
                squares(mem[:, m, :], rstd[:, 0:NM], mem_stat[:])
            nc.gpsimd.tensor_copy(mem_stat[:, 0:1], mem_stat[:, 0:1]).then_inc(sq_done, 1)

            def x_squares(first_out):
                pool.wait_ge(acc_free, first_out + 1)
                link(nc.gpsimd.memset(sq_sum[:], 0.0))
                with repeat(pool, KT, [(step, 2)]) as m:
                    pool.wait_ge(acc_free, m + (first_out + 1))
                    squares(x[:, m, :], rstd[:], sq_sum[:])
                nc.gpsimd.tensor_copy(sq_sum[:, 0:1], sq_sum[:, 0:1]).then_inc(sq_done, 1)

            x_squares(A_OUT + KT)
            x_squares(A_XO)
            x_squares(A_END - KT)

        @block.scalar
        def _(act):
            act.dma_start(par[:], params).then_inc(par_in, 16)
            for c in range(4):
                act.dma_start(x[:, 4 * c:4 * c + 4, :], xT[:, 4 * c:4 * c + 4, :]).then_inc(x_in[c], 16)
            hd, step, pair, out_no, tr = Tally(), Tally(), Tally(), Tally(), Tally()

            def link(ins):
                ins.then_inc(act_step, 1)
                step.add()
                act.wait_ge(act_step, step.at())

            converted = Tally()

            def convert():
                s = converted.n % RING
                loop = [(i, st // RING) for i, st in converted.loops]
                turn = converted.n // RING + 1
                for i, st in loop:
                    turn = i * st + turn
                act.wait_ge(raw_in[s], turn * 16)
                if converted.loops or converted.n >= RING:
                    act.wait_ge(unit_done, converted.at(1 - RING))
                nc.scalar.activation(w_hi[:, s, :], raw[:, s, :], ACT.Copy).then_inc(hi_done, 1)
                converted.add()

            def units(n=1):
                for _ in range(n):
                    convert()

            def x_square(m):
                if m in OTHER_TILES:
                    n = OTHER_TILES.index(m)
                    if n >= 2:
                        act.wait_ge(half_summed, n)
                    nc.scalar.activation(pf[n % 2][:, 0:S], x[:, m, :], ACT.Square).then_inc(half_squared, 1)

            convert()
            act.wait_ge(par_in, 16)
            for c in range(4):
                act.wait_ge(x_in[c], 16)
                for m in range(4 * c, 4 * c + 4):
                    nc.scalar.activation(act_hi[:, m, :], x[:, m, :], ACT.Copy,
                                         scale=par[:, G_MIX + m:G_MIX + m + 1]).then_inc(h_hi, 1)
                    if c < 3:
                        x_square(m)
                if c < 2:
                    convert()
            for m in range(12, KT):
                x_square(m)
            assert converted.n == AHEAD

            def std(n, bank, dst, width):
                act.wait_ge(stat_done, n)
                if n == 1:
                    act.wait_ge(const_ready, 4)
                nc.scalar.activation(dst[:, 0:width], bank[:, 0:width], ACT.Sqrt, bias=eps_t[:, 0:1],
                                     scale=1.0 / D).then_inc(std_ready, 1)

            def soft(par_):
                act.wait_ge(zb_ready, hd.at(1 + par_))
                link(nc.scalar.activation(pf[par_][:], zb[par_][:], ACT.Abs))
                link(nc.scalar.activation(pf[par_][:], pf[par_][:], ACT.Exp, scale=-1.0))
                nc.scalar.activation(pf[par_][:], pf[par_][:], ACT.Ln, bias=1.0).then_inc(soft_ready, 1)

            def p_high(par_):
                act.wait_ge(p_ready, hd.at(1 + par_))
                nc.scalar.activation(pa_hi[par_][:], pf[par_][:], ACT.Copy).then_inc(p_hi_done, 1)

            def a_high(par_):
                act.wait_ge(u_ready, hd.at(1 + par_))
                nc.scalar.activation(pf[par_][:], zb[par_][:], ACT.Exp).then_inc(a_ready, 1)
                act.wait_ge(a_ready, hd.at(1 + par_))
                nc.scalar.activation(pa_hi[par_][:], pf[par_][:], ACT.Copy).then_inc(a_hi_done, 1)

            def o_high(par_):
                act.wait_ge(pv_done, hd.at(1 + par_))
                rows = slice(HD * par_, HD * par_ + HD)
                nc.scalar.activation(o_hi[rows, pair.at(), :], ps[par_][rows, 0:S], ACT.Copy)\
                    .then_inc(o_hi_done, 1)

            def read_out():
                act.wait_ge(acc_free, out_no.at(1))
                out_no.add()

            def qk_high(dst):
                read_out()
                nc.scalar.activation(dst[:], scaled[:], ACT.Copy).then_inc(qk_hi_done, 1)

            def v_high():
                act.wait_ge(tr_done, tr.at(1))
                nc.scalar.activation(v_hi[:], acc[1][:], ACT.Copy).then_inc(v_hi_done, 1)
                tr.add()
                out_no.add()

            def sb_body():
                soft(0)
                soft(1)
                p_high(0)
                v_high()
                p_high(1)
                units(3)
                a_high(0)
                qk_high(q_hi)
                units()
                a_high(1)
                qk_high(k_hi)
                units()
                o_high(0)
                units()
                out_no.add()
                o_high(1)
                hd.add(2)
                pair.add()

            units(2)
            std(1, ps[0], rstd, S)
            units(1)
            qk_high(q_hi)
            units()
            qk_high(k_hi)
            units(2)
            out_no.add()
            nc.scalar.preload_act_table_set("natural_log_exp_and_others")
            with repeat(act, (PAIRS - 2) // 2, [(converted, 12), (hd, 4), (step, 8), (pair, 2), (out_no, 8), (tr, 2)]):
                sb_body()
                sb_body()
            sb_body()

            def sigmoid(tile, column):
                read_out()
                nc.scalar.activation(tile[:], tile[:], ACT.Sigmoid, bias=par[:, bass.ds(column, 1)])\
                    .then_inc(sig_ready, 1)

            def gates(tiles_, first, before_last=lambda: None):
                def turn(m):
                    units(2)
                    out_no.add(2)
                    for b in range(2):
                        units(2)
                        sigmoid(tiles_[b], m + (b + 2 + first))

                nc.scalar.preload_act_table_set("sigmoid_and_others")
                with repeat(act, (KT // 2 - 1) // 2, [(converted, 12), (out_no, 8)]) as i:
                    turn(i * 4)
                    turn(i * 4 + 2)
                turn(KT - 4)
                before_last()
                units(2)
                out_no.add(2)

            def sb_last():
                soft(0)
                soft(1)
                p_high(0)
                v_high()
                p_high(1)
                units(3)
                a_high(0)
                units()
                a_high(1)
                o_high(0)
                o_high(1)
                for b in range(2):
                    sigmoid(gate_b[b], B_GATE + KT + b)
                hd.add(2)
                pair.add()

            sb_last()
            act.dma_start(rc[:], rope_const).then_inc(pos_in, 16)
            act.wait_ge(ps_free, 2 + 2 * PAIRS)
            act.dma_start(ra[:].bitcast(I32), pos).then_inc(pos_in, 16)
            gates(gate_b, B_GATE + KT)

            act.wait_ge(ang_ready, 1)
            nc.scalar.activation(sin_t[:], sin_t[:], ACT.Sin)
            nc.scalar.activation(cos_t[:], cos_t[:], ACT.Sin).then_inc(trig_ready, 1)
            swa = Tally()

            def rotate(n, units_used, a):
                act.wait_ge(unit_done, units_used)
                if n:
                    act.wait_ge(qa_ready, n)
                for h in range(2):
                    for to, src in ((0, HALF), (HALF, 0)):
                        last = nc.scalar.activation(rb[HD * h + to:HD * h + to + HALF, :],
                                                    acc[a][HD * h + src:HD * h + src + HALF, :], ACT.Copy)
                last.then_inc(rot_ready, 1)

            def rotate_q(t):
                rotate(t + 2, U_SWA + 8 + 2 * (t + 1), (A_SWA + 6 + t) % 2)

            def swa_exp(t, hf):
                act.wait_ge(max_ready, 2 * t + hf + 1)
                st = stat_a[:, hf]
                for n in range(4):
                    rows = ps[hf][:, 2 * P * n:2 * P * (n + 1)]
                    nc.scalar.activation(rows, rows, ACT.Exp, bias=st[:, 1, n:n + 1], accum_out=st[:, 3, n:n + 1])
                nc.scalar.activation(st[:, 4, :], st[:, 2, :], ACT.Exp).then_inc(exp_ready, 1)

            def swa_pt(t, hf):
                act.wait_ge(ptr_done, 2 * t + hf + 1)
                nc.scalar.activation(pt_a[:], ps[hf][:, 0:2 * S], ACT.Copy).then_inc(pt_ready, 1)

            def swa_o(t, hf):
                act.wait_ge(pv_done, 2 * PAIRS + 2 * t + hf + 1)
                for h in range(2):
                    rows = slice(HD * h, HD * h + HD)
                    last = nc.scalar.activation(o_hi[rows, t, 2 * P * hf:2 * P * (hf + 1)],
                                                ps[hf][rows, 2 * S + 2 * P * h:2 * S + 2 * P * (h + 1)], ACT.Copy)
                last.then_inc(o_hi_done, 1)

            units(6)
            rotate(0, U_SWA + 6, A_SWA % 2)
            units(2)
            rotate(1, U_SWA + 8, (A_SWA + 5) % 2)
            units(2)
            rotate_q(0)
            units(1)
            for t in range(PAIRS):
                swa_exp(t, 0)
                if t:
                    swa_o(t - 1, 1)
                units()
                swa_exp(t, 1)
                if t < PAIRS - 1:
                    rotate_q(t + 1)
                swa_pt(t, 0)
                units()
                swa_o(t, 0)
                swa_pt(t, 1)
            units()
            swa_o(PAIRS - 1, 1)
            out_no.n = A_DA
            for b in range(2):
                sigmoid(gate_a[b], B_GATE + b)
            swa.n, hd.n = 2 * PAIRS, 4 * PAIRS

            def merged_high(first, n):
                with act.Fori(first, first + n) as m:
                    act.wait_ge(mix_ready, m + 1)
                    nc.scalar.activation(act_hi[:, m, :], merged[:, m, :], ACT.Copy).then_inc(mg_hi, 1)

            def merged_begun():
                act.wait_ge(unit_done, U_OUT - 2)
                merged_high(0, KT - 2)

            gates(gate_a, B_GATE, merged_begun)
            merged_high(KT - 2, 2)

            act.wait_ge(unit_done, U_OUT)
            for c in range(4):
                act.dma_start(x[:, 4 * c:4 * c + 4, :], xT[:, 4 * c:4 * c + 4, :]).then_inc(x_in[c], 16)
            act.dma_start(mem[:], memT).then_inc(mem_in, 16)
            with repeat(act, KT // 4, [(converted, 4)]):
                units(4)
            out_no.add(KT)

            def x_high(dst, m, gain):
                read_out()
                nc.scalar.activation(dst, x[:, m, :], ACT.Copy, scale=par[:, bass.ds(m + gain, 1)])\
                    .then_inc(h_hi, 1)

            for half, dst in ((0, act_hi), (1, act2_hi)):
                with repeat(act, 2, [(converted, 4), (out_no, 4)]) as i:
                    for b in range(4):
                        units()
                        x_high(dst[:, i * 4 + b, :], i * 4 + (b + UK * half), G_CROSS)

            act.wait_ge(unit_done, U_XQ)
            act.wait_ge(mem_in, 16)
            for p in range(XH):
                units(2)
                with act.Fori(4 * p, 4 * p + 4) as m:
                    nc.scalar.activation(mem_hi_v[:, m, :], mem[:, m, :], ACT.Copy,
                                         scale=par[:, bass.ds(m + G_MEM, 1)]).then_inc(mem_hi, 1)
                if p == 0:
                    std(2, ps[0], rstd, S)
            units(3)
            std(3, ps[1], mem_stat, NM)
            units(5)
            def x_exp(h):
                act.wait_ge(max_ready, swa.at(1 + h))
                for n in range(4):
                    last = nc.scalar.activation(s_x[:, n, :], ps[h % 2][:, n * NM:(n + 1) * NM], ACT.Exp,
                                                bias=stat_x[:, 1, n:n + 1], scale=XD ** -0.5,
                                                accum_out=stat_x[:, 2, n:n + 1])
                last.then_inc(exp_ready, 1)

            def x_pt(h):
                act.wait_ge(ptr_done, swa.at(1 + h))
                nc.scalar.activation(pt_x[:], ps[h % 2][:, 0:2 * S].rearrange("p (a b) -> p a b", a=2), ACT.Copy)\
                    .then_inc(pt_ready, 1)

            def x_o(h):
                act.wait_ge(pv_done, hd.at(1))
                nc.scalar.activation(act2_hi[:, h, :], ps[h % 2][:, 2 * S:3 * S], ACT.Copy).then_inc(o_hi_done, 1)
                hd.add()

            x_exp(0)
            units(8)
            out_no.add(2 * XH + 2)
            for h in range(XH):
                x_pt(h)
                if h + 1 < XH:
                    x_exp(h + 1)
                x_o(h)
            out_no.add(XH)

            with repeat(act, KT // 8, [(converted, 4), (out_no, 8)]) as i:
                for b in range(4):
                    units()
                    for n in range(2):
                        x_high(act_hi[:, i * 8 + (2 * b + n), :], i * 8 + (2 * b + n), G_FFN)

            std(4, ps[0], rstd, S)

            def ffn(last):
                with repeat(act, GROUP, [(converted, 4), (out_no, 2)]) as t:
                    units(2)
                    read_out()
                    nc.scalar.activation(sg[:], gt[:], ACT.Sigmoid).then_inc(sig_ready, 1)
                    units(2)
                    read_out()
                    nc.scalar.activation(act2_hi[:, t, :], gt[:], ACT.Copy).then_inc(hid_hi, 1)
                if last:
                    units(KT // 2 - AHEAD)
                else:
                    with repeat(act, 2, [(converted, 4)]):
                        units(4)
                    out_no.add(KT)

            with repeat(act, GROUPS - 1, [(converted, FFN_UNITS), (out_no, GROUP * 2 + KT)]):
                ffn(False)
            ffn(True)
            assert converted.n == UNITS
            std(5, ps[1], rstd, S)

        @block.vector
        def _(dve):
            hd, step, pair, out_no, tr, sig = Tally(), Tally(), Tally(), Tally(), Tally(), Tally()
            converted, swa, hid = Tally(), Tally(), Tally()

            def link(ins):
                ins.then_inc(dve_step, 1)
                step.add()
                dve.wait_ge(dve_step, step.at())

            def units(n=1):
                for _ in range(n):
                    s = converted.n % RING
                    dve.wait_ge(hi_done, converted.at(1))
                    nc.vector.tensor_tensor(w_lo[:, s, :], raw[:, s, :], f(w_hi[:, s, :]), ALU.subtract)\
                        .then_inc(lo_done, 1)
                    converted.add()

            def output():
                a = acc[out_no.n % 2]
                out_no.add()
                return a

            unit = Tally()

            def rstd_of(n, dst, width):
                dve.wait_ge(std_ready, n)
                nc.vector.reciprocal(dst[:, 0:width], dst[:, 0:width]).then_inc(rstd_ready, 1)
                dve.wait_ge(rstd_ready, n)

            def scale_out(dst, k=2):
                unit.add(k)
                dve.wait_ge(unit_done, unit.at())
                nc.vector.tensor_tensor(dst, output()[:], rstd[:], ALU.mult).then_inc(acc_free, 1)

            nc.vector.memset(stat_x[:, 2, :], 0.0).then_inc(hid_lo, 1)
            for n in range(2):
                nc.vector.memset(stat_x[:, n, :], 0.0).then_inc(ps_free, 1)
            dve.wait_ge(const_ready, 4)
            nc.vector.tensor_copy(ones_r[:], ones[:]).then_inc(const_r_ready, 1)
            nc.vector.tensor_copy(tri_r[:], zb[0][:, 0:P]).then_inc(const_r_ready, 1)
            units(1)
            h = Tally()

            def x_low(dst, hi, m, gain):
                dve.wait_ge(h_hi, h.at(1))
                nc.vector.scalar_tensor_tensor(dst, x[:, m, :], par[:, bass.ds(m + gain, 1)], f(hi),
                                               ALU.mult, ALU.subtract).then_inc(h_lo, 1)
                h.add()

            nc.vector.memset(sq_half[:], 0.0).then_inc(half_summed, 1)

            def add_square(m):
                if m in OTHER_TILES:
                    n = OTHER_TILES.index(m)
                    dve.wait_ge(half_squared, n + 1)
                    dve.wait_ge(half_summed, n + 1)
                    nc.vector.tensor_tensor(sq_half[:], sq_half[:], pf[n % 2][:, 0:S], ALU.add)\
                        .then_inc(half_summed, 1)

            for m in range(KT):
                x_low(act_lo[:, m, :], act_hi[:, m, :], m, G_MIX)
                if m < 12:
                    add_square(m)
                if m in (3, 7):
                    units()
            for m in range(12, KT):
                add_square(m)

            def z_out(n):
                dve.wait_ge(z_done, hd.at(1 + n))
                nc.vector.scalar_tensor_tensor(zb[n][:], ps[n][:, 0:SB_COLS], HD ** -0.5, sb_mask[:],
                                               ALU.mult, ALU.add).then_inc(zb_ready, 1)

            def softplus(n):
                dve.wait_ge(soft_ready, hd.at(1 + n))
                nc.vector.scalar_tensor_tensor(pf[n][:], zb[n][:], 0.0, pf[n][:], ALU.max, ALU.add)\
                    .then_inc(p_ready, 1)

            def log_beta(n):
                dve.wait_ge(p_ready, hd.at(1 + n))
                nc.vector.tensor_tensor(zb[n][:], zb[n][:], pf[n][:], ALU.subtract).then_inc(lb_ready, 1)

            def p_low(n):
                dve.wait_ge(p_hi_done, hd.at(1 + n))
                nc.vector.tensor_tensor(pa_lo[n][:], pf[n][:], f(pa_hi[n][:]), ALU.subtract)\
                    .then_inc(p_lo_done, 1)

            def tail(n):
                dve.wait_ge(t_done, hd.at(1 + n))
                nc.vector.tensor_tensor(zb[n][:], zb[n][:], ps[n][:, 0:SB_COLS], ALU.subtract)\
                    .then_inc(u_ready, 1)

            def a_low(n):
                dve.wait_ge(a_hi_done, hd.at(1 + n))
                nc.vector.tensor_tensor(pa_lo[n][:], pf[n][:], f(pa_hi[n][:]), ALU.subtract)\
                    .then_inc(a_lo_done, 1)

            def o_low(n):
                dve.wait_ge(o_hi_done, hd.at(1 + n))
                rows = slice(HD * n, HD * n + HD)
                nc.vector.tensor_tensor(o_lo[rows, pair.at(), :], ps[n][rows, 0:S], f(o_hi[rows, pair.at(), :]),
                                        ALU.subtract).then_inc(ps_free, 1)

            qk = Tally()

            def qk_scale():
                if qk.loops or qk.n:
                    dve.wait_ge(qk_lo_done, qk.at())
                scale_out(scaled[:])

            def qk_low(hi, lo):
                dve.wait_ge(qk_hi_done, qk.at(1))
                nc.vector.tensor_tensor(lo[:], scaled[:], f(hi[:]), ALU.subtract).then_inc(qk_lo_done, 1)
                qk.add()

            def qk_out(hi, lo):
                qk_scale()
                qk_low(hi, lo)

            def until_split():
                z_out(0)
                z_out(1)
                softplus(0)
                log_beta(0)
                softplus(1)
                p_low(0)
                log_beta(1)
                dve.wait_ge(v_hi_done, tr.at(1))
                nc.vector.tensor_tensor(v_lo[:], output()[:], f(v_hi[:]), ALU.subtract).then_inc(acc_free, 1)
                tr.add()
                p_low(1)
                units(3)

            def sb_body():
                until_split()
                qk_scale()
                tail(0)
                a_low(0)
                qk_low(q_hi, q_lo)
                units()
                tail(1)
                a_low(1)
                qk_out(k_hi, k_lo)
                units()
                o_low(0)
                units()
                o_low(1)
                scale_out(vt[:])
                hd.add(2)
                pair.add()

            def sb_last():
                until_split()
                dve.wait_ge(qk_lo_done, qk.at())
                scale_out(gate_b[0][:])
                tail(0)
                a_low(0)
                units()
                tail(1)
                a_low(1)
                scale_out(gate_b[1][:])
                o_low(0)
                o_low(1)
                hd.add(2)
                pair.add()

            units(2)
            rstd_of(1, rstd, S)
            units(1)
            qk_out(q_hi, q_lo)
            units()
            qk_out(k_hi, k_lo)
            units(2)
            scale_out(vt[:])
            with repeat(dve, (PAIRS - 2) // 2, [(converted, 12), (unit, 12), (hd, 4), (pair, 2), (out_no, 8),
                                                (tr, 2), (qk, 4)]):
                sb_body()
                sb_body()
            sb_body()
            sb_last()

            mixed = Tally()

            def gates(tiles_, first_pass):
                def branches(m):
                    for b in range(2):
                        g = tiles_[b][:]
                        units()
                        unit.add()
                        dve.wait_ge(unit_done, unit.at())
                        dve.wait_ge(sig_ready, sig.at(1))
                        sig.add()
                        dst = merged[:, m + b, :]
                        nc.vector.tensor_tensor(dst if first_pass else g, output()[:], g, ALU.mult)\
                            .then_inc(acc_free, 1)
                        if not first_pass:
                            dve.wait_ge(acc_free, out_no.at())
                            nc.vector.tensor_tensor(dst, dst, g, ALU.add).then_inc(mix_ready, 1)
                            mixed.add()

                def next_gates():
                    for b in range(2):
                        units(2)
                        if not first_pass and b == 0:
                            dve.wait_ge(mix_ready, mixed.at())
                        scale_out(tiles_[b][:])

                moves = [(converted, 12), (unit, 12), (out_no, 8), (sig, 4)]
                with repeat(dve, (KT // 2 - 1) // 2, moves + ([] if first_pass else [(mixed, 4)])) as i:
                    for n in range(2):
                        branches(i * 4 + 2 * n)
                        next_gates()
                branches(KT - 4)
                next_gates()
                if not first_pass:
                    merged_low(0, KT - 2)
                branches(KT - 2)

            def merged_low(first, n):
                with dve.Fori(first, first + n) as m:
                    dve.wait_ge(mg_hi, m + 1)
                    nc.vector.tensor_tensor(act_lo[:, m, :], merged[:, m, :], f(act_hi[:, m, :]), ALU.subtract)\
                        .then_inc(mg_lo, 1)

            gates(gate_b, True)

            dve.wait_ge(pos_in, 32)
            link(nc.vector.tensor_copy(sin_t[:], ra[:].bitcast(I32)))
            link(nc.vector.tensor_scalar(sin_t[:], sin_t[:], rc[:, 0:1], None, ALU.mult))
            link(nc.vector.tensor_scalar(ra[:], sin_t[:], 1 / (2 * np.pi), None, ALU.mult))
            link(nc.vector.tensor_scalar(ra[:], ra[:], ROUND, None, ALU.add))
            link(nc.vector.tensor_scalar(ra[:], ra[:], -ROUND, None, ALU.add))
            for c in TWO_PI:
                link(nc.vector.scalar_tensor_tensor(sin_t[:], ra[:], -c, sin_t[:], ALU.mult, ALU.add))
            link(nc.vector.tensor_scalar(cos_t[:], sin_t[:], np.pi / 2, None, ALU.add))
            link(nc.vector.tensor_scalar(ra[:], cos_t[:], np.pi, -2 * np.pi, ALU.is_gt, ALU.mult))
            link(nc.vector.tensor_tensor(cos_t[:], cos_t[:], ra[:], ALU.add))
            link(nc.vector.tensor_scalar(cos_t[:], cos_t[:], PI_DOWN, -PI_DOWN, ALU.min, ALU.max))
            nc.vector.tensor_scalar(sin_t[:], sin_t[:], PI_DOWN, -PI_DOWN, ALU.min, ALU.max).then_inc(ang_ready, 1)

            def rope(dst, n):
                unit.add(2)
                dve.wait_ge(unit_done, unit.at())
                if n:
                    dve.wait_ge(qa_ready, n)
                dve.wait_ge(rot_ready, n + 1)
                link(nc.vector.tensor_tensor(ra[:], output()[:], cos_t[:], ALU.mult))
                nc.vector.tensor_tensor(rb[:], rb[:], sin_t[:], ALU.mult).then_inc(acc_free, 1)
                dve.wait_ge(acc_free, out_no.at())
                nc.vector.tensor_tensor(dst, ra[:], rb[:], ALU.add).then_inc(qa_ready, 1)

            def v_out(n, width, dst):
                dve.wait_ge(tr_done, tr.at(1))
                nc.vector.tensor_copy(dst, output()[:].rearrange("p (a b) -> p a b", b=width)).then_inc(acc_free, 1)
                tr.add()

            def swa_max(t, hf):
                dve.wait_ge(s_done, 2 * t + hf + 1)
                st = stat_a[:, hf]
                mask = band[:] if hf == 0 else band[:, 1:2, :].broadcast_to([P, 2, 2 * P])
                for n in range(2):
                    z = ps[hf][:, S * n:S * (n + 1)].rearrange("p (a b) -> p a b", a=2)
                    last = nc.vector.scalar_tensor_tensor(z, z, HD ** -0.5, mask, ALU.mult, ALU.add)
                link(last)
                link(nc.vector.reduce_max(st[:, 0, :], ps[hf][:, 0:2 * S].rearrange("p (a b) -> p a b", a=4), AX.X))
                for n in range(2):
                    sink = SINK + 2 * t + n
                    last = nc.vector.tensor_scalar(st[:, 0, 2 * n:2 * n + 2], st[:, 0, 2 * n:2 * n + 2],
                                                   par[:, sink:sink + 1], None, ALU.max)
                link(last)
                link(nc.vector.tensor_scalar(st[:, 1, :], st[:, 0, :], -1.0, None, ALU.mult))
                for n in range(2):
                    sink = SINK + 2 * t + n
                    last = nc.vector.tensor_scalar(st[:, 2, 2 * n:2 * n + 2], st[:, 1, 2 * n:2 * n + 2],
                                                   par[:, sink:sink + 1], None, ALU.add)
                last.then_inc(max_ready, 1)

            def swa_prob(t, hf):
                dve.wait_ge(exp_ready, 2 * t + hf + 1)
                st = stat_a[:, hf]
                link(nc.vector.tensor_tensor(st[:, 5, :], st[:, 3, :], st[:, 4, :], ALU.add))
                link(nc.vector.reciprocal(st[:, 5, :], st[:, 5, :]))
                if t or hf:
                    dve.wait_ge(ptr_done, 2 * t + hf)
                nc.vector.tensor_tensor(s_a[:], ps[hf][:, 0:2 * S].rearrange("p (a b) -> p a b", a=4),
                                        st[:, 5, :].unsqueeze(2).broadcast_to([P, 4, 2 * P]), ALU.mult)\
                    .then_inc(prob_ready, 1)

            def swa_o(t, hf):
                dve.wait_ge(o_hi_done, 2 * PAIRS + 2 * t + hf + 1)
                for n in range(2):
                    rows = slice(HD * n, HD * n + HD)
                    cols = slice(2 * P * hf, 2 * P * (hf + 1))
                    last = nc.vector.tensor_tensor(o_lo[rows, t, cols],
                                                   ps[hf][rows, 2 * S + 2 * P * n:2 * S + 2 * P * (n + 1)],
                                                   f(o_hi[rows, t, cols]), ALU.subtract)
                last.then_inc(ps_free, 1)

            units(4)
            for n in range(2):
                scale_out(va_t[n])
            dve.wait_ge(trig_ready, 1)
            link(nc.vector.scalar_tensor_tensor(sin_t[:], sin_t[:], rc[:, 1:2], rstd[:], ALU.mult, ALU.mult))
            link(nc.vector.tensor_tensor(cos_t[:], cos_t[:], rstd[:], ALU.mult))
            units(2)
            rope(ka[:, 0, :], 0)
            v_out(0, P, va[:, :, 0:P])
            v_out(1, P, va[:, :, P:2 * P])
            units(2)
            rope(ka[:, 1, :], 1)
            units(2)
            rope(qa[:], 2)
            units(1)
            dve.wait_ge(const_ready, 5)
            for t in range(PAIRS):
                swa_max(t, 0)
                swa_max(t, 1)
                swa_prob(t, 0)
                if t:
                    swa_o(t - 1, 1)
                units()
                if t < PAIRS - 1:
                    rope(qa[:], t + 3)
                else:
                    dve.wait_ge(qa_ready, PAIRS + 2)
                    scale_out(gate_a[0][:])
                units()
                swa_prob(t, 1)
                swa_o(t, 0)
            units()
            scale_out(gate_a[1][:])
            swa_o(PAIRS - 1, 1)
            swa.n, hd.n = 2 * PAIRS, 4 * PAIRS

            gates(gate_a, False)
            merged_low(KT - 2, 2)

            def add_out(m):
                nc.vector.tensor_tensor(x[:, m, :], x[:, m, :], output()[:], ALU.add).then_inc(acc_free, 1)

            for c in range(4):
                dve.wait_ge(x_in[c], 32)
                for b in range(4):
                    units()
                    unit.add()
                    dve.wait_ge(unit_done, unit.at())
                    add_out(4 * c + b)

            for half, hi, lo in ((0, act_hi, act_lo), (1, act2_hi, act2_lo)):
                with repeat(dve, 2, [(converted, 4), (unit, 4), (out_no, 4), (h, 4)]) as i:
                    for b in range(4):
                        units()
                        unit.add()
                        dve.wait_ge(unit_done, unit.at())
                        add_out(i * 4 + (b + UK * half))
                        x_low(lo[:, i * 4 + b, :], hi[:, i * 4 + b, :], i * 4 + (b + UK * half), G_CROSS)

            mems = Tally()
            for p in range(XH):
                units(2)
                with repeat(dve, 4, [(mems, 1)]) as i:
                    dve.wait_ge(mem_hi, mems.at(1))
                    nc.vector.scalar_tensor_tensor(mem_lo_v[:, i + 4 * p, :], mem[:, i + 4 * p, :],
                                                   par[:, bass.ds(i + (4 * p + G_MEM), 1)],
                                                   f(mem_hi_v[:, i + 4 * p, :]), ALU.mult, ALU.subtract)\
                        .then_inc(mem_lo, 1)
                    mems.add()
                if p == 0:
                    rstd_of(2, rstd, S)
                scale_out(qx[:, p, :])

            def kv_out(dst):
                unit.add(2)
                dve.wait_ge(unit_done, unit.at())
                nc.vector.tensor_tensor(dst, output()[:, 0:NM], mem_stat[:], ALU.mult).then_inc(acc_free, 1)

            units(3)
            rstd_of(3, mem_stat, NM)
            kv_out(kx[:, 0, :])
            units(1)
            kv_out(kx[:, 1, :])
            units(2)
            kv_out(kx[:, 2, :])
            units(2)
            kv_out(kx[:, 3, :])

            def x_max(n):
                dve.wait_ge(s_done, swa.at(1))
                link(nc.vector.reduce_max(stat_x[:, 0, :], ps[n % 2][:, 0:4 * NM].rearrange("p (a b) -> p a b", a=4),
                                          AX.X))
                nc.vector.tensor_scalar(stat_x[:, 1, :], stat_x[:, 0, :], -XD ** -0.5, None, ALU.mult)\
                    .then_inc(max_ready, 1)

            def x_prob(n):
                dve.wait_ge(exp_ready, swa.at(1))
                link(nc.vector.reciprocal(stat_x[:, 0, :], stat_x[:, 2, :]))
                nc.vector.tensor_tensor(s_x[:], s_x[:], stat_x[:, 0, :].unsqueeze(2).broadcast_to([P, 4, NM]),
                                        ALU.mult).then_inc(prob_ready, 1)
                swa.add()

            def x_o(n):
                dve.wait_ge(o_hi_done, hd.at(1))
                nc.vector.tensor_tensor(act2_lo[:, n, :], ps[n % 2][:, 2 * S:3 * S], f(act2_hi[:, n, :]),
                                        ALU.subtract).then_inc(ps_free, 1)
                hd.add()

            x_max(0)
            units(2)
            kv_out(vt[:, 0:NM])
            x_prob(0)
            units(2)
            kv_out(vt[:, NM:2 * NM])
            units(2)
            dve.wait_ge(tr_done, PAIRS + 3)
            kv_out(vt[:, 0:NM])
            v_out(0, XD, vx[:, :, 0:2 * XD].rearrange("p a (h b) -> p h a b", h=2))
            units(2)
            kv_out(vt[:, NM:2 * NM])
            v_out(1, XD, vx[:, :, 2 * XD:4 * XD].rearrange("p a (h b) -> p h a b", h=2))
            for n in range(XH):
                if n + 1 < XH:
                    x_max(n + 1)
                    x_prob(n + 1)
                x_o(n)

            with repeat(dve, KT // 8, [(converted, 4), (unit, 4), (out_no, 8), (h, 8)]) as i:
                for b in range(4):
                    units()
                    for n in range(2):
                        m = i * 8 + (2 * b + n)
                        dve.wait_ge(half_done if n == 0 else unit_done, unit.at(1 - (0 if n else U_XO)))
                        add_out(m)
                        x_low(act_lo[:, m, :], act_hi[:, m, :], m, G_FFN)
                    unit.add()

            rstd_of(4, rstd, S)
            half = Tally(KT // 2)

            def ffn(last):
                with repeat(dve, GROUP, [(converted, 4), (unit, 4), (out_no, 2), (sig, 1), (step, 2), (hid, 1)]) as t:
                    units(2)
                    dve.wait_ge(hid_lo, hid.at(1))
                    scale_out(gt[:])
                    dve.wait_ge(sig_ready, sig.at(1))
                    link(nc.vector.tensor_tensor(gt[:], gt[:], sg[:], ALU.mult))
                    link(nc.vector.tensor_tensor(gt[:], gt[:], rstd[:], ALU.mult))
                    sig.add()
                    units(2)
                    unit.add(2)
                    dve.wait_ge(unit_done, unit.at())
                    nc.vector.tensor_tensor(gt[:], gt[:], output()[:], ALU.mult).then_inc(acc_free, 1)
                    dve.wait_ge(hid_hi, hid.at(1))
                    nc.vector.tensor_tensor(act2_lo[:, t, :], gt[:], f(act2_hi[:, t, :]), ALU.subtract)\
                        .then_inc(hid_lo, 1)
                    hid.add()

                def down(m, split):
                    if split:
                        units()
                    dve.wait_ge(half_done, half.at(1))
                    add_out(m)
                    dve.wait_ge(unit_done, unit.at(1))
                    add_out(m + 1)
                    unit.add()
                    half.add()

                if last:
                    for n in range(KT // 2):
                        down(2 * n, n < KT // 2 - AHEAD)
                else:
                    with repeat(dve, 2, [(converted, 4), (unit, 4), (out_no, 8), (half, 4)]) as i:
                        for b in range(4):
                            down(i * 8 + 2 * b, True)

            with repeat(dve, GROUPS - 1, [(converted, FFN_UNITS), (unit, FFN_UNITS), (out_no, GROUP * 2 + KT),
                                          (sig, GROUP), (step, 2 * GROUP), (hid, GROUP), (half, KT // 2)]):
                ffn(False)
            ffn(True)
            assert out_no.n == A_END and unit.n == UNITS and converted.n == UNITS

            rstd_of(5, rstd, S)
            with dve.Fori(0, KT) as m:
                nc.vector.scalar_tensor_tensor(x[:, m, :], x[:, m, :], par[:, bass.ds(m + G_FINAL, 1)], rstd[:],
                                               ALU.mult, ALU.mult).then_inc(out_ready, 1)

        @block.tensor
        def _(pe):
            u, out_no, hd, tr, swa = Tally(), Tally(), Tally(), Tally(), Tally()
            half, hid = Tally(), Tally()

            def output():
                a = acc[out_no.n % 2]
                if out_no.loops or out_no.n >= 2:
                    pe.wait_ge(acc_free, out_no.at(-1))
                out_no.add()
                return a

            def split_products(dst, pairs):
                for n, (wh, wl, ah, al) in enumerate(pairs):
                    nc.tensor.matmul(dst, wh, ah, start=n == 0, stop=False)
                    nc.tensor.matmul(dst, wh, al, start=False, stop=False)
                    last = nc.tensor.matmul(dst, wl, ah, start=False, stop=n == len(pairs) - 1)
                return last

            def unit(dst, tiles, start, stop, arrive=None):
                s = u.n % RING
                pe.wait_ge(lo_done, u.at(1))
                for k, (ah, al) in enumerate(tiles):
                    if arrive:
                        pe.wait_ge(*arrive(k))
                    wh, wl = (t[:, s, P * k:P * (k + 1)] for t in (w_hi, w_lo))
                    nc.tensor.matmul(dst, wh, ah, start=start and k == 0, stop=False)
                    nc.tensor.matmul(dst, wh, al, start=False, stop=False)
                    last = nc.tensor.matmul(dst, wl, ah, start=False, stop=stop and k == UK - 1)
                last.then_inc(unit_done, 1)
                u.add()

            def two_outputs(hidden=None):
                s = u.n % RING
                pe.wait_ge(lo_done, u.at(1))
                for n in range(2):
                    dst = output()[:]
                    for k in range(GROUP):
                        if hidden is not None and n == 0 and k % (GROUP - 1) == 0:
                            pe.wait_ge(hid_lo, hidden + (1 if k else 0))
                        ah, al = act2_tile(k)
                        wh, wl = (t[:, s, P * (GROUP * n + k):P * (GROUP * n + k + 1)] for t in (w_hi, w_lo))
                        nc.tensor.matmul(dst, wh, ah, start=k == 0, stop=False)
                        nc.tensor.matmul(dst, wh, al, start=False, stop=False)
                        last = nc.tensor.matmul(dst, wl, ah, start=False, stop=k == GROUP - 1)
                    last.then_inc(unit_done if n else half_done, 1)
                u.add()

            def panel(tile, width=S, arrive=None):
                dst = output()[:, 0:width]
                for n in range(2):
                    unit(dst, [tile(UK * n + k) for k in range(UK)], n == 0, n == 1,
                         arrive and (lambda k, n=n: arrive(UK * n + k)))

            def stat(n, squares, bank, src, width):
                pe.wait_ge(sq_done, squares)
                nc.tensor.matmul(bank[:, 0:width], ones[:], src[:, 0:width], start=True, stop=True)\
                    .then_inc(stat_done, 1)

            def scores(n):
                if n == 0:
                    pe.wait_ge(qk_lo_done, hd.at(2))
                pe.wait_ge(ps_free, hd.at(n + 1))
                rows = slice(HD * n, HD * n + HD)
                for j in range(QT):
                    keys, cols = slice(P * j, P * (j + 1)), slice(P * j, S)
                    last = split_products(ps[n][:, SB_OFF[j]:SB_OFF[j] + SB_LEN[j]],
                                          [(k_hi[rows, keys], k_lo[rows, keys], q_hi[rows, cols], q_lo[rows, cols])])
                last.then_inc(z_done, 1)

            def tails(n):
                pe.wait_ge(p_lo_done, hd.at(1 + n))
                for j in range(QT):
                    terms = [(tri_r, j)] + [(ones_r, i) for i in range(j + 1, QT)]
                    for m, (mat, i) in enumerate(terms):
                        dst = ps[n][:, SB_OFF[j] + P * (i - j):SB_OFF[j] + SB_LEN[j]]
                        cols = slice(SB_OFF[i], SB_OFF[i] + SB_LEN[i])
                        nc.tensor.matmul(dst, mat[:], pa_hi[n][:, cols], start=m == 0, stop=False)
                        last = nc.tensor.matmul(dst, mat[:], pa_lo[n][:, cols], start=False, stop=m == len(terms) - 1)
                last.then_inc(t_done, 1)

            def values(n):
                if n == 0:
                    pe.wait_ge(acc_free, v_out_no.at())
                pe.wait_ge(a_lo_done, hd.at(1 + n))
                for j in range(QT):
                    toks, cols = slice(P * j, P * (j + 1)), slice(SB_OFF[j], SB_OFF[j] + SB_LEN[j])
                    dst = ps[n][:, P * j:S]
                    nc.tensor.matmul(dst, v_hi[:, toks], pa_hi[n][:, cols], start=j == 0, stop=False)
                    nc.tensor.matmul(dst, v_hi[:, toks], pa_lo[n][:, cols], start=False, stop=False)
                    last = nc.tensor.matmul(dst, v_lo[:, toks], pa_hi[n][:, cols], start=False, stop=j == QT - 1)
                last.then_inc(pv_done, 1)

            v_out_no = Tally(4)

            def turn(src, blocks):
                dst = output()
                for b in range(blocks):
                    last = nc.tensor.transpose(dst[:, P * b:P * (b + 1)], src[:, P * b:P * (b + 1)], ident[:])
                last.then_inc(tr_done, 1)
                tr.add()

            def sb_last():
                scores(0)
                scores(1)
                pe.wait_ge(acc_free, out_no.at())
                turn(vt, QT)
                panel(act_tile)
                tails(0)
                dst = output()[:]
                unit(dst, [act_tile(k) for k in range(UK)], True, False)
                tails(1)
                unit(dst, [act_tile(UK + k) for k in range(UK)], False, True)
                values(0)
                values(1)
                hd.add(2)

            def sb_body():
                scores(0)
                scores(1)
                pe.wait_ge(acc_free, out_no.at())
                turn(vt, QT)
                panel(act_tile)
                tails(0)
                dst = output()[:]
                unit(dst, first, True, False)
                tails(1)
                unit(dst, second, False, True)
                values(0)
                dst = output()[:]
                unit(dst, first, True, False)
                values(1)
                unit(dst, second, False, True)
                hd.add(2)
                v_out_no.add(4)

            pe.wait_ge(const_r_ready, 2)
            panel(act_tile, arrive=lambda k: (h_lo, k + 1))
            first, second = ([act_tile(UK * n + k) for k in range(UK)] for n in range(2))
            dst = output()[:]
            unit(dst, first, True, False)
            pe.wait_ge(sq_done, 1)
            pe.wait_ge(half_summed, len(OTHER_TILES) + 1)
            nc.tensor.matmul(ps[0][:, 0:S], ones[:], sq_sum[:], start=True, stop=False)
            nc.tensor.matmul(ps[0][:, 0:S], ones[:], sq_half[:], start=False, stop=True).then_inc(stat_done, 1)
            unit(dst, second, False, True)
            panel(act_tile)
            with repeat(pe, (PAIRS - 2) // 2, [(u, 12), (out_no, 8), (hd, 4), (tr, 2), (v_out_no, 8)]):
                sb_body()
                sb_body()
            sb_body()
            sb_last()

            def gates(o_written):
                def branches():
                    for _ in range(2):
                        unit(output()[:], [o_tile(k) for k in range(UK)], True, True)

                def next_gates():
                    panel(act_tile)
                    panel(act_tile)

                pe.wait_ge(ps_free, 2 + o_written)
                with repeat(pe, (KT // 2 - 1) // 2, [(u, 12), (out_no, 8)]):
                    for _ in range(2):
                        branches()
                        next_gates()
                branches()
                next_gates()
                branches()

            gates(2 * PAIRS)
            assert out_no.n == A_SWA and u.n == U_SWA

            def swa_scores(t, hf):
                if hf == 0:
                    pe.wait_ge(qa_ready, t + 3)
                for i in range(2):
                    qt = 2 * hf + i
                    for n in range(2):
                        rows = slice(HD * n, HD * n + HD)
                        for side, kb in ((0, max(qt - 1, 0)), (1, qt)):
                            at = S * n + 2 * P * i + P * side
                            last = nc.tensor.matmul(ps[hf][:, at:at + P], qa[rows, P * qt:P * (qt + 1)],
                                                    ka[rows, t // GQ, P * kb:P * (kb + 1)], start=True, stop=True)
                last.then_inc(s_done, 1)

            def swa_turn(t, hf):
                pe.wait_ge(prob_ready, 2 * t + hf + 1)
                for b in range(8):
                    last = nc.tensor.transpose(ps[hf][:, P * b:P * (b + 1)],
                                               s_a[:, b // 2, P * (b % 2):P * (b % 2 + 1)], ident[:])
                last.then_inc(ptr_done, 1)

            def swa_values(t, hf):
                pe.wait_ge(pt_ready, 2 * t + hf + 1)
                pe.wait_ge(ps_free, 2 * PAIRS + 2 * t + hf + 1)
                for n in range(2):
                    for i in range(2):
                        qt = 2 * hf + i
                        dst = ps[hf][:, 2 * S + P * (2 * n + i):2 * S + P * (2 * n + i + 1)]
                        sides = [(1, qt)] + ([(0, qt - 1)] if qt else [])
                        for m, (side, kb) in enumerate(sides):
                            b = 2 * (2 * n + i) + side
                            last = nc.tensor.matmul(dst, va[:, kb, P * (t // GQ):P * (t // GQ + 1)],
                                                    pt_a[:, P * b:P * (b + 1)], start=m == 0, stop=m == len(sides) - 1)
                last.then_inc(pv_done, 1)

            panel(act_tile)
            panel(act_tile)
            panel(act_tile)
            for n in range(2):
                turn(va_t[n], QT)
            panel(act_tile)
            panel(act_tile)
            dst = output()[:]
            unit(dst, first, True, False)
            for t in range(PAIRS):
                swa_scores(t, 0)
                if t:
                    swa_values(t - 1, 1)
                swa_scores(t, 1)
                unit(dst, second, False, True)
                swa_turn(t, 0)
                dst = output()[:]
                unit(dst, first, True, False)
                swa_values(t, 0)
                swa_turn(t, 1)
            unit(dst, second, False, True)
            swa_values(PAIRS - 1, 1)
            assert out_no.n == A_DA + 2 and u.n == U_DA + 4
            swa.n, hd.n = 2 * PAIRS, 4 * PAIRS

            gates(4 * PAIRS)
            assert out_no.n == A_OUT and u.n == U_OUT

            def out_units(n, turns):
                with repeat(pe, turns, [(u, 4), (out_no, 4)]):
                    for b in range(4):
                        unit(output()[:], [act_tile(UK * n + k) for k in range(UK)], True, True)

            for b in range(4):
                unit(output()[:], first, True, True, (lambda k: (mg_lo, k + 1)) if b == 0 else None)
            out_units(0, KT // 4 - 1)
            pe.wait_ge(mg_lo, KT)
            out_units(1, KT // 4)

            panel(hc_tile, arrive=lambda k: (h_lo, KT + k + 1))
            stat(2, 3, ps[0], sq_sum, S)
            for _ in range(XH - 1):
                panel(hc_tile)
            panel(mem_tile, NM, arrive=lambda k: (mem_lo, k + 1))
            stat(3, 2, ps[1], mem_stat, NM)
            for _ in range(XH - 1):
                panel(mem_tile, NM)

            def x_scores(n):
                for t in range(QT):
                    last = nc.tensor.matmul(ps[n % 2][:, NM * t:NM * (t + 1)], qx[:, n, P * t:P * (t + 1)],
                                            kx[:, n, :], start=True, stop=True)
                last.then_inc(s_done, 1)

            def x_turn(n):
                pe.wait_ge(prob_ready, swa.at(1))
                for b in range(2):
                    for t in range(QT):
                        last = nc.tensor.transpose(ps[n % 2][:, S * b + P * t:S * b + P * (t + 1)],
                                                   s_x[:, t, P * b:P * (b + 1)], ident[:])
                last.then_inc(ptr_done, 1)

            def x_values(n):
                pe.wait_ge(pt_ready, swa.at(1))
                for b in range(2):
                    last = nc.tensor.matmul(ps[n % 2][:, 2 * S:3 * S], vx[:, b, XD * n:XD * (n + 1)], pt_x[:, b, :],
                                            start=b == 0, stop=b == 1)
                last.then_inc(pv_done, 1)
                swa.add()

            pe.wait_ge(acc_free, A_XKV + XH)
            x_scores(0)
            panel(mem_tile, NM)
            panel(mem_tile, NM)
            pe.wait_ge(acc_free, out_no.at())
            panel(mem_tile, NM)

            def v_turn():
                dst = output()
                for b in range(4):
                    last = nc.tensor.transpose(dst[:, P * b:P * (b + 1)], vt[:, P * b:P * (b + 1)], ident[:])
                last.then_inc(tr_done, 1)

            v_turn()
            panel(mem_tile, NM)
            pe.wait_ge(acc_free, out_no.at())
            v_turn()
            x_scores(1)
            for n in range(XH):
                x_turn(n)
                if n == 0:
                    pe.wait_ge(acc_free, out_no.at())
                x_values(n)
                if n + 2 < XH:
                    pe.wait_ge(ps_free, 4 * PAIRS + n + 3)
                    x_scores(n + 2)

            pe.wait_ge(ps_free, 4 * PAIRS + XH + 2)
            with repeat(pe, KT // 8, [(u, 4), (out_no, 8)]):
                for b in range(4):
                    two_outputs()

            stat(4, 4, ps[0], sq_sum, S)
            pe.wait_ge(h_lo, 3 * KT)

            def ffn():
                with repeat(pe, GROUP, [(u, 4), (out_no, 2)]):
                    panel(act_tile)
                    panel(act_tile)
                hid.add(GROUP)
                with repeat(pe, 2, [(u, 4), (out_no, 8)]):
                    for b in range(4):
                        two_outputs(hid.at() if b == 0 else None)

            with repeat(pe, GROUPS - 1, [(u, FFN_UNITS), (out_no, GROUP * 2 + KT), (hid, GROUP)]):
                ffn()
            ffn()
            assert out_no.n == A_END and u.n == UNITS
            stat(5, 5, ps[1], sq_sum, S)


def stream(m, halves_outside=False):
    k, n = m.shape
    b = m.reshape(k // P, P, n // P, P)
    if halves_outside:
        b = b.reshape(k // P // UK, UK, P, n // P, P).transpose(0, 3, 2, 1, 4)
    else:
        b = b.transpose(2, 0, 1, 3).reshape(-1, UK, P, P).transpose(0, 2, 1, 3)
    return b.reshape(-1, P, UK * P)


def columns(m, n):
    return m[:, P * n:P * (n + 1)]


GQ = SWA_HEADS // SWA_KV
LOWER = [g * GQ + i for g in range(0, SWA_KV, 2) for i in range(GQ)]
HEADS = [h + o * GQ for h in LOWER for o in (0, 1)]


def gates_and_branches(w_gate, w_branch):
    gates, branches = ([stream(columns(w, m)) for m in range(KT)] for w in (w_gate, w_branch))
    parts = gates[:2]
    for m in range(0, KT, 2):
        parts += branches[m:m + 2] + gates[m + 2:m + 4]
    return parts


def weight_stream(w_in, w_gate, w_a, w_b, w_out, w_xq, w_xkv, w_xo, w_gu, w_down):
    qa, ka, va, qb, kb, vb = np.split(w_in, np.cumsum([SWA_W, KV_W, KV_W, SB_W, SB_W]), axis=1)
    qa = qa.reshape(D, SWA_HEADS, HD)[:, HEADS].reshape(D, SWA_W)
    w_a = w_a.reshape(SWA_HEADS, HD, D)[HEADS].reshape(SWA_W, D)
    parts = [stream(columns(m, p)) for p in range(PAIRS) for m in (qb, kb, vb)]
    parts += gates_and_branches(w_gate[:, D:], w_b)
    parts += [stream(columns(va, 0)), stream(columns(va, 1)), stream(ka), stream(qa)]
    parts += gates_and_branches(w_gate[:, :D], w_a)
    parts += [stream(w_out, True), stream(w_xq), stream(w_xkv), stream(w_xo)]
    width = GROUP * P
    for g in range(GROUPS):
        for t in range(GROUP):
            parts += [stream(columns(w_gu, g * GROUP + t)), stream(columns(w_gu, FFN // P + g * GROUP + t))]
        parts += [stream(w_down[width * g:width * (g + 1)])]
    return np.concatenate(parts)


def tiles(v):
    return v.reshape(-1, P).T


def kernel(x, mem, positions, norm_mix_g, w_in, sinks, w_branch_a, w_branch_b, w_gate, b_gate, w_out,
           norm_cross_g, norm_mem_g, w_xq, w_xkv, w_xo, norm_ffn_g, w_gu, w_down, final_norm_g):
    import concourse.bacc as bacc
    from concourse.bass_utils import run_bass_kernel_spmd

    a = {k: np.asarray(v) for k, v in locals().items() if k not in ("bacc", "run_bass_kernel_spmd")}
    w = weight_stream(*(a[k][0] for k in ("w_in", "w_gate", "w_branch_a", "w_branch_b", "w_out", "w_xq", "w_xkv",
                                          "w_xo", "w_gu", "w_down")))
    params = np.concatenate(
        [tiles(a[k].reshape(-1)) for k in ("norm_mix_g", "norm_cross_g", "norm_mem_g", "norm_ffn_g", "final_norm_g",
                                           "b_gate")]
        + [np.broadcast_to(a["sinks"][0][HEADS], (P, SWA_HEADS))], axis=1)
    inv = (ROPE_THETA ** (-np.arange(HALF, dtype=np.float64) / HALF)).astype(np.float32)
    sign = np.repeat(np.array([-1, 1], np.float32), HALF)
    arrays = {
        "w_stream": w,
        "x_t": a["x"][0].T.reshape(KT, P, S).transpose(1, 0, 2),
        "mem_t": a["mem"][0].T.reshape(KT, P, NM).transpose(1, 0, 2),
        "params": params,
        "rope_const": np.stack([np.tile(inv, P // HALF), np.tile(sign, P // HD)], axis=1),
        "pos": np.broadcast_to(a["positions"].astype(np.int32), (P, S)),
    }
    arrays = {k: np.ascontiguousarray(v) for k, v in arrays.items()}
    nc = bacc.Bacc("TRN2", target_bir_lowering=False, num_devices=1)
    args = [nc.dram_tensor(k, v.shape, mybir.dt.from_np(v.dtype), kind="ExternalInput").ap() for k, v in arrays.items()]
    out = nc.dram_tensor("out_t", (KT, P, S), mybir.dt.float32, kind="ExternalOutput").ap()
    block_kernel(nc, *args, out)
    r = run_bass_kernel_spmd(nc, [arrays], core_ids=[0])
    return r.results[0]["out_t"].reshape(D, S).T[None]
```

```python
import numpy as np
from contextlib import ExitStack, contextmanager

import concourse.bass as bass
from concourse import mybir

P = 128
D = 2048
S = 512
KT = D // P
HD = 64
HALF = HD // 2
SWA_HEADS, SWA_KV = D // 128, D // 128 // 4
SWA_W, KV_W = SWA_HEADS * HD, SWA_KV * HD
SB_W = (D // 128) * HD
PAIRS = SB_W // P
MIX_KT = SB_W // P
NM = 256
XH, XD = 4, 128
FFN = -(-8 * D // 768) * 256
UK = 8
RING = 4
AHEAD = RING - 1
GROUP = 4
GROUPS = FFN // P // GROUP
X_TILES = 2
CHUNK = 64
EPS = 1e-6
NEG = -1e30
ROPE_THETA = 10000.0
QT = S // P

U_SB = 0
U_DB = U_SB + PAIRS * 6
U_SWA = U_DB + KT * 3
U_DA = U_SWA + 4 * 2 + PAIRS * 2
U_OUT = U_DA + KT * 3
U_X = U_OUT + KT * 2
U_XO = U_X + 3 * XH * 2
U_FFN = U_XO + KT // 2
FFN_UNITS = GROUP * 4 + KT // 2
UNITS = U_FFN + GROUPS * FFN_UNITS

A_DB = PAIRS * 4
A_SWA = A_DB + KT * 2
A_DA = A_SWA + 4 + PAIRS
A_OUT = A_DA + KT * 2
A_X = A_OUT + KT * 2
A_XO = A_X + 3 * XH + 2
A_FFN = A_XO + KT
A_END = A_FFN + GROUPS * (GROUP * 2 + KT)

G_MIX, G_CROSS, G_MEM, G_FFN, G_FINAL = (KT * n for n in range(5))
B_GATE = 5 * KT
SINK = B_GATE + 2 * KT
PARAMS = SINK + SWA_HEADS

SB_OFF = (0, 512, 1024, 896)
SB_LEN = tuple(S - P * j for j in range(QT))
SB_COLS = sum(SB_LEN)


ROUND = float(3 << 22)
TWO_PI = (6.28125, 0.0019350051879882812, float(2 * np.pi - 6.28125 - 0.0019350051879882812))
PI_DOWN = 3.1415925


MERGED_EARLY = 6
POOL_TILES = (1, 3, 5, 7, 9, 11, 13)
OTHER_TILES = tuple(m for m in range(KT) if m not in POOL_TILES)


class Tally:

    def __init__(self, n=0):
        self.n, self.loops = n, []

    def at(self, k=0):
        v = self.n + k
        for i, stride in self.loops:
            v = i * stride + v
        return v

    def add(self, k=1):
        self.n += k


@contextmanager
def repeat(eng, times, strides):
    with eng.Fori(0, times) as i:
        began = [(t, t.n, s) for t, s in strides]
        for t, s in strides:
            t.loops.append((i, s))
        yield i
        for t, n, s in began:
            assert t.n - n == s, (t.n - n, s)
            t.n = n + s * times
            t.loops.pop()


def block_kernel(nc, w, xT, memT, params, rope_const, pos, out):
    F32, F32R, BF16, I32 = mybir.dt.float32, mybir.dt.float32r, mybir.dt.bfloat16, mybir.dt.int32
    ALU, ACT, AX = mybir.AluOpType, mybir.ActivationFunctionType, mybir.AxisListType
    ctx = ExitStack()
    with ctx:
        def sb(name, shape, dt, stack=ctx):
            return stack.enter_context(nc.sbuf_tensor(name, shape, dt))

        def sem(name):
            return ctx.enter_context(nc.semaphore(name))

        stat_x = sb("stat_x", [P, 3, 4], F32)
        par = sb("par", [P, PARAMS], F32)
        rc = sb("rc", [P, 2], F32)
        ident = sb("ident", [P, P], F32)
        ones = sb("ones", [P, P], F32)
        ones_r = sb("ones_r", [P, P], F32R)
        tri_r = sb("tri_r", [P, P], F32R)
        eps_t = sb("eps_t", [P, 1], F32)
        rstd = sb("rstd", [P, S], F32)
        sq_sum = sb("sq_sum", [P, S], F32)
        act_hi = sb("act_hi", [P, KT, S], F32R)
        act_lo = sb("act_lo", [P, KT, S], F32R)
        raw = sb("raw", [P, RING, UK * P], F32)
        w_hi = sb("w_hi", [P, RING, UK * P], F32R)
        w_lo = sb("w_lo", [P, RING, UK * P], F32R)

        with ExitStack() as a:
            x = sb("x", [P, KT, S], F32, a)
        o_hi = sb("o_hi", [P, MIX_KT, S], F32R)
        o_lo = sb("o_lo", [P, MIX_KT, S], F32R)

        with ExitStack() as a:
            sb_mask = sb("sb_mask", [P, SB_COLS], BF16, a)
            zb = [sb(f"zb{n}", [P, SB_COLS], F32, a) for n in range(2)]
            pf = [sb(f"pf{n}", [P, SB_COLS], F32, a) for n in range(2)]
            pa_hi = [sb(f"pa_hi{n}", [P, SB_COLS], F32R, a) for n in range(2)]
            pa_lo = [sb(f"pa_lo{n}", [P, SB_COLS], F32R, a) for n in range(2)]
            q_hi, k_hi, v_hi = (sb(f"{n}_hi", [P, S], F32R, a) for n in "qkv")
            q_lo, k_lo, v_lo = (sb(f"{n}_lo", [P, S], F32R, a) for n in "qkv")
            scaled = sb("scaled", [P, S], F32, a)
        vt = rb = sq_sum

        with ExitStack() as a:
            merged = sb("merged", [P, KT, S], F32, a)
        act2_hi = sb("act2_hi", [P, UK, S], F32R)
        act2_lo = sb("act2_lo", [P, UK, S], F32R)

        with ExitStack() as a:
            cos_t = sb("cos_t", [P, S], F32, a)
            sin_t = sb("sin_t", [P, S], F32, a)
            ka = sb("ka", [P, 2, S], F32, a)
            va = sb("va", [P, QT, KV_W], F32, a)
            qa = sb("qa", [P, S], F32, a)
            ra = sb("ra", [P, S], F32, a)
            s_a = sb("s_a", [P, 4, 2 * P], F32, a)
            pt_a = sb("pt_a", [P, 8 * P], F32, a)
            band = sb("band", [P, 2, 2 * P], BF16, a)
            stat_a = sb("stat_a", [P, 2, 6, 4], F32, a)
        mem_stat = sb("mem_stat", [P, NM], F32)
        qx = sb("qx", [P, XH, S], F32)
        with ExitStack() as a:
            mem = sb("mem", [P, KT, NM], F32, a)
        with ExitStack() as a:
            kx = sb("kx", [P, XH, NM], F32, a)
            vx = sb("vx", [P, 2, XH * XD], F32, a)
            s_x = sb("s_x", [P, 4, NM], F32, a)
            pt_x = sb("pt_x", [P, 2, S], F32, a)
        with ExitStack() as a:
            gt = sb("gt", [P, S], F32, a)
            sg = sb("sg", [P, S], F32, a)

        va_t = tuple(s_a[:, 2 * n:2 * n + 2, :].rearrange("p a b -> p (a b)") for n in range(2))
        gate_b, gate_a = (scaled, vt), (ra, rb)
        sq_half = scaled

        square_tmp = (gt, sg)

        acc = [ctx.enter_context(nc.psum_tensor(f"acc{n}", [P, S], F32)) for n in range(2)]
        ps = [ctx.enter_context(nc.psum_tensor(f"ps{n}", [P, 3 * S], F32)) for n in range(2)]

        raw_in = [sem(f"raw_in{n}") for n in range(RING)]
        hi_done, lo_done = sem("hi_done"), sem("lo_done")
        unit_done = sem("unit_done")
        half_done = sem("half_done")
        acc_free = sem("acc_free")
        par_in, pos_in, mem_in = sem("par_in"), sem("pos_in"), sem("mem_in")
        x_in = [sem(f"x_in{n}") for n in range(KT // X_TILES)]
        const_ready, const_r_ready = sem("const_ready"), sem("const_r_ready")
        half_squared, half_summed = sem("half_squared"), sem("half_summed")
        h_hi, h_lo = sem("h_hi"), sem("h_lo")
        mg_hi, mg_lo = sem("mg_hi"), sem("mg_lo")
        mem_hi, mem_lo = sem("mem_hi"), sem("mem_lo")
        cross_squared, cross_summed = sem("cross_squared"), sem("cross_summed")
        squared, squares_added = sem("squared"), sem("squares_added")
        sq_ready, sq_done = sem("sq_ready"), sem("sq_done")
        stat_done, std_ready, rstd_ready = sem("stat_done"), sem("std_ready"), sem("rstd_ready")
        z_done, t_done, pv_done = sem("z_done"), sem("t_done"), sem("pv_done")
        zb_ready, lb_ready, p_ready = sem("zb_ready"), sem("lb_ready"), sem("p_ready")
        soft_ready = sem("soft_ready")
        p_hi_done, p_lo_done = sem("p_hi_done"), sem("p_lo_done")
        u_ready, a_ready, a_hi_done, a_lo_done = (sem(n) for n in ("u_ready", "a_ready", "a_hi_done", "a_lo_done"))
        o_hi_done = sem("o_hi_done")
        ps_free = sem("ps_free")
        qk_hi_done, qk_lo_done = sem("qk_hi_done"), sem("qk_lo_done")
        tr_done, v_hi_done, va_ready = sem("tr_done"), sem("v_hi_done"), sem("va_ready")
        sig_ready, mix_ready = sem("sig_ready"), sem("mix_ready")
        ang_ready, trig_ready = sem("ang_ready"), sem("trig_ready")
        rot_ready, qa_ready = sem("rot_ready"), sem("qa_ready")
        s_done, max_ready, exp_ready, prob_ready = (sem(n) for n in ("s_done", "max_ready", "exp_ready", "prob_ready"))
        ptr_done, pt_ready = sem("ptr_done"), sem("pt_ready")
        hid_hi = sem("hid_hi")
        hid_lo = sem("hid_lo")
        out_ready, stored = sem("out_ready"), sem("stored")
        act_step, dve_step = sem("act_step"), sem("dve_step")

        def act_tile(k):
            return act_hi[:, k, :], act_lo[:, k, :]

        def hc_tile(k):
            return act_tile(k) if k < UK else (act2_hi[:, k - UK, :], act2_lo[:, k - UK, :])

        def o_tile(k):
            return o_hi[:, k, :], o_lo[:, k, :]

        def act2_tile(k):
            return act2_hi[:, k, :], act2_lo[:, k, :]

        mem_hi_v = act_hi[:, UK:KT, :].rearrange("p a (b n) -> p (a b) n", n=NM)
        mem_lo_v = act_lo[:, UK:KT, :].rearrange("p a (b n) -> p (a b) n", n=NM)

        def mem_tile(k):
            return mem_hi_v[:, k, :], mem_lo_v[:, k, :]

        def f(ap):
            return ap.bitcast(F32)

        block = ctx.enter_context(nc.Block())

        @block.sync
        def _(sp):
            sp.dma_start(raw[:, 0, :], w[0, :, :]).then_inc(raw_in[0], 16)
            for c in range(KT // X_TILES):
                part = slice(X_TILES * c, X_TILES * (c + 1))
                sp.dma_start(x[:, part, :], xT[:, part, :]).then_inc(x_in[c], 16)
                if c in (2, 5):
                    s = (c + 1) // 3
                    sp.dma_start(raw[:, s, :], w[s, :, :]).then_inc(raw_in[s], 16)
            sp.dma_start(raw[:, 3, :], w[3, :, :]).then_inc(raw_in[3], 16)
            with sp.Fori(1, UNITS // RING) as i:
                for s in range(RING):
                    sp.wait_ge(lo_done, i * RING + (s - RING + 1))
                    sp.dma_start(raw[:, s, :], w[i * RING + s, :, :]).then_inc(raw_in[s], 16)
            for m in range(KT):
                sp.wait_ge(out_ready, m + 1)
                sp.dma_start(out[m, :, :], x[:, m, :]).then_inc(stored, 16)
            sp.wait_ge(stored, 16 * KT)

        @block.gpsimd
        def _(pool):
            step = Tally()

            def link(ins):
                ins.then_inc(sq_ready, 1)
                step.add()
                pool.wait_ge(sq_ready, step.at())

            link(nc.gpsimd.memset(ident[:], 0.0))
            link(nc.gpsimd.affine_select(out=ident[:], in_=ident[:], compare_op=ALU.not_equal, fill=1.0,
                                         base=0, pattern=[[-1, P]], channel_multiplier=1))
            nc.gpsimd.memset(ones[:], 1.0).then_inc(const_ready, 1)
            nc.gpsimd.memset(eps_t[:], EPS).then_inc(const_ready, 1)
            link(nc.gpsimd.memset(zb[0][:, 0:P], 1.0))
            nc.gpsimd.affine_select(out=zb[0][:, 0:P], in_=zb[0][:, 0:P], compare_op=ALU.is_gt, fill=0.0,
                                    base=0, pattern=[[-1, P]], channel_multiplier=1).then_inc(const_ready, 1)
            link(nc.gpsimd.memset(sb_mask[:], 0.0))
            for j in range(QT):
                d = sb_mask[:, SB_OFF[j]:SB_OFF[j] + P]
                last = nc.gpsimd.affine_select(out=d, in_=d, compare_op=ALU.is_gt, fill=NEG, base=0,
                                               pattern=[[1, P]], channel_multiplier=-1)
            last.then_inc(const_ready, 1)

            def squares(tile, tmp, total):
                link(nc.gpsimd.tensor_tensor(tmp, tile, tile, ALU.mult))
                link(nc.gpsimd.tensor_tensor(total, total, tmp, ALU.add))

            link(nc.gpsimd.memset(sq_sum[:], 0.0))
            for m in POOL_TILES:
                pool.wait_ge(x_in[m // X_TILES], 16)
                squares(x[:, m, :], rstd[:], sq_sum[:])
            nc.gpsimd.tensor_copy(sq_sum[:, 0:1], sq_sum[:, 0:1]).then_inc(sq_done, 1)

            pool.wait_ge(acc_free, A_SWA)
            link(nc.gpsimd.memset(band[:], 0.0))
            link(nc.gpsimd.memset(band[:, :, 0:CHUNK], NEG))
            link(nc.gpsimd.memset(band[CHUNK:P, :, CHUNK:P], NEG))
            link(nc.gpsimd.memset(band[0:CHUNK, :, P + CHUNK:2 * P], NEG))
            nc.gpsimd.memset(band[:, 0, 0:P], NEG).then_inc(const_ready, 1)

            pool.wait_ge(mem_in, 16)
            link(nc.gpsimd.memset(mem_stat[:], 0.0))
            with repeat(pool, KT, [(step, 2)]) as m:
                squares(mem[:, m, :], rstd[:, 0:NM], mem_stat[:])
            nc.gpsimd.tensor_copy(mem_stat[:, 0:1], mem_stat[:, 0:1]).then_inc(sq_done, 1)

            pool.wait_ge(acc_free, A_OUT + KT + 1)
            link(nc.gpsimd.memset(sq_sum[:], 0.0))
            with repeat(pool, KT, [(step, 2)]) as m:
                pool.wait_ge(acc_free, m + (A_OUT + KT + 1))
                squares(x[:, m, :], rstd[:], sq_sum[:])
            nc.gpsimd.tensor_copy(sq_sum[:, 0:1], sq_sum[:, 0:1]).then_inc(sq_done, 1)

            pool.wait_ge(acc_free, A_XO + 1)
            link(nc.gpsimd.memset(sq_sum[:], 0.0))
            for m in range(KT):
                pool.wait_ge(cross_squared, m + 1)
                nc.gpsimd.tensor_tensor(sq_sum[:], sq_sum[:], square_tmp[m % 2][:], ALU.add)\
                    .then_inc(cross_summed, 1)
                pool.wait_ge(cross_summed, m + 1)

        @block.scalar
        def _(act):
            act.dma_start(par[:], params).then_inc(par_in, 16)

            hd, step, pair, out_no, tr = Tally(), Tally(), Tally(), Tally(), Tally()

            def link(ins):
                ins.then_inc(act_step, 1)
                step.add()
                act.wait_ge(act_step, step.at())

            converted = Tally()

            def convert():
                s = converted.n % RING
                loop = [(i, st // RING) for i, st in converted.loops]
                turn = converted.n // RING + 1
                for i, st in loop:
                    turn = i * st + turn
                act.wait_ge(raw_in[s], turn * 16)
                if converted.loops or converted.n >= RING:
                    act.wait_ge(unit_done, converted.at(1 - RING))
                nc.scalar.activation(w_hi[:, s, :], raw[:, s, :], ACT.Copy).then_inc(hi_done, 1)
                converted.add()

            def units(n=1):
                for _ in range(n):
                    convert()

            def x_square(m):
                if m in OTHER_TILES:
                    n = OTHER_TILES.index(m)
                    if n >= 2:
                        act.wait_ge(half_summed, n)
                    nc.scalar.activation(pf[n % 2][:, 0:S], x[:, m, :], ACT.Square).then_inc(half_squared, 1)

            nc.scalar.preload_act_table_set("sqrt_and_others")
            convert()
            act.wait_ge(par_in, 16)
            for m in range(KT):
                if m % X_TILES == 0:
                    act.wait_ge(x_in[m // X_TILES], 16)
                nc.scalar.activation(act_hi[:, m, :], x[:, m, :], ACT.Copy,
                                     scale=par[:, G_MIX + m:G_MIX + m + 1]).then_inc(h_hi, 1)
                if m in (5, 11):
                    convert()
            for m in range(KT):
                x_square(m)
            assert converted.n == AHEAD

            def std(n, bank, dst, width):
                act.wait_ge(stat_done, n)
                if n == 1:
                    act.wait_ge(const_ready, 4)
                nc.scalar.activation(dst[:, 0:width], bank[:, 0:width], ACT.Sqrt, bias=eps_t[:, 0:1],
                                     scale=1.0 / D).then_inc(std_ready, 1)

            def soft(par_):
                act.wait_ge(zb_ready, hd.at(1 + par_))
                link(nc.scalar.activation(pf[par_][:], zb[par_][:], ACT.Abs))
                link(nc.scalar.activation(pf[par_][:], pf[par_][:], ACT.Exp, scale=-1.0))
                nc.scalar.activation(pf[par_][:], pf[par_][:], ACT.Ln, bias=1.0).then_inc(soft_ready, 1)

            def p_high(par_):
                act.wait_ge(p_ready, hd.at(1 + par_))
                nc.scalar.activation(pa_hi[par_][:], pf[par_][:], ACT.Copy).then_inc(p_hi_done, 1)

            def a_high(par_):
                act.wait_ge(u_ready, hd.at(1 + par_))
                nc.scalar.activation(pf[par_][:], zb[par_][:], ACT.Exp).then_inc(a_ready, 1)
                act.wait_ge(a_ready, hd.at(1 + par_))
                nc.scalar.activation(pa_hi[par_][:], pf[par_][:], ACT.Copy).then_inc(a_hi_done, 1)

            def o_high(par_):
                act.wait_ge(pv_done, hd.at(1 + par_))
                rows = slice(HD * par_, HD * par_ + HD)
                nc.scalar.activation(o_hi[rows, pair.at(), :], ps[par_][rows, 0:S], ACT.Copy)\
                    .then_inc(o_hi_done, 1)

            def read_out():
                act.wait_ge(acc_free, out_no.at(1))
                out_no.add()

            def qk_high(dst):
                read_out()
                nc.scalar.activation(dst[:], scaled[:], ACT.Copy).then_inc(qk_hi_done, 1)

            def v_high():
                act.wait_ge(tr_done, tr.at(1))
                nc.scalar.activation(v_hi[:], acc[1][:], ACT.Copy).then_inc(v_hi_done, 1)
                tr.add()
                out_no.add()

            def sb_body():
                soft(0)
                soft(1)
                p_high(0)
                v_high()
                p_high(1)
                units(3)
                a_high(0)
                qk_high(q_hi)
                units()
                a_high(1)
                qk_high(k_hi)
                units()
                o_high(0)
                units()
                out_no.add()
                o_high(1)
                hd.add(2)
                pair.add()

            units(2)
            std(1, ps[0], rstd, S)
            units(1)
            qk_high(q_hi)
            units()
            qk_high(k_hi)
            units(2)
            out_no.add()
            nc.scalar.preload_act_table_set("natural_log_exp_and_others")
            with repeat(act, (PAIRS - 2) // 2, [(converted, 12), (hd, 4), (step, 8), (pair, 2), (out_no, 8), (tr, 2)]):
                sb_body()
                sb_body()
            sb_body()

            def sigmoid(tile, column):
                read_out()
                nc.scalar.activation(tile[:], tile[:], ACT.Sigmoid, bias=par[:, bass.ds(column, 1)])\
                    .then_inc(sig_ready, 1)

            def gates(gate_tiles, first, merge=lambda first, n: None):
                def turn(m):
                    units(2)
                    out_no.add(2)
                    for b in range(2):
                        units(2)
                        sigmoid(gate_tiles[b], m + (b + 2 + first))

                nc.scalar.preload_act_table_set("sigmoid_and_others")
                with repeat(act, (KT // 2 - 1) // 2, [(converted, 12), (out_no, 8)]) as i:
                    turn(i * 4)
                    turn(i * 4 + 2)
                turn(KT - 4)
                merge(0, MERGED_EARLY)
                units()
                merge(MERGED_EARLY, KT - 2 - MERGED_EARLY)
                units()
                out_no.add(2)
                merge(KT - 2, 2)

            def sb_last():
                soft(0)
                soft(1)
                p_high(0)
                v_high()
                p_high(1)
                units(3)
                a_high(0)
                units()
                a_high(1)
                o_high(0)
                o_high(1)
                for b in range(2):
                    sigmoid(gate_b[b], B_GATE + KT + b)
                hd.add(2)
                pair.add()

            sb_last()
            act.dma_start(rc[:], rope_const).then_inc(pos_in, 16)
            act.wait_ge(ps_free, 2 + 2 * PAIRS)
            act.dma_start(ra[:].bitcast(I32), pos).then_inc(pos_in, 16)
            gates(gate_b, B_GATE + KT)

            act.wait_ge(ang_ready, 1)
            nc.scalar.activation(sin_t[:], sin_t[:], ACT.Sin)
            nc.scalar.activation(cos_t[:], cos_t[:], ACT.Sin).then_inc(trig_ready, 1)
            swa = Tally()

            def rotate(n, units_used, a):
                act.wait_ge(unit_done, units_used)
                if n:
                    act.wait_ge(qa_ready, n)
                for h in range(2):
                    for to, src in ((0, HALF), (HALF, 0)):
                        last = nc.scalar.activation(rb[HD * h + to:HD * h + to + HALF, :],
                                                    acc[a][HD * h + src:HD * h + src + HALF, :], ACT.Copy)
                last.then_inc(rot_ready, 1)

            def rotate_q(t):
                rotate(t + 2, U_SWA + 8 + 2 * (t + 1), (A_SWA + 4 + t) % 2)

            def swa_exp(t, hf):
                act.wait_ge(max_ready, 2 * t + hf + 1)
                st = stat_a[:, hf]
                for n in range(4):
                    rows = ps[hf][:, 2 * P * n:2 * P * (n + 1)]
                    nc.scalar.activation(rows, rows, ACT.Exp, bias=st[:, 1, n:n + 1], accum_out=st[:, 3, n:n + 1])
                nc.scalar.activation(st[:, 4, :], st[:, 2, :], ACT.Exp).then_inc(exp_ready, 1)

            def swa_pt(t, hf):
                act.wait_ge(ptr_done, 2 * t + hf + 1)
                nc.scalar.activation(pt_a[:], ps[hf][:, 0:2 * S], ACT.Copy).then_inc(pt_ready, 1)

            def swa_o(t, hf):
                act.wait_ge(pv_done, 2 * PAIRS + 2 * t + hf + 1)
                for h in range(2):
                    rows = slice(HD * h, HD * h + HD)
                    last = nc.scalar.activation(o_hi[rows, t, 2 * P * hf:2 * P * (hf + 1)],
                                                ps[hf][rows, 2 * S + 2 * P * h:2 * S + 2 * P * (h + 1)], ACT.Copy)
                last.then_inc(o_hi_done, 1)

            units(6)
            rotate(0, U_SWA + 6, A_SWA % 2)
            units(2)
            rotate(1, U_SWA + 8, (A_SWA + 3) % 2)
            units(2)
            rotate_q(0)
            units(1)
            for t in range(PAIRS):
                swa_exp(t, 0)
                if t:
                    swa_o(t - 1, 1)
                units()
                swa_exp(t, 1)
                if t < PAIRS - 1:
                    rotate_q(t + 1)
                swa_pt(t, 0)
                units()
                swa_o(t, 0)
                swa_pt(t, 1)
            units()
            swa_o(PAIRS - 1, 1)
            out_no.n = A_DA
            for b in range(2):
                sigmoid(gate_a[b], B_GATE + b)
            swa.n, hd.n = 2 * PAIRS, 4 * PAIRS

            def merged_high(first, n):
                act.wait_ge(unit_done, U_OUT - 2)
                for m in range(first, first + n):
                    act.wait_ge(mix_ready, m + 1)
                    nc.scalar.activation(act_hi[:, m, :], merged[:, m, :], ACT.Copy).then_inc(mg_hi, 1)

            gates(gate_a, B_GATE, merged_high)

            act.wait_ge(unit_done, U_OUT)
            for c in range(KT // X_TILES):
                part = slice(X_TILES * c, X_TILES * (c + 1))
                act.dma_start(x[:, part, :], xT[:, part, :]).then_inc(x_in[c], 16)
            act.dma_start(mem[:], memT).then_inc(mem_in, 16)
            with repeat(act, KT // 4, [(converted, 4)]):
                units(4)
            out_no.add(KT)

            def x_high(dst, m, gain):
                read_out()
                nc.scalar.activation(dst, x[:, m, :], ACT.Copy, scale=par[:, bass.ds(m + gain, 1)])\
                    .then_inc(h_hi, 1)

            for half, dst in ((0, act_hi), (1, act2_hi)):
                with repeat(act, 2, [(converted, 4), (out_no, 4)]) as i:
                    for b in range(4):
                        units()
                        x_high(dst[:, i * 4 + b, :], i * 4 + (b + UK * half), G_CROSS)

            act.wait_ge(unit_done, U_X)
            act.wait_ge(mem_in, 16)

            def mem_high(first, n):
                for m in range(first, first + n):
                    nc.scalar.activation(mem_hi_v[:, m, :], mem[:, m, :], ACT.Copy,
                                         scale=par[:, G_MEM + m:G_MEM + m + 1]).then_inc(mem_hi, 1)

            mem_high(0, KT // 2)
            units()
            mem_high(KT // 2, KT // 2)
            units()
            std(2, ps[0], rstd, S)
            units(2)
            std(3, ps[1], mem_stat, NM)
            units(6)

            def x_exp(h):
                act.wait_ge(max_ready, swa.at(1 + h))
                for n in range(4):
                    last = nc.scalar.activation(s_x[:, n, :], ps[h % 2][:, n * NM:(n + 1) * NM], ACT.Exp,
                                                bias=stat_x[:, 1, n:n + 1], scale=XD ** -0.5,
                                                accum_out=stat_x[:, 2, n:n + 1])
                last.then_inc(exp_ready, 1)

            def x_pt(h):
                if h:
                    act.wait_ge(pv_done, 4 * PAIRS + h)
                act.wait_ge(ptr_done, swa.at(1 + h))
                nc.scalar.activation(pt_x[:], ps[h % 2][:, 0:2 * S].rearrange("p (a b) -> p a b", a=2), ACT.Copy)\
                    .then_inc(pt_ready, 1)

            def x_o(h):
                act.wait_ge(pv_done, hd.at(1))
                nc.scalar.activation(act2_hi[:, h, :], ps[h % 2][:, 2 * S:3 * S], ACT.Copy).then_inc(o_hi_done, 1)
                hd.add()

            x_exp(0)
            units(8)
            x_pt(0)
            units(2)
            for h in range(1, XH - 1):
                x_exp(h)
                units()
                x_pt(h)
                units()
            act.wait_ge(unit_done, U_XO)
            x_o(0)
            x_o(1)
            x_exp(XH - 1)
            x_o(2)
            x_pt(XH - 1)
            x_o(3)
            out_no.n = A_XO

            for n in range(KT // 2):
                units()
                for m in (2 * n, 2 * n + 1):
                    x_high(act_hi[:, m, :], m, G_FFN)
                    if m > 1:
                        act.wait_ge(cross_summed, m - 1)
                    nc.scalar.activation(square_tmp[m % 2][:], x[:, m, :], ACT.Square).then_inc(cross_squared, 1)

            def hidden(t, first=False):
                if first:
                    units()
                    std(4, ps[0], rstd, S)
                    units()
                    nc.scalar.preload_act_table_set("sigmoid_and_others")
                else:
                    units(2)
                read_out()
                nc.scalar.activation(sg[:], gt[:], ACT.Sigmoid).then_inc(sig_ready, 1)
                units(2)
                read_out()
                nc.scalar.activation(act2_hi[:, t, :], gt[:], ACT.Copy).then_inc(hid_hi, 1)

            def final_square(m):
                read_out()
                if m > 2:
                    act.wait_ge(squares_added, m - 2)
                nc.scalar.activation(square_tmp[m % 2][:] if m else sq_sum[:], x[:, m, :], ACT.Square)\
                    .then_inc(squared, 1)

            def ffn(first=0, last=False):
                with repeat(act, GROUP - first, [(converted, 4), (out_no, 2)]) as t:
                    hidden(t + first)
                if last:
                    for n in range(KT // 2):
                        if n < KT // 2 - AHEAD:
                            units()
                        final_square(2 * n)
                        final_square(2 * n + 1)
                else:
                    with repeat(act, 2, [(converted, 4)]):
                        units(4)
                    out_no.add(KT)

            hidden(0, True)
            ffn(first=1)
            with repeat(act, GROUPS - 2, [(converted, FFN_UNITS), (out_no, GROUP * 2 + KT)]):
                ffn()
            ffn(last=True)
            assert converted.n == UNITS
            std(5, ps[1], rstd, S)

        @block.vector
        def _(dve):
            hd, step, pair, out_no, tr, sig = Tally(), Tally(), Tally(), Tally(), Tally(), Tally()
            converted, swa, hid = Tally(), Tally(), Tally()

            def link(ins):
                ins.then_inc(dve_step, 1)
                step.add()
                dve.wait_ge(dve_step, step.at())

            def units(n=1):
                for _ in range(n):
                    s = converted.n % RING
                    dve.wait_ge(hi_done, converted.at(1))
                    nc.vector.tensor_tensor(w_lo[:, s, :], raw[:, s, :], f(w_hi[:, s, :]), ALU.subtract)\
                        .then_inc(lo_done, 1)
                    converted.add()

            def output():
                a = acc[out_no.n % 2]
                out_no.add()
                return a

            unit = Tally()

            def rstd_of(n, dst, width):
                dve.wait_ge(std_ready, n)
                nc.vector.reciprocal(dst[:, 0:width], dst[:, 0:width]).then_inc(rstd_ready, 1)
                dve.wait_ge(rstd_ready, n)

            def scale_out(dst, k=2):
                unit.add(k)
                dve.wait_ge(unit_done, unit.at())
                nc.vector.tensor_tensor(dst, output()[:], rstd[:], ALU.mult).then_inc(acc_free, 1)

            nc.vector.memset(stat_x[:, 2, :], 0.0).then_inc(hid_lo, 1)
            nc.vector.memset(sq_half[:], 0.0).then_inc(half_summed, 1)
            for n in range(2):
                nc.vector.memset(stat_x[:, n, :], 0.0).then_inc(ps_free, 1)
            dve.wait_ge(const_ready, 4)
            nc.vector.tensor_copy(ones_r[:], ones[:]).then_inc(const_r_ready, 1)
            nc.vector.tensor_copy(tri_r[:], zb[0][:, 0:P]).then_inc(const_r_ready, 1)
            units(1)
            h = Tally()

            def x_low(dst, hi, m, gain):
                dve.wait_ge(h_hi, h.at(1))
                nc.vector.scalar_tensor_tensor(dst, x[:, m, :], par[:, bass.ds(m + gain, 1)], f(hi),
                                               ALU.mult, ALU.subtract).then_inc(h_lo, 1)
                h.add()


            def add_square(m):
                if m in OTHER_TILES:
                    n = OTHER_TILES.index(m)
                    dve.wait_ge(half_squared, n + 1)
                    dve.wait_ge(half_summed, n + 1)
                    nc.vector.tensor_tensor(sq_half[:], sq_half[:], pf[n % 2][:, 0:S], ALU.add)\
                        .then_inc(half_summed, 1)

            for m in range(KT):
                x_low(act_lo[:, m, :], act_hi[:, m, :], m, G_MIX)
                if m in (5, 11):
                    units()
            for m in range(KT):
                add_square(m)

            def z_out(n):
                dve.wait_ge(z_done, hd.at(1 + n))
                nc.vector.scalar_tensor_tensor(zb[n][:], ps[n][:, 0:SB_COLS], HD ** -0.5, sb_mask[:],
                                               ALU.mult, ALU.add).then_inc(zb_ready, 1)

            def softplus(n):
                dve.wait_ge(soft_ready, hd.at(1 + n))
                nc.vector.scalar_tensor_tensor(pf[n][:], zb[n][:], 0.0, pf[n][:], ALU.max, ALU.add)\
                    .then_inc(p_ready, 1)

            def log_beta(n):
                dve.wait_ge(p_ready, hd.at(1 + n))
                nc.vector.tensor_tensor(zb[n][:], zb[n][:], pf[n][:], ALU.subtract).then_inc(lb_ready, 1)

            def p_low(n):
                dve.wait_ge(p_hi_done, hd.at(1 + n))
                nc.vector.tensor_tensor(pa_lo[n][:], pf[n][:], f(pa_hi[n][:]), ALU.subtract)\
                    .then_inc(p_lo_done, 1)

            def tail(n):
                dve.wait_ge(t_done, hd.at(1 + n))
                nc.vector.tensor_tensor(zb[n][:], zb[n][:], ps[n][:, 0:SB_COLS], ALU.subtract)\
                    .then_inc(u_ready, 1)

            def a_low(n):
                dve.wait_ge(a_hi_done, hd.at(1 + n))
                nc.vector.tensor_tensor(pa_lo[n][:], pf[n][:], f(pa_hi[n][:]), ALU.subtract)\
                    .then_inc(a_lo_done, 1)

            def o_low(n):
                dve.wait_ge(o_hi_done, hd.at(1 + n))
                rows = slice(HD * n, HD * n + HD)
                nc.vector.tensor_tensor(o_lo[rows, pair.at(), :], ps[n][rows, 0:S], f(o_hi[rows, pair.at(), :]),
                                        ALU.subtract).then_inc(ps_free, 1)

            qk = Tally()

            def qk_scale():
                if qk.loops or qk.n:
                    dve.wait_ge(qk_lo_done, qk.at())
                scale_out(scaled[:])

            def qk_low(hi, lo):
                dve.wait_ge(qk_hi_done, qk.at(1))
                nc.vector.tensor_tensor(lo[:], scaled[:], f(hi[:]), ALU.subtract).then_inc(qk_lo_done, 1)
                qk.add()

            def qk_out(hi, lo):
                qk_scale()
                qk_low(hi, lo)

            def until_split():
                z_out(0)
                z_out(1)
                softplus(0)
                log_beta(0)
                softplus(1)
                p_low(0)
                log_beta(1)
                dve.wait_ge(v_hi_done, tr.at(1))
                nc.vector.tensor_tensor(v_lo[:], output()[:], f(v_hi[:]), ALU.subtract).then_inc(acc_free, 1)
                tr.add()
                p_low(1)
                units(3)

            def sb_body():
                until_split()
                qk_scale()
                tail(0)
                a_low(0)
                qk_low(q_hi, q_lo)
                units()
                tail(1)
                a_low(1)
                qk_out(k_hi, k_lo)
                units()
                o_low(0)
                units()
                o_low(1)
                scale_out(vt[:])
                hd.add(2)
                pair.add()

            def sb_last():
                until_split()
                dve.wait_ge(qk_lo_done, qk.at())
                scale_out(gate_b[0][:])
                tail(0)
                a_low(0)
                tail(1)
                units()
                a_low(1)
                scale_out(gate_b[1][:])
                o_low(0)
                o_low(1)
                hd.add(2)
                pair.add()

            units(2)
            rstd_of(1, rstd, S)
            units(1)
            qk_out(q_hi, q_lo)
            units()
            qk_out(k_hi, k_lo)
            units(2)
            scale_out(vt[:])
            with repeat(dve, (PAIRS - 2) // 2, [(converted, 12), (unit, 12), (hd, 4), (pair, 2), (out_no, 8),
                                                (tr, 2), (qk, 4)]):
                sb_body()
                sb_body()
            sb_body()
            sb_last()

            mixed = Tally()

            def gates(gate_tiles, first_pass):
                def branches(m, last=False):
                    for b in range(2):
                        if last and b:
                            merged_low(MERGED_EARLY, KT - 2 - MERGED_EARLY)
                        g = gate_tiles[b][:]
                        units()
                        unit.add()
                        dve.wait_ge(unit_done, unit.at())
                        dve.wait_ge(sig_ready, sig.at(1))
                        sig.add()
                        dst = merged[:, m + b, :]
                        nc.vector.tensor_tensor(dst if first_pass else g, output()[:], g, ALU.mult)\
                            .then_inc(acc_free, 1)
                        if not first_pass:
                            dve.wait_ge(acc_free, out_no.at())
                            nc.vector.tensor_tensor(dst, dst, g, ALU.add).then_inc(mix_ready, 1)
                            mixed.add()

                def next_gates():
                    for b in range(2):
                        units(2)
                        if not first_pass and b == 0:
                            dve.wait_ge(mix_ready, mixed.at())
                        scale_out(gate_tiles[b][:])

                moves = [(converted, 12), (unit, 12), (out_no, 8), (sig, 4)]
                with repeat(dve, (KT // 2 - 1) // 2, moves + ([] if first_pass else [(mixed, 4)])) as i:
                    for n in range(2):
                        branches(i * 4 + 2 * n)
                        next_gates()
                branches(KT - 4)
                next_gates()
                if not first_pass:
                    merged_low(0, MERGED_EARLY)
                branches(KT - 2, not first_pass)
                if not first_pass:
                    merged_low(KT - 2, 2)

            def merged_low(first, n):
                for m in range(first, first + n):
                    dve.wait_ge(mg_hi, m + 1)
                    nc.vector.tensor_tensor(act_lo[:, m, :], merged[:, m, :], f(act_hi[:, m, :]), ALU.subtract)\
                        .then_inc(mg_lo, 1)

            gates(gate_b, True)

            dve.wait_ge(pos_in, 32)
            link(nc.vector.tensor_copy(sin_t[:], ra[:].bitcast(I32)))
            link(nc.vector.tensor_scalar(sin_t[:], sin_t[:], rc[:, 0:1], None, ALU.mult))
            link(nc.vector.tensor_scalar(ra[:], sin_t[:], 1 / (2 * np.pi), None, ALU.mult))
            link(nc.vector.tensor_scalar(ra[:], ra[:], ROUND, None, ALU.add))
            link(nc.vector.tensor_scalar(ra[:], ra[:], -ROUND, None, ALU.add))
            for c in TWO_PI:
                link(nc.vector.scalar_tensor_tensor(sin_t[:], ra[:], -c, sin_t[:], ALU.mult, ALU.add))
            link(nc.vector.tensor_scalar(cos_t[:], sin_t[:], np.pi / 2, None, ALU.add))
            link(nc.vector.tensor_scalar(ra[:], cos_t[:], np.pi, -2 * np.pi, ALU.is_gt, ALU.mult))
            link(nc.vector.tensor_tensor(cos_t[:], cos_t[:], ra[:], ALU.add))
            link(nc.vector.tensor_scalar(cos_t[:], cos_t[:], PI_DOWN, -PI_DOWN, ALU.min, ALU.max))
            nc.vector.tensor_scalar(sin_t[:], sin_t[:], PI_DOWN, -PI_DOWN, ALU.min, ALU.max).then_inc(ang_ready, 1)

            def rope(dst, n):
                unit.add(2)
                dve.wait_ge(unit_done, unit.at())
                if n:
                    dve.wait_ge(qa_ready, n)
                dve.wait_ge(rot_ready, n + 1)
                link(nc.vector.tensor_tensor(ra[:], output()[:], cos_t[:], ALU.mult))
                nc.vector.tensor_tensor(rb[:], rb[:], sin_t[:], ALU.mult).then_inc(acc_free, 1)
                dve.wait_ge(acc_free, out_no.at())
                nc.vector.tensor_tensor(dst, ra[:], rb[:], ALU.add).then_inc(qa_ready, 1)

            def v_out(n, width, dst):
                dve.wait_ge(tr_done, tr.at(1))
                nc.vector.tensor_copy(dst, output()[:].rearrange("p (a b) -> p a b", b=width)).then_inc(acc_free, 1)
                tr.add()

            def swa_max(t, hf):
                dve.wait_ge(s_done, 2 * t + hf + 1)
                st = stat_a[:, hf]
                mask = band[:] if hf == 0 else band[:, 1:2, :].broadcast_to([P, 2, 2 * P])
                for n in range(2):
                    z = ps[hf][:, S * n:S * (n + 1)].rearrange("p (a b) -> p a b", a=2)
                    last = nc.vector.scalar_tensor_tensor(z, z, HD ** -0.5, mask, ALU.mult, ALU.add)
                link(last)
                link(nc.vector.reduce_max(st[:, 0, :], ps[hf][:, 0:2 * S].rearrange("p (a b) -> p a b", a=4), AX.X))
                for n in range(2):
                    sink = SINK + 2 * t + n
                    last = nc.vector.tensor_scalar(st[:, 0, 2 * n:2 * n + 2], st[:, 0, 2 * n:2 * n + 2],
                                                   par[:, sink:sink + 1], None, ALU.max)
                link(last)
                link(nc.vector.tensor_scalar(st[:, 1, :], st[:, 0, :], -1.0, None, ALU.mult))
                for n in range(2):
                    sink = SINK + 2 * t + n
                    last = nc.vector.tensor_scalar(st[:, 2, 2 * n:2 * n + 2], st[:, 1, 2 * n:2 * n + 2],
                                                   par[:, sink:sink + 1], None, ALU.add)
                last.then_inc(max_ready, 1)

            def swa_prob(t, hf):
                dve.wait_ge(exp_ready, 2 * t + hf + 1)
                st = stat_a[:, hf]
                link(nc.vector.tensor_tensor(st[:, 5, :], st[:, 3, :], st[:, 4, :], ALU.add))
                link(nc.vector.reciprocal(st[:, 5, :], st[:, 5, :]))
                if t or hf:
                    dve.wait_ge(ptr_done, 2 * t + hf)
                nc.vector.tensor_tensor(s_a[:], ps[hf][:, 0:2 * S].rearrange("p (a b) -> p a b", a=4),
                                        st[:, 5, :].unsqueeze(2).broadcast_to([P, 4, 2 * P]), ALU.mult)\
                    .then_inc(prob_ready, 1)

            def swa_o(t, hf):
                dve.wait_ge(o_hi_done, 2 * PAIRS + 2 * t + hf + 1)
                for n in range(2):
                    rows = slice(HD * n, HD * n + HD)
                    cols = slice(2 * P * hf, 2 * P * (hf + 1))
                    last = nc.vector.tensor_tensor(o_lo[rows, t, cols],
                                                   ps[hf][rows, 2 * S + 2 * P * n:2 * S + 2 * P * (n + 1)],
                                                   f(o_hi[rows, t, cols]), ALU.subtract)
                last.then_inc(ps_free, 1)

            units(4)
            for n in range(2):
                scale_out(va_t[n])
            dve.wait_ge(trig_ready, 1)
            link(nc.vector.scalar_tensor_tensor(sin_t[:], sin_t[:], rc[:, 1:2], rstd[:], ALU.mult, ALU.mult))
            link(nc.vector.tensor_tensor(cos_t[:], cos_t[:], rstd[:], ALU.mult))
            units(2)
            rope(ka[:, 0, :], 0)
            for n in range(2):
                dve.wait_ge(tr_done, tr.at(1))
                nc.vector.tensor_copy(va[:, :, P * n:P * (n + 1)], ps[n][:, 0:S].rearrange("p (a b) -> p a b", b=P))\
                    .then_inc(va_ready, 1)
                tr.add()
            units(2)
            rope(ka[:, 1, :], 1)
            units(2)
            rope(qa[:], 2)
            units(1)
            dve.wait_ge(const_ready, 5)
            for t in range(PAIRS):
                swa_max(t, 0)
                swa_max(t, 1)
                swa_prob(t, 0)
                if t:
                    swa_o(t - 1, 1)
                units()
                if t < PAIRS - 1:
                    rope(qa[:], t + 3)
                else:
                    dve.wait_ge(qa_ready, PAIRS + 2)
                    scale_out(gate_a[0][:])
                units()
                swa_prob(t, 1)
                swa_o(t, 0)
            units()
            scale_out(gate_a[1][:])
            swa_o(PAIRS - 1, 1)
            swa.n, hd.n = 2 * PAIRS, 4 * PAIRS

            gates(gate_a, False)

            def add_out(m):
                nc.vector.tensor_tensor(x[:, m, :], x[:, m, :], output()[:], ALU.add).then_inc(acc_free, 1)

            for m in range(KT):
                if m % X_TILES == 0:
                    dve.wait_ge(x_in[m // X_TILES], 32)
                units()
                unit.add()
                dve.wait_ge(unit_done, unit.at())
                add_out(m)

            for half, hi, lo in ((0, act_hi, act_lo), (1, act2_hi, act2_lo)):
                with repeat(dve, 2, [(converted, 4), (unit, 4), (out_no, 4), (h, 4)]) as i:
                    for b in range(4):
                        units()
                        unit.add()
                        dve.wait_ge(unit_done, unit.at())
                        add_out(i * 4 + (b + UK * half))
                        x_low(lo[:, i * 4 + b, :], hi[:, i * 4 + b, :], i * 4 + (b + UK * half), G_CROSS)

            def mem_low(first, n):
                for m in range(first, first + n):
                    dve.wait_ge(mem_hi, m + 1)
                    nc.vector.scalar_tensor_tensor(mem_lo_v[:, m, :], mem[:, m, :], par[:, G_MEM + m:G_MEM + m + 1],
                                                   f(mem_hi_v[:, m, :]), ALU.mult, ALU.subtract).then_inc(mem_lo, 1)

            mem_low(0, KT // 2)
            units()
            mem_low(KT // 2, KT // 2)
            units()
            rstd_of(2, rstd, S)
            scale_out(qx[:, 0, :])
            units(2)

            def kv_out(dst):
                unit.add(2)
                dve.wait_ge(unit_done, unit.at())
                nc.vector.tensor_tensor(dst, output()[:, 0:NM], mem_stat[:], ALU.mult).then_inc(acc_free, 1)

            rstd_of(3, mem_stat, NM)
            kv_out(kx[:, 0, :])
            units(2)
            kv_out(kx[:, 1, :])
            units(2)
            kv_out(kx[:, 2, :])
            units(2)
            kv_out(kx[:, 3, :])

            def x_max(n):
                dve.wait_ge(s_done, swa.at(1))
                link(nc.vector.reduce_max(stat_x[:, 0, :], ps[n % 2][:, 0:4 * NM].rearrange("p (a b) -> p a b", a=4),
                                          AX.X))
                nc.vector.tensor_scalar(stat_x[:, 1, :], stat_x[:, 0, :], -XD ** -0.5, None, ALU.mult)\
                    .then_inc(max_ready, 1)

            def x_prob(n):
                dve.wait_ge(exp_ready, swa.at(1))
                link(nc.vector.reciprocal(stat_x[:, 0, :], stat_x[:, 2, :]))
                nc.vector.tensor_tensor(s_x[:], s_x[:], stat_x[:, 0, :].unsqueeze(2).broadcast_to([P, 4, NM]),
                                        ALU.mult).then_inc(prob_ready, 1)
                swa.add()

            def x_o(n):
                dve.wait_ge(o_hi_done, hd.at(1))
                nc.vector.tensor_tensor(act2_lo[:, n, :], ps[n % 2][:, 2 * S:3 * S], f(act2_hi[:, n, :]),
                                        ALU.subtract).then_inc(ps_free, 1)
                hd.add()

            x_max(0)
            units(2)
            kv_out(vt[:, 0:NM])
            x_prob(0)
            units(2)
            kv_out(vt[:, NM:2 * NM])
            units(2)
            dve.wait_ge(tr_done, PAIRS + 3)
            kv_out(vt[:, 0:NM])
            v_out(0, XD, vx[:, :, 0:2 * XD].rearrange("p a (h b) -> p h a b", h=2))
            units(2)
            kv_out(vt[:, NM:2 * NM])
            v_out(1, XD, vx[:, :, 2 * XD:4 * XD].rearrange("p a (h b) -> p h a b", h=2))
            units()
            scale_out(qx[:, 1, :])
            units()
            for n in range(1, XH - 1):
                x_max(n)
                x_prob(n)
                units(2)
                scale_out(qx[:, n + 1, :])
            x_o(0)
            x_max(XH - 1)
            x_o(1)
            x_prob(XH - 1)
            x_o(2)
            x_o(3)

            for m in range(KT):
                if m % 2 == 0:
                    units()
                dve.wait_ge(half_done if m % 2 == 0 else unit_done, unit.at(1 - (0 if m % 2 else U_XO)))
                add_out(m)
                if m:
                    x_low(act_lo[:, m - 1, :], act_hi[:, m - 1, :], m - 1, G_FFN)
                if m % 2:
                    unit.add()
            x_low(act_lo[:, KT - 1, :], act_hi[:, KT - 1, :], KT - 1, G_FFN)

            half = Tally(KT // 2)

            def hidden(t, first=False):
                if first:
                    units()
                    rstd_of(4, rstd, S)
                    units()
                else:
                    units(2)
                dve.wait_ge(hid_lo, hid.at(1))
                scale_out(gt[:])
                dve.wait_ge(sig_ready, sig.at(1))
                link(nc.vector.tensor_tensor(gt[:], gt[:], sg[:], ALU.mult))
                link(nc.vector.tensor_tensor(gt[:], gt[:], rstd[:], ALU.mult))
                sig.add()
                units(2)
                unit.add(2)
                dve.wait_ge(unit_done, unit.at())
                nc.vector.tensor_tensor(gt[:], gt[:], output()[:], ALU.mult).then_inc(acc_free, 1)
                dve.wait_ge(hid_hi, hid.at(1))
                nc.vector.tensor_tensor(act2_lo[:, t, :], gt[:], f(act2_hi[:, t, :]), ALU.subtract)\
                    .then_inc(hid_lo, 1)
                hid.add()

            def add_final_square(m):
                if 1 <= m < KT - 1:
                    dve.wait_ge(squared, m + 1)
                    if m > 1:
                        dve.wait_ge(squares_added, m - 1)
                    nc.vector.tensor_tensor(sq_sum[:], sq_sum[:], square_tmp[m % 2][:], ALU.add)\
                        .then_inc(squares_added, 1)

            def ffn(first=0, last=False):
                with repeat(dve, GROUP - first, [(converted, 4), (unit, 4), (out_no, 2), (sig, 1), (step, 2),
                                                 (hid, 1)]) as t:
                    hidden(t + first)

                def down(m, split):
                    if split:
                        units()
                    dve.wait_ge(half_done, half.at(1))
                    add_out(m)
                    if last:
                        add_final_square(m - 1)
                    dve.wait_ge(unit_done, unit.at(1))
                    add_out(m + 1)
                    if last:
                        add_final_square(m)
                    unit.add()
                    half.add()

                if last:
                    for n in range(KT // 2):
                        down(2 * n, n < KT // 2 - AHEAD)
                else:
                    with repeat(dve, 2, [(converted, 4), (unit, 4), (out_no, 8), (half, 4)]) as i:
                        for b in range(4):
                            down(i * 8 + 2 * b, True)

            hidden(0, True)
            ffn(first=1)
            with repeat(dve, GROUPS - 2, [(converted, FFN_UNITS), (unit, FFN_UNITS), (out_no, GROUP * 2 + KT),
                                          (sig, GROUP), (step, 2 * GROUP), (hid, GROUP), (half, KT // 2)]):
                ffn()
            ffn(last=True)
            assert out_no.n == A_END and unit.n == UNITS and converted.n == UNITS

            rstd_of(5, rstd, S)
            for m in range(KT):
                nc.vector.scalar_tensor_tensor(x[:, m, :], x[:, m, :], par[:, G_FINAL + m:G_FINAL + m + 1], rstd[:],
                                               ALU.mult, ALU.mult).then_inc(out_ready, 1)

        @block.tensor
        def _(pe):
            u, out_no, hd, tr, swa = Tally(), Tally(), Tally(), Tally(), Tally()
            half, hid = Tally(), Tally()

            def output():
                a = acc[out_no.n % 2]
                if out_no.loops or out_no.n >= 2:
                    pe.wait_ge(acc_free, out_no.at(-1))
                out_no.add()
                return a

            def split_products(dst, pairs):
                for n, (wh, wl, ah, al) in enumerate(pairs):
                    nc.tensor.matmul(dst, wh, ah, start=n == 0, stop=False)
                    nc.tensor.matmul(dst, wh, al, start=False, stop=False)
                    last = nc.tensor.matmul(dst, wl, ah, start=False, stop=n == len(pairs) - 1)
                return last

            def unit(dst, tiles, start, stop, arrive=None):
                s = u.n % RING
                pe.wait_ge(lo_done, u.at(1))
                for k, (ah, al) in enumerate(tiles):
                    if arrive:
                        pe.wait_ge(*arrive(k))
                    wh, wl = (t[:, s, P * k:P * (k + 1)] for t in (w_hi, w_lo))
                    nc.tensor.matmul(dst, wh, ah, start=start and k == 0, stop=False)
                    nc.tensor.matmul(dst, wh, al, start=False, stop=False)
                    last = nc.tensor.matmul(dst, wl, ah, start=False, stop=stop and k == UK - 1)
                last.then_inc(unit_done, 1)
                u.add()

            def two_outputs(ready=None, value=None):
                s = u.n % RING
                pe.wait_ge(lo_done, u.at(1))
                order = [(n, k) for n in range(2) for k in range(GROUP)]
                if ready:
                    pe.wait_ge(ready, value)
                    order.remove((0, GROUP - 1))
                    order.insert(GROUP + 1, (0, GROUP - 1))
                dst = {}
                for n, k in order:
                    if k == 0:
                        dst[n] = output()[:]
                    if ready and (n, k) == (0, GROUP - 1):
                        pe.wait_ge(ready, value + 1)
                    ah, al = act2_tile(k)
                    wh, wl = (t[:, s, P * (GROUP * n + k):P * (GROUP * n + k + 1)] for t in (w_hi, w_lo))
                    nc.tensor.matmul(dst[n], wh, ah, start=k == 0, stop=False)
                    nc.tensor.matmul(dst[n], wh, al, start=False, stop=False)
                    last = nc.tensor.matmul(dst[n], wl, ah, start=False, stop=k == GROUP - 1)
                    if k == GROUP - 1:
                        last.then_inc(unit_done if n else half_done, 1)
                u.add()

            def panel(tile, width=S, arrive=None):
                dst = output()[:, 0:width]
                for n in range(2):
                    unit(dst, [tile(UK * n + k) for k in range(UK)], n == 0, n == 1,
                         arrive and (lambda k, n=n: arrive(UK * n + k)))

            def stat(n, ready, value, bank, src, width):
                pe.wait_ge(ready, value)
                nc.tensor.matmul(bank[:, 0:width], ones[:], src[:, 0:width], start=True, stop=True)\
                    .then_inc(stat_done, 1)

            def scores(n):
                if n == 0:
                    pe.wait_ge(qk_lo_done, hd.at(2))
                pe.wait_ge(ps_free, hd.at(n + 1))
                rows = slice(HD * n, HD * n + HD)
                for j in range(QT):
                    keys, cols = slice(P * j, P * (j + 1)), slice(P * j, S)
                    last = split_products(ps[n][:, SB_OFF[j]:SB_OFF[j] + SB_LEN[j]],
                                          [(k_hi[rows, keys], k_lo[rows, keys], q_hi[rows, cols], q_lo[rows, cols])])
                last.then_inc(z_done, 1)

            def tails(n):
                pe.wait_ge(p_lo_done, hd.at(1 + n))
                for j in range(QT):
                    terms = [(tri_r, j)] + [(ones_r, i) for i in range(j + 1, QT)]
                    for m, (mat, i) in enumerate(terms):
                        dst = ps[n][:, SB_OFF[j] + P * (i - j):SB_OFF[j] + SB_LEN[j]]
                        cols = slice(SB_OFF[i], SB_OFF[i] + SB_LEN[i])
                        nc.tensor.matmul(dst, mat[:], pa_hi[n][:, cols], start=m == 0, stop=False)
                        last = nc.tensor.matmul(dst, mat[:], pa_lo[n][:, cols], start=False, stop=m == len(terms) - 1)
                last.then_inc(t_done, 1)

            def values(n):
                if n == 0:
                    pe.wait_ge(acc_free, v_out_no.at())
                pe.wait_ge(a_lo_done, hd.at(1 + n))
                for j in range(QT):
                    toks, cols = slice(P * j, P * (j + 1)), slice(SB_OFF[j], SB_OFF[j] + SB_LEN[j])
                    dst = ps[n][:, P * j:S]
                    nc.tensor.matmul(dst, v_hi[:, toks], pa_hi[n][:, cols], start=j == 0, stop=False)
                    nc.tensor.matmul(dst, v_hi[:, toks], pa_lo[n][:, cols], start=False, stop=False)
                    last = nc.tensor.matmul(dst, v_lo[:, toks], pa_hi[n][:, cols], start=False, stop=j == QT - 1)
                last.then_inc(pv_done, 1)

            v_out_no = Tally(4)

            def turn(src, blocks):
                dst = output()
                for b in range(blocks):
                    last = nc.tensor.transpose(dst[:, P * b:P * (b + 1)], src[:, P * b:P * (b + 1)], ident[:])
                last.then_inc(tr_done, 1)
                tr.add()

            def sb_last():
                scores(0)
                scores(1)
                pe.wait_ge(acc_free, out_no.at())
                turn(vt, QT)
                panel(act_tile)
                tails(0)
                dst = output()[:]
                unit(dst, [act_tile(k) for k in range(UK)], True, False)
                tails(1)
                unit(dst, [act_tile(UK + k) for k in range(UK)], False, True)
                values(0)
                values(1)
                hd.add(2)

            def sb_body():
                scores(0)
                scores(1)
                pe.wait_ge(acc_free, out_no.at())
                turn(vt, QT)
                panel(act_tile)
                tails(0)
                dst = output()[:]
                unit(dst, first, True, False)
                tails(1)
                unit(dst, second, False, True)
                values(0)
                dst = output()[:]
                unit(dst, first, True, False)
                values(1)
                unit(dst, second, False, True)
                hd.add(2)
                v_out_no.add(4)

            pe.wait_ge(const_r_ready, 2)
            panel(act_tile, arrive=lambda k: (h_lo, k + 1))
            first, second = ([act_tile(UK * n + k) for k in range(UK)] for n in range(2))
            dst = output()[:]
            unit(dst, first, True, False)
            pe.wait_ge(sq_done, 1)
            pe.wait_ge(half_summed, len(OTHER_TILES) + 1)
            nc.tensor.matmul(ps[0][:, 0:S], ones[:], sq_sum[:], start=True, stop=False)
            nc.tensor.matmul(ps[0][:, 0:S], ones[:], sq_half[:], start=False, stop=True).then_inc(stat_done, 1)
            unit(dst, second, False, True)
            panel(act_tile)
            with repeat(pe, (PAIRS - 2) // 2, [(u, 12), (out_no, 8), (hd, 4), (tr, 2), (v_out_no, 8)]):
                sb_body()
                sb_body()
            sb_body()
            sb_last()

            def gates(o_written):
                def branches():
                    for b in range(2):
                        unit(output()[:], [o_tile(k) for k in range(UK)], True, True,
                             (lambda k: (ps_free, 2 + o_written - (0 if k == UK - 1 else 2))) if b == 0 else None)

                def next_gates():
                    panel(act_tile)
                    panel(act_tile)

                with repeat(pe, (KT // 2 - 1) // 2, [(u, 12), (out_no, 8)]):
                    for _ in range(2):
                        branches()
                        next_gates()
                branches()
                next_gates()
                branches()

            gates(2 * PAIRS)
            assert out_no.n == A_SWA and u.n == U_SWA

            def swa_scores(t, hf):
                if hf == 0:
                    pe.wait_ge(qa_ready, t + 3)
                for i in range(2):
                    qt = 2 * hf + i
                    for n in range(2):
                        rows = slice(HD * n, HD * n + HD)
                        for side, kb in ((0, max(qt - 1, 0)), (1, qt)):
                            at = S * n + 2 * P * i + P * side
                            last = nc.tensor.matmul(ps[hf][:, at:at + P], qa[rows, P * qt:P * (qt + 1)],
                                                    ka[rows, t // GQ, P * kb:P * (kb + 1)], start=True, stop=True)
                last.then_inc(s_done, 1)

            def swa_turn(t, hf):
                pe.wait_ge(prob_ready, 2 * t + hf + 1)
                for b in range(8):
                    last = nc.tensor.transpose(ps[hf][:, P * b:P * (b + 1)],
                                               s_a[:, b // 2, P * (b % 2):P * (b % 2 + 1)], ident[:])
                last.then_inc(ptr_done, 1)

            def swa_values(t, hf):
                pe.wait_ge(pt_ready, 2 * t + hf + 1)
                pe.wait_ge(ps_free, 2 * PAIRS + 2 * t + hf + 1)
                for n in range(2):
                    for i in range(2):
                        qt = 2 * hf + i
                        dst = ps[hf][:, 2 * S + P * (2 * n + i):2 * S + P * (2 * n + i + 1)]
                        sides = [(1, qt)] + ([(0, qt - 1)] if qt else [])
                        for m, (side, kb) in enumerate(sides):
                            b = 2 * (2 * n + i) + side
                            last = nc.tensor.matmul(dst, va[:, kb, P * (t // GQ):P * (t // GQ + 1)],
                                                    pt_a[:, P * b:P * (b + 1)], start=m == 0, stop=m == len(sides) - 1)
                last.then_inc(pv_done, 1)

            panel(act_tile)
            panel(act_tile)
            panel(act_tile)
            pe.wait_ge(ps_free, 2 + 2 * PAIRS)
            pe.wait_ge(acc_free, A_SWA + 2)
            for n in range(2):
                for b in range(QT):
                    last = nc.tensor.transpose(ps[n][:, P * b:P * (b + 1)], va_t[n][:, P * b:P * (b + 1)], ident[:])
                last.then_inc(tr_done, 1)
                tr.add()
            panel(act_tile)
            panel(act_tile)
            dst = output()[:]
            unit(dst, first, True, False)
            pe.wait_ge(va_ready, 2)
            for t in range(PAIRS):
                swa_scores(t, 0)
                if t:
                    swa_values(t - 1, 1)
                swa_scores(t, 1)
                unit(dst, second, False, True)
                swa_turn(t, 0)
                dst = output()[:]
                unit(dst, first, True, False)
                swa_values(t, 0)
                swa_turn(t, 1)
            unit(dst, second, False, True)
            swa_values(PAIRS - 1, 1)
            assert out_no.n == A_DA + 2 and u.n == U_DA + 4
            swa.n, hd.n = 2 * PAIRS, 4 * PAIRS

            gates(4 * PAIRS)
            assert out_no.n == A_OUT and u.n == U_OUT

            def out_units(n, turns):
                with repeat(pe, turns, [(u, 4), (out_no, 4)]):
                    for b in range(4):
                        unit(output()[:], [act_tile(UK * n + k) for k in range(UK)], True, True)

            for b in range(4):
                unit(output()[:], first, True, True, (lambda k: (mg_lo, k + 1)) if b == 0 else None)
            out_units(0, KT // 4 - 1)
            pe.wait_ge(mg_lo, KT)
            out_units(1, KT // 4)

            panel(hc_tile, arrive=lambda k: (h_lo, KT + k + 1))
            stat(2, sq_done, 3, ps[0], sq_sum, S)
            panel(mem_tile, NM, arrive=lambda k: (mem_lo, k + 1))
            stat(3, sq_done, 2, ps[1], mem_stat, NM)
            for _ in range(XH - 1):
                panel(mem_tile, NM)

            def x_scores(n):
                for t in range(QT):
                    last = nc.tensor.matmul(ps[n % 2][:, NM * t:NM * (t + 1)], qx[:, n, P * t:P * (t + 1)],
                                            kx[:, n, :], start=True, stop=True)
                last.then_inc(s_done, 1)

            def x_turn(n):
                pe.wait_ge(prob_ready, 2 * PAIRS + n + 1)
                for b in range(2):
                    for t in range(QT):
                        last = nc.tensor.transpose(ps[n % 2][:, S * b + P * t:S * b + P * (t + 1)],
                                                   s_x[:, t, P * b:P * (b + 1)], ident[:])
                last.then_inc(ptr_done, 1)

            def x_values(n):
                pe.wait_ge(pt_ready, 2 * PAIRS + n + 1)
                for b in range(2):
                    last = nc.tensor.matmul(ps[n % 2][:, 2 * S:3 * S], vx[:, b, XD * n:XD * (n + 1)], pt_x[:, b, :],
                                            start=b == 0, stop=b == 1)
                last.then_inc(pv_done, 1)

            pe.wait_ge(acc_free, A_X + 1 + XH)
            x_scores(0)
            panel(mem_tile, NM)
            panel(mem_tile, NM)
            pe.wait_ge(acc_free, out_no.at())
            panel(mem_tile, NM)

            def v_turn():
                dst = output()
                for b in range(4):
                    last = nc.tensor.transpose(dst[:, P * b:P * (b + 1)], vt[:, P * b:P * (b + 1)], ident[:])
                last.then_inc(tr_done, 1)

            v_turn()
            panel(mem_tile, NM)
            pe.wait_ge(acc_free, out_no.at())
            v_turn()
            x_turn(0)
            x_first, x_second = ([hc_tile(UK * n + k) for k in range(UK)] for n in range(2))
            dst = output()[:]
            unit(dst, x_first, True, False)
            pe.wait_ge(acc_free, out_no.at(-1))
            x_values(0)
            unit(dst, x_second, False, True)
            for n in range(1, XH - 1):
                pe.wait_ge(acc_free, out_no.at())
                x_scores(n)
                dst = output()[:]
                unit(dst, x_first, True, False)
                x_turn(n)
                unit(dst, x_second, False, True)
                if n == 1:
                    x_values(n)
            pe.wait_ge(acc_free, out_no.at())
            x_scores(XH - 1)
            for n in (XH - 2, XH - 1):
                if n == XH - 1:
                    x_turn(n)
                pe.wait_ge(ps_free, 4 * PAIRS + n + 1)
                x_values(n)

            two_outputs(ps_free, 4 * PAIRS + 2 + XH - 1)
            for _ in range(KT // 2 - 1):
                two_outputs()

            def ffn_first():
                panel(act_tile, arrive=lambda k: (h_lo, 2 * KT + k + 1))
                stat(4, cross_summed, KT, ps[0], sq_sum, S)
                panel(act_tile)

            def ffn(turns=GROUP):
                with repeat(pe, turns, [(u, 4), (out_no, 2)]):
                    panel(act_tile)
                    panel(act_tile)
                hid.add(GROUP)
                two_outputs(hid_lo, hid.at())
                for _ in range(KT // 2 - 1):
                    two_outputs()

            ffn_first()
            ffn(GROUP - 1)
            with repeat(pe, GROUPS - 2, [(u, FFN_UNITS), (out_no, GROUP * 2 + KT), (hid, GROUP)]):
                ffn()
            ffn()
            assert out_no.n == A_END and u.n == UNITS

            pe.wait_ge(squares_added, KT - 2)
            nc.tensor.matmul(ps[1][:, 0:S], ones[:], sq_sum[:], start=True, stop=False)
            pe.wait_ge(squared, KT)
            nc.tensor.matmul(ps[1][:, 0:S], ones[:], square_tmp[(KT - 1) % 2][:], start=False, stop=True)\
                .then_inc(stat_done, 1)


def stream(m, halves_outside=False):
    k, n = m.shape
    b = m.reshape(k // P, P, n // P, P)
    if halves_outside:
        b = b.reshape(k // P // UK, UK, P, n // P, P).transpose(0, 3, 2, 1, 4)
    else:
        b = b.transpose(2, 0, 1, 3).reshape(-1, UK, P, P).transpose(0, 2, 1, 3)
    return b.reshape(-1, P, UK * P)


def columns(m, n):
    return m[:, P * n:P * (n + 1)]


GQ = SWA_HEADS // SWA_KV
LOWER = [g * GQ + i for g in range(0, SWA_KV, 2) for i in range(GQ)]
HEADS = [h + o * GQ for h in LOWER for o in (0, 1)]


def gates_and_branches(w_gate, w_branch):
    gates, branches = ([stream(columns(w, m)) for m in range(KT)] for w in (w_gate, w_branch))
    parts = gates[:2]
    for m in range(0, KT, 2):
        parts += branches[m:m + 2] + gates[m + 2:m + 4]
    return parts


def weight_stream(w_in, w_gate, w_a, w_b, w_out, w_xq, w_xkv, w_xo, w_gu, w_down):
    qa, ka, va, qb, kb, vb = np.split(w_in, np.cumsum([SWA_W, KV_W, KV_W, SB_W, SB_W]), axis=1)
    qa = qa.reshape(D, SWA_HEADS, HD)[:, HEADS].reshape(D, SWA_W)
    w_a = w_a.reshape(SWA_HEADS, HD, D)[HEADS].reshape(SWA_W, D)
    parts = [stream(columns(m, p)) for p in range(PAIRS) for m in (qb, kb, vb)]
    parts += gates_and_branches(w_gate[:, D:], w_b)
    parts += [stream(columns(va, 0)), stream(columns(va, 1)), stream(ka), stream(qa)]
    parts += gates_and_branches(w_gate[:, :D], w_a)
    parts += [stream(w_out, True), stream(w_xq[:, :XD]), stream(w_xkv), stream(w_xq[:, XD:]), stream(w_xo)]
    width = GROUP * P
    for g in range(GROUPS):
        for t in range(GROUP):
            parts += [stream(columns(w_gu, g * GROUP + t)), stream(columns(w_gu, FFN // P + g * GROUP + t))]
        parts += [stream(w_down[width * g:width * (g + 1)])]
    return np.concatenate(parts)


def tiles(v):
    return v.reshape(-1, P).T


def kernel(x, mem, positions, norm_mix_g, w_in, sinks, w_branch_a, w_branch_b, w_gate, b_gate, w_out,
           norm_cross_g, norm_mem_g, w_xq, w_xkv, w_xo, norm_ffn_g, w_gu, w_down, final_norm_g):
    import concourse.bacc as bacc
    from concourse.bass_utils import run_bass_kernel_spmd

    a = {k: np.asarray(v) for k, v in locals().items() if k not in ("bacc", "run_bass_kernel_spmd")}
    w = weight_stream(*(a[k][0] for k in ("w_in", "w_gate", "w_branch_a", "w_branch_b", "w_out", "w_xq", "w_xkv",
                                          "w_xo", "w_gu", "w_down")))
    params = np.concatenate(
        [tiles(a[k].reshape(-1)) for k in ("norm_mix_g", "norm_cross_g", "norm_mem_g", "norm_ffn_g", "final_norm_g",
                                           "b_gate")]
        + [np.broadcast_to(a["sinks"][0][HEADS], (P, SWA_HEADS))], axis=1)
    inv = (ROPE_THETA ** (-np.arange(HALF, dtype=np.float64) / HALF)).astype(np.float32)
    sign = np.repeat(np.array([-1, 1], np.float32), HALF)
    arrays = {
        "w_stream": w,
        "x_t": a["x"][0].T.reshape(KT, P, S).transpose(1, 0, 2),
        "mem_t": a["mem"][0].T.reshape(KT, P, NM).transpose(1, 0, 2),
        "params": params,
        "rope_const": np.stack([np.tile(inv, P // HALF), np.tile(sign, P // HD)], axis=1),
        "pos": np.broadcast_to(a["positions"].astype(np.int32), (P, S)),
    }
    arrays = {k: np.ascontiguousarray(v) for k, v in arrays.items()}
    nc = bacc.Bacc("TRN2", target_bir_lowering=False, num_devices=1)
    args = [nc.dram_tensor(k, v.shape, mybir.dt.from_np(v.dtype), kind="ExternalInput").ap() for k, v in arrays.items()]
    out = nc.dram_tensor("out_t", (KT, P, S), mybir.dt.float32, kind="ExternalOutput").ap()
    block_kernel(nc, *args, out)
    r = run_bass_kernel_spmd(nc, [arrays], core_ids=[0])
    return r.results[0]["out_t"].reshape(D, S).T[None]
```
